# Optimizing a Trainium2 kernel written in Bass

```python
import jax, jax.numpy as jnp
from jax import lax
import numpy as np

D_MODEL = 1024
BATCH = 1
SEQ = 2048
DEPTH = 1

CHUNK = 64
HEAD_DIM = 64
N_HEADS_A = 8
KV_A = 2
GROUP_A = N_HEADS_A // KV_A
WINDOW = 128
WINDOW_CHUNKS = WINDOW // CHUNK
N_HEADS_B = 8
Q_BLOCK = 128
WIDTH_A = N_HEADS_A * HEAD_DIM
WIDTH_B = N_HEADS_B * HEAD_DIM
MIX_WIDTH = WIDTH_A + WIDTH_B
D_FF = ((8 * D_MODEL + 3 * 256 - 1) // (3 * 256)) * 256
SPLITS = (WIDTH_A, KV_A * HEAD_DIM, KV_A * HEAD_DIM, WIDTH_B, WIDTH_B, WIDTH_B, N_HEADS_B)
IN_COLS = sum(SPLITS)
EPS = 1e-6
ATTN_SCALE = HEAD_DIM ** -0.5
NEG_INF = -1e30

kernel_name = 'hybrid_swa_sink_fox_adaln_block'

def rms_norm(x, g):
    xf = x.astype(jnp.float32)
    y = xf * lax.rsqrt(jnp.mean(xf * xf, axis=-1, keepdims=True) + EPS)
    return (y * g.astype(jnp.float32)).astype(x.dtype)

def alibi_slopes(n_heads):
    return jnp.exp2(-8.0 * (jnp.arange(n_heads, dtype=jnp.float32) + 1.0) / n_heads)

def swa_sink_attention(q, k, v, sinks, slopes):
    B, S = q.shape[0], q.shape[1]
    n_chunks = S // CHUNK
    band = WINDOW_CHUNKS * CHUNK
    qc = q.reshape(B, n_chunks, CHUNK, KV_A, GROUP_A, HEAD_DIM)

    def band_of(t):
        tc = t.reshape(B, n_chunks, CHUNK, KV_A, HEAD_DIM)
        tp = jnp.pad(tc, ((0, 0), (WINDOW_CHUNKS - 1, 0), (0, 0), (0, 0), (0, 0)))
        return jnp.concatenate([tp[:, w:w + n_chunks] for w in range(WINDOW_CHUNKS)], axis=2)

    kb, vb = band_of(k), band_of(v)
    scores = jnp.einsum('bnqkgd,bnskd->bnkgqs', qc, kb).astype(jnp.float32) * ATTN_SCALE
    qi = jnp.arange(CHUNK)[:, None]
    kj = jnp.arange(band)[None, :]
    dist = jnp.abs(qi - kj + (WINDOW_CHUNKS - 1) * CHUNK).astype(jnp.float32)
    alibi = -slopes.reshape(KV_A, GROUP_A, 1, 1) * dist
    chunk_idx = jnp.arange(n_chunks)[:, None]
    valid = (chunk_idx - (WINDOW_CHUNKS - 1) + kj // CHUNK) >= 0
    scores = jnp.where(valid[None, :, None, None, None, :], scores + alibi, NEG_INF)
    sink = sinks.astype(jnp.float32).reshape(KV_A, GROUP_A, 1, 1)
    m = jnp.maximum(scores.max(axis=-1, keepdims=True), sink)
    p = jnp.exp(scores - m)
    denom = p.sum(axis=-1, keepdims=True) + jnp.exp(sink - m)
    probs = (p / denom).astype(v.dtype)
    out = jnp.einsum('bnkgqs,bnskd->bnqkgd', probs, vb)
    return out.reshape(B, S, WIDTH_A)

def forgetting_attention(q, k, v, log_f):
    B, S = q.shape[0], q.shape[1]
    n_blocks = S // Q_BLOCK
    F = jnp.cumsum(log_f, axis=1)
    Fk = jnp.transpose(F, (0, 2, 1))
    key_pos = jnp.arange(S)

    def block(i):
        start = i * Q_BLOCK
        qb = lax.dynamic_slice_in_dim(q, start, Q_BLOCK, axis=1)
        Fq = lax.dynamic_slice_in_dim(F, start, Q_BLOCK, axis=1)
        s = jnp.einsum('bqhd,bshd->bhqs', qb, k).astype(jnp.float32) * ATTN_SCALE
        s = s + (jnp.transpose(Fq, (0, 2, 1))[..., None] - Fk[:, :, None, :])
        q_pos = start + jnp.arange(Q_BLOCK)
        s = jnp.where(key_pos[None, :] <= q_pos[:, None], s, NEG_INF)
        p = jax.nn.softmax(s, axis=-1).astype(v.dtype)
        return jnp.einsum('bhqs,bshd->bqhd', p, v)

    out = lax.map(block, jnp.arange(n_blocks))
    return jnp.transpose(out, (1, 0, 2, 3, 4)).reshape(B, S, WIDTH_B)

def setup_inputs(seed: int = 0) -> dict:
    key = jax.random.key(seed)
    ks = jax.random.split(key, 16)
    nrm = jax.random.normal
    D = D_MODEL
    return {
        'x': nrm(ks[0], (BATCH, SEQ, D), jnp.float32),
        'c': nrm(ks[1], (BATCH, D), jnp.float32),
        'w_ada': nrm(ks[2], (DEPTH, D, 6 * D), jnp.float32) * D ** -0.5,
        'b_ada': 0.02 * nrm(ks[3], (DEPTH, 6 * D), jnp.float32),
        'g_norm_mix': 1.0 + 0.02 * nrm(ks[4], (DEPTH, D), jnp.float32),
        'w_in': nrm(ks[5], (DEPTH, D, IN_COLS), jnp.float32) * D ** -0.5,
        'b_forget': jax.random.uniform(ks[6], (DEPTH, N_HEADS_B), jnp.float32, 1.0, 4.0),
        'sinks': 0.5 * nrm(ks[7], (DEPTH, N_HEADS_A), jnp.float32),
        'g_grp_a': 1.0 + 0.02 * nrm(ks[8], (DEPTH, WIDTH_A), jnp.float32),
        'g_grp_b': 1.0 + 0.02 * nrm(ks[9], (DEPTH, WIDTH_B), jnp.float32),
        'w_out': nrm(ks[10], (DEPTH, MIX_WIDTH, D), jnp.float32) * MIX_WIDTH ** -0.5,
        'g_norm_ffn': 1.0 + 0.02 * nrm(ks[11], (DEPTH, D), jnp.float32),
        'w_gate_up': nrm(ks[12], (DEPTH, D, 2 * D_FF), jnp.float32) * D ** -0.5,
        'w_down': nrm(ks[13], (DEPTH, D_FF, D), jnp.float32) * D_FF ** -0.5,
        'g_final': 1.0 + 0.02 * nrm(ks[14], (D,), jnp.float32),
    }

def reference(x, c, w_ada, b_ada, g_norm_mix, w_in, b_forget, sinks, g_grp_a, g_grp_b,
              w_out, g_norm_ffn, w_gate_up, w_down, g_final):
    B, S, D = x.shape
    slopes = alibi_slopes(N_HEADS_A)
    split_idx = list(np.cumsum(SPLITS)[:-1])
    c_act = jax.nn.silu(c)
    for l in range(DEPTH):
        mod = c_act @ w_ada[l] + b_ada[l]
        shift_a, scale_a, gate_a, shift_f, scale_f, gate_f = [m[:, None, :] for m in jnp.split(mod, 6, axis=-1)]

        h = rms_norm(x, g_norm_mix[l]) * (1.0 + scale_a) + shift_a
        proj = h @ w_in[l]
        qa, ka, va, qb, kb, vb, f_logit = jnp.split(proj, split_idx, axis=-1)
        qa = qa.reshape(B, S, N_HEADS_A, HEAD_DIM)
        ka = ka.reshape(B, S, KV_A, HEAD_DIM)
        va = va.reshape(B, S, KV_A, HEAD_DIM)
        qb = qb.reshape(B, S, N_HEADS_B, HEAD_DIM)
        kb = kb.reshape(B, S, N_HEADS_B, HEAD_DIM)
        vb = vb.reshape(B, S, N_HEADS_B, HEAD_DIM)
        log_f = jax.nn.log_sigmoid(f_logit.astype(jnp.float32) + b_forget[l].astype(jnp.float32))

        ya = swa_sink_attention(qa, ka, va, sinks[l], slopes)
        yb = forgetting_attention(qb, kb, vb, log_f)
        y = jnp.concatenate([rms_norm(ya, g_grp_a[l]), rms_norm(yb, g_grp_b[l])], axis=-1)
        x = x + gate_a * (y @ w_out[l])

        h = rms_norm(x, g_norm_ffn[l]) * (1.0 + scale_f) + shift_f
        g, u = jnp.split(h @ w_gate_up[l], 2, axis=-1)
        x = x + gate_f * ((jax.nn.silu(g) * u) @ w_down[l])
    return rms_norm(x, g_final)


_drawn_inputs = setup_inputs


def setup_inputs(seed=0):
    import zlib

    import numpy as np

    out = dict(_drawn_inputs(seed))
    spreads = {}
    factors = {'g_norm_mix': 4.794,
     'sinks': 8.0,
     'g_grp_a': 7.115,
     'g_grp_b': 7.728,
     'g_norm_ffn': 4.846,
     'g_final': 2.917}
    for name, (base, spread) in spreads.items():
        noise = np.random.default_rng([zlib.crc32(name.encode()), seed]).standard_normal(out[name].shape)
        drawn = base * np.exp(spread * noise) if base else spread * noise
        out[name] = __import__('jax').numpy.asarray(drawn.astype(out[name].dtype))
    for name, factor in factors.items():
        out[name] = (out[name] * factor).astype(out[name].dtype)
    return out
```

```python
from contextlib import ExitStack

import concourse.bass as bass
from concourse import mybir
from concourse.alu_op_type import AluOpType as ALU

F32 = mybir.dt.float32
F32R = mybir.dt.float32r
ACT = mybir.ActivationFunctionType
AXX = mybir.AxisListType.X

P = 128
D = 1024
S = 2048
HD = 64
HA, KVA, HB = 8, 2, 8
GA = HA // KVA
WA, WB = HA * HD, HB * HD
DFF = 2816
EPS = 1e-6
START = 1
SCALE = HD ** -0.5
INV_SCALE = 8.0
NEG = -1e30
DT = D // P
RT = S // P
RG = 512
NRG = S // RG
TPG = RG // P
FT = DFF // P
QA0, KA0, VA0 = 0, WA, WA + KVA * HD
QB0 = VA0 + KVA * HD
KB0, VB0, FG0 = QB0 + WB, QB0 + 2 * WB, QB0 + 3 * WB
IN_COLS = FG0 + HB
PT = FG0 // P
BAND = 192
V_BADA, V_GMIX, V_GFFN, V_GFIN, V_GGRP = 0, 48, 56, 64, 72
V_ROWS = 80


class Core:

    def __init__(self, nc, stack):
        self.nc, self.stack, self.stage_sems = nc, stack, []
        self.ident = self.sbuf("ident", [P, P])
        self.ones_r = self.sbuf("ones_r", [P, P], F32R)
        self.cols = self.sbuf("cols", [P, V_ROWS])
        self.mod = self.sbuf("mod", [P, 48])
        self.a_mix = self.sbuf("a_mix", [P, DT])
        self.a_ffn = self.sbuf("a_ffn", [P, DT])

    def sbuf(self, name, shape, dt=F32, stack=None):
        return (stack or self.stack).enter_context(self.nc.sbuf_tensor(name, shape, dt))

    def banks(self, name, n, stack):
        return [stack.enter_context(self.nc.psum_tensor(f"{name}{i}", [P, RG], F32)) for i in range(n)]

    def sem(self, name):
        self.stage_sems.append(self.nc.alloc_semaphore(name=name))
        return self.stage_sems[-1]

    def end_stage(self):
        self.nc.clear_and_free_semaphores(self.stage_sems)
        self.stage_sems = []
        self.nc.all_engine_barrier()

    def sems(self, name, n):
        return [self.sem(f"{name}{i}") for i in range(n)]


def start_counts(k):
    with k.nc.Block() as block:
        @block.gpsimd
        def _(pool):
            for sem in k.stage_sems:
                pool.sem_inc(sem, START)


def wait_apart(eng, passed, sem, value):
    eng.wait_ge(sem, value)
    eng.sem_inc(passed, 1)


def f32(ap):
    return ap.bitcast(F32)


def stage_modulation(k, c, w_ada, vectors, ident_in, ones_in):
    nc = k.nc
    CH, SL = 12, 4
    with ExitStack() as st:
        c_col = k.sbuf("c_col", [P, DT], stack=st)
        c_act = k.sbuf("c_act", [P, DT], stack=st)
        table = k.sbuf("table", [V_ROWS, P], stack=st)
        ones = k.sbuf("ones_raw", [P, P], stack=st)
        w = [k.sbuf(f"w_ada{s}", [P, DT, RG], stack=st) for s in range(SL)]
        row = k.sbuf("mod_row", [1, CH * RG], stack=st)
        acc = k.banks("mod_acc", SL, st)
        small = k.banks("mod_col", 2, st)
        const_in, c_in = k.sem("const_in"), k.sem("c_in")
        w_in = k.sems("w_ada_in", SL)
        c_ready, ones_ready = k.sem("c_ready"), k.sem("ones_ready")
        table_t, table_used = k.sem("table_t"), k.sem("table_used")
        prod = k.sems("ada_product", SL)
        row_ready = k.sems("ada_row", SL)
        mod_t, mod_ready = k.sem("mod_t"), k.sem("mod_ready")
        w_view = w_ada.rearrange("o (p t) n -> p (o t) n", t=DT)

        start_counts(k)
        with nc.Block() as block:
            @block.sync
            def _(sp):
                sp.dma_start(c_col[:, :], c.rearrange("o (p t) -> p (o t)", t=DT)).then_inc(c_in, 16)
                sp.dma_start(k.ident[:, :], ident_in).then_inc(const_in, 16)
                sp.dma_start(ones[:, :], ones_in).then_inc(const_in, 16)
                for at, v in vectors:
                    n = v.shape[0]
                    sp.dma_start(table[at:at + n, :], v).then_inc(const_in, 16)
                with sp.Fori(0, CH // SL) as i:
                    for s in range(SL):
                        sp.wait_ge(prod[s], START + i)
                        sp.dma_start(w[s][:, :, :], w_view[:, :, bass.ds((i * SL + s) * RG, RG)]).then_inc(w_in[s], 16)

            @block.scalar
            def _(act):
                act.wait_ge(c_in, START + 16)
                nc.scalar.activation(c_act[:, :], c_col[:, :], ACT.Silu).then_inc(c_ready, 1)

            @block.tensor
            def _(pe):
                pe.wait_ge(const_in, START + 16 * (2 + len(vectors)))
                nc.tensor.transpose(small[0][:, 0:V_ROWS], table[:, :], k.ident[0:V_ROWS, 0:V_ROWS]).then_inc(table_t, 1)
                pe.wait_ge(c_ready, START + 1)
                with pe.Fori(0, CH // SL) as i:
                    for s in range(SL):
                        pe.wait_ge(w_in[s], START + (i + 1) * 16)
                        pe.wait_ge(row_ready[s], START + i)
                        for t in range(DT):
                            last = nc.tensor.matmul(acc[s][0:1, :], c_act[:, t:t + 1], w[s][:, t, :],
                                                    start=(t == 0), stop=(t == DT - 1))
                        last.then_inc(prod[s], 1)
                for s in range(SL):
                    pe.wait_ge(row_ready[s], START + CH // SL)
                for j in range(48):
                    last = nc.tensor.matmul(small[1][:, j:j + 1], row[0:1, j * P:(j + 1) * P], k.ident[0:1, 0:1],
                                            start=True, stop=True)
                last.then_inc(mod_t, 1)

            @block.vector
            def _(dve):
                dve.wait_ge(const_in, START + 16 * (2 + len(vectors)))
                nc.vector.tensor_copy(k.ones_r[:, :], ones[:, :]).then_inc(ones_ready, 1)
                dve.wait_ge(table_t, START + 1)
                nc.vector.tensor_copy(k.cols[:, :], small[0][:, 0:V_ROWS]).then_inc(table_used, 1)
                with dve.Fori(0, CH // SL) as i:
                    for s in range(SL):
                        dve.wait_ge(prod[s], START + i + 1)
                        nc.vector.tensor_copy(row[0:1, bass.ds((i * SL + s) * RG, RG)], acc[s][0:1, :]).then_inc(row_ready[s], 1)
                dve.wait_ge(mod_t, START + 1)
                dve.wait_ge(table_used, START + 1)
                nc.vector.tensor_add(k.mod[:, :], small[1][:, 0:48], k.cols[:, V_BADA:V_BADA + 48]).then_inc(mod_ready, 1)
                dve.wait_ge(mod_ready, START + 1)
                for a, g, j in ((k.a_mix, V_GMIX, 1), (k.a_ffn, V_GFFN, 4)):
                    nc.vector.scalar_tensor_tensor(a[:, :], k.mod[:, DT * j:DT * (j + 1)], 1.0, k.cols[:, g:g + DT],
                                                   ALU.add, ALU.mult).then_inc(mod_ready, 1)


def stage_input_norm(k, x, eps, h_hi, h_lo, stack):
    nc = k.nc
    NS = 2 * TPG
    with ExitStack() as st:
        xs = [k.sbuf(f"x_in{s}", [P, D], stack=st) for s in range(NS)]
        junk = k.sbuf("squares", [P, D], stack=st)
        ssq = k.sbuf("ssq", [P, NS], stack=st)
        rms = k.sbuf("rms", [P, NS], stack=st)
        rstd = k.sbuf("rstd", [P, NS], stack=st)
        h = [k.sbuf(f"h_f32{s}", [P, RG], stack=st) for s in range(2)]
        tr = k.banks("x_t", 4, st)
        x_in = k.sems("n_x_in", NS)
        squared, rms_ready, rstd_ready, x_scaled = (k.sem("n_" + n) for n in ("squared", "rms", "rstd", "scaled"))
        tr_done, h_ready, hi_ready, lo_ready = (k.sem("n_" + n) for n in ("t", "h", "hi", "lo"))
        x_rows = x.rearrange("o (t p) d -> (o t) p d", p=P)

        start_counts(k)
        with nc.Block() as block:
            @block.sync
            def _(sp):
                with sp.Fori(0, NRG // 2) as i:
                    for s in range(NS):
                        sp.wait_ge(tr_done, START + i * 2 * DT)
                        sp.dma_start(xs[s][:, :], x_rows[bass.ds(i * NS + s, 1), :, :].rearrange("o p d -> p (o d)"))\
                          .then_inc(x_in[s], 16)

            @block.scalar
            def _(act):
                with act.Fori(0, NRG // 2) as i:
                    for r in range(2):
                        for s in range(r * TPG, (r + 1) * TPG):
                            act.wait_ge(x_in[s], START + (i + 1) * 16)
                            if s % TPG == 0:
                                act.wait_ge(rstd_ready, START + i * 2 + r)
                            act.wait_ge(squared, START + i * NS + s)
                            nc.scalar.activation(junk[:, :], xs[s][:, :], ACT.Square, accum_out=ssq[:, s:s + 1])\
                              .then_inc(squared, 1)
                        g = slice(r * TPG, (r + 1) * TPG)
                        act.wait_ge(squared, START + i * NS + (r + 1) * TPG)
                        nc.scalar.activation(rms[:, g], ssq[:, g], ACT.Sqrt, bias=eps[:, 0:1], scale=1.0 / D)\
                          .then_inc(rms_ready, 1)
                        for t in range(DT):
                            n = r * DT + t
                            act.wait_ge(tr_done, START + i * 2 * DT + n + 1)
                            act.wait_ge(lo_ready, START + i * 2 * DT + (n - 1 if n >= 2 else 0))
                            nc.scalar.activation(h[n % 2][:, :], tr[n % 4][:, :], ACT.Identity,
                                                 bias=k.mod[:, t:t + 1], scale=k.a_mix[:, t:t + 1]).then_inc(h_ready, 1)

            @block.tensor
            def _(pe):
                with pe.Fori(0, NRG // 2) as i:
                    for r in range(2):
                        pe.wait_ge(x_scaled, START + i * NS + (r + 1) * TPG)
                        for t in range(DT):
                            n = r * DT + t
                            pe.wait_ge(h_ready, START + i * 2 * DT + (n - 3 if n >= 4 else 0))
                            for q in range(TPG):
                                last = nc.tensor.transpose(tr[n % 4][:, q * P:(q + 1) * P],
                                                           xs[r * TPG + q][:, t * P:(t + 1) * P], k.ident[:, :])
                            last.then_inc(tr_done, 1)

            @block.vector
            def _(dve):
                with dve.Fori(0, NRG // 2) as i:
                    for r in range(2):
                        g = slice(r * TPG, (r + 1) * TPG)
                        dve.wait_ge(rms_ready, START + i * 2 + r + 1)
                        nc.vector.reciprocal(rstd[:, g], rms[:, g]).then_inc(rstd_ready, 1)
                        dve.wait_ge(rstd_ready, START + i * 2 + r + 1)
                        for s in range(r * TPG, (r + 1) * TPG):
                            nc.vector.tensor_scalar(xs[s][:, :], xs[s][:, :], rstd[:, s:s + 1], None, ALU.mult)\
                              .then_inc(x_scaled, 1)
                        rows = bass.ds((i * 2 + r) * RG, RG)
                        for t in range(DT):
                            n = r * DT + t
                            dve.wait_ge(h_ready, START + i * 2 * DT + n + 1)
                            nc.vector.tensor_copy(h_hi[:, t, rows], h[n % 2][:, :]).then_inc(hi_ready, 1)
                            dve.wait_ge(hi_ready, START + i * 2 * DT + n + 1)
                            nc.vector.tensor_sub(h_lo[:, t, rows], h[n % 2][:, :], f32(h_hi[:, t, rows]))\
                              .then_inc(lo_ready, 1)


def split_product(nc, out, w_hi, w_lo, a_hi, a_lo, first, last):
    nc.tensor.matmul(out, w_hi, a_hi, start=first, stop=False)
    nc.tensor.matmul(out, w_hi, a_lo, start=False, stop=False)
    return nc.tensor.matmul(out, w_lo, a_hi, start=False, stop=last)


def stage_projection(k, w_in, b_forget, h_hi, h_lo, proj, nf_dram):
    nc = k.nc
    with ExitStack() as st:
        raw = [k.sbuf(f"wp_raw{s}", [P, DT, P], stack=st) for s in range(2)]
        hi = [k.sbuf(f"wp_hi{s}", [P, DT, P], F32R, stack=st) for s in range(2)]
        lo = [k.sbuf(f"wp_lo{s}", [P, DT, P], F32R, stack=st) for s in range(2)]
        f_raw = k.sbuf("wf_raw", [P, DT, HB], stack=st)
        f_hi = k.sbuf("wf_hi", [P, DT, HB], F32R, stack=st)
        f_lo = k.sbuf("wf_lo", [P, DT, HB], F32R, stack=st)
        b_f = k.sbuf("b_f", [HB, 1], stack=st)
        out = [k.sbuf(f"proj_out{s}", [P, S], stack=st) for s in range(2)]
        acc = [k.banks(f"proj_acc{s}_", NRG, st) for s in range(2)]
        logit, soft = out[0][0:HB, :], out[1][0:HB, :]
        one = k.sbuf("one_f", [HB, S], stack=st)
        f_in, f_split, f_acc, f_chain = (k.sem("p_" + n) for n in ("f_in", "f_split", "f_acc", "f_chain"))
        f_dve, f_saved = k.sem("p_f_dve"), k.sem("p_f_saved")
        w_ld, w_hi, w_lo = k.sems("p_w_in", 2), k.sems("p_w_hi", 2), k.sems("p_w_lo", 2)
        done, copied, saved = k.sems("p_done", 2), k.sems("p_copied", 2), k.sems("p_saved", 2)
        w_view = w_in.rearrange("o (t p) n -> p (o t) n", p=P)

        start_counts(k)
        with nc.Block() as block:
            @block.sync
            def _(sp):
                with nc.allow_non_contiguous_dma(reason="eight columns of forget gates"):
                    sp.dma_start(f_raw[:, :, :], w_view[:, :, FG0:IN_COLS]).then_inc(f_in, 16)
                    sp.dma_start(b_f[:, :], b_forget.rearrange("o h -> h o")).then_inc(f_in, 16)
                with sp.Fori(0, PT // 2) as i:
                    for s in range(2):
                        sp.wait_ge(w_lo[s], START + i)
                        sp.dma_start(raw[s][:, :, :], w_view[:, :, bass.ds((i * 2 + s) * P, P)]).then_inc(w_ld[s], 16)

            @block.tensor
            def _(pe):
                pe.wait_ge(f_split, START + 2)
                for r in range(NRG):
                    for t in range(DT):
                        a = slice(r * RG, (r + 1) * RG)
                        last = split_product(nc, acc[1][r][0:HB, :], f_hi[:, t, :], f_lo[:, t, :],
                                             h_hi[:, t, a], h_lo[:, t, a], t == 0, t == DT - 1)
                    last.then_inc(f_acc, 1)
                with pe.Fori(0, PT // 2) as i:
                    for s in range(2):
                        pe.wait_ge(w_lo[s], START + i + 1)
                        if s == 1:
                            pe.wait_ge(f_chain, START + NRG)
                        pe.wait_ge(copied[s], START + i * NRG)
                        for r in range(NRG):
                            a = slice(r * RG, (r + 1) * RG)
                            for t in range(DT):
                                last = split_product(nc, acc[s][r][:, :], hi[s][:, t, :], lo[s][:, t, :],
                                                     h_hi[:, t, a], h_lo[:, t, a], t == 0, t == DT - 1)
                            last.then_inc(done[s], 1)

            @block.scalar
            def _(act):
                act.wait_ge(f_in, START + 32)
                for r in range(NRG):
                    act.wait_ge(f_acc, START + r + 1)
                    nc.scalar.activation(logit[:, r * RG:(r + 1) * RG], acc[1][r][0:HB, :], ACT.Identity,
                                         bias=b_f[:, 0:1]).then_inc(f_chain, 1)
                act.wait_ge(f_chain, START + NRG)
                nc.scalar.activation(soft, logit, ACT.Abs).then_inc(f_chain, 1)
                act.wait_ge(f_chain, START + NRG + 1)
                nc.scalar.activation(soft, soft, ACT.Exp, scale=-1.0).then_inc(f_chain, 1)
                act.wait_ge(f_chain, START + NRG + 2)
                nc.scalar.activation(soft, soft, ACT.Ln, bias=1.0).then_inc(f_chain, 1)
                act.wait_ge(f_dve, START + 4)
                act.dma_start(nf_dram, logit).then_inc(f_saved, 16)
                act.wait_ge(f_saved, START + 16)
                with act.Fori(0, PT // 2) as i:
                    for s in range(2):
                        act.wait_ge(saved[s], START + i * 16)
                        for r in range(NRG):
                            act.wait_ge(done[s], START + i * NRG + r + 1)
                            nc.scalar.activation(out[s][:, r * RG:(r + 1) * RG], acc[s][r][:, :], ACT.Copy)\
                              .then_inc(copied[s], 1)
                        act.wait_ge(copied[s], START + (i + 1) * NRG)
                        act.dma_start(proj[bass.ds((i * 2 + s) * P, P), :], out[s][:, :]).then_inc(saved[s], 16)
                for s in range(2):
                    act.wait_ge(saved[s], START + PT // 2 * 16)

            @block.vector
            def _(dve):
                dve.wait_ge(f_in, START + 32)
                nc.vector.tensor_copy(f_hi[:, :, :], f_raw[:, :, :]).then_inc(f_split, 1)
                nc.vector.memset(one[:, :], 1.0).then_inc(f_dve, 1)
                dve.wait_ge(f_split, START + 1)
                nc.vector.tensor_sub(f_lo[:, :, :], f_raw[:, :, :], f32(f_hi[:, :, :])).then_inc(f_split, 1)

                def split(i, s):
                    dve.wait_ge(w_ld[s], START + (i + 1) * 16)
                    dve.wait_ge(done[s], START + i * NRG)
                    nc.vector.tensor_copy(hi[s][:, :, :], raw[s][:, :, :]).then_inc(w_hi[s], 1)
                    dve.wait_ge(w_hi[s], START + i + 1)
                    nc.vector.tensor_sub(lo[s][:, :, :], raw[s][:, :, :], f32(hi[s][:, :, :])).then_inc(w_lo[s], 1)

                split(0, 0)
                split(0, 1)
                dve.wait_ge(f_chain, START + NRG + 3)
                nc.vector.scalar_tensor_tensor(soft, logit, 0.0, soft, ALU.min, ALU.subtract).then_inc(f_dve, 1)
                dve.wait_ge(f_dve, START + 2)
                nc.vector.tensor_tensor_scan(logit, one[:, :], soft, 0.0, ALU.mult, ALU.add).then_inc(f_dve, 1)
                dve.wait_ge(f_dve, START + 3)
                nc.vector.tensor_scalar(logit, logit, -INV_SCALE, None, ALU.mult).then_inc(f_dve, 1)
                with dve.Fori(1, PT // 2) as i:
                    for s in range(2):
                        split(i, s)


def stage_attention_b(k, proj, nf_dram, mask_in, y):
    nc = k.nc
    NP = HB // 2
    units = [(hh, g) for hh in range(2) for g in (3, 2, 1, 0)]
    NU = len(units)
    n_chunks = [TPG * (g + 1) for _, g in units]
    n_keys = [TPG * (g + 1) for _, g in units]
    C0 = [sum(n_chunks[:u]) for u in range(NU + 1)]
    K0 = [sum(n_keys[:u]) for u in range(NU + 1)]
    NC, NK, NT = C0[-1], K0[-1], NU * TPG
    SB, TB = 3, 2
    with ExitStack() as st:
        q_in = [k.sbuf(f"bq_in{s}", [P, S], stack=st) for s in range(2)]
        k_in = [k.sbuf(f"bk_in{s}", [P, S], stack=st) for s in range(2)]
        q_st = [k.sbuf(f"bq{s}", [P, S], F32R, stack=st) for s in range(2)]
        k_hi = [k.sbuf(f"bk_hi{s}", [P, S], F32R, stack=st) for s in range(2)]
        k_lo = [k.sbuf(f"bk_lo{s}", [P, S], F32R, stack=st) for s in range(2)]
        v_in = [k.sbuf(f"bv_in{s}", [HD, S], stack=st) for s in range(2)]
        v_st = [k.sbuf(f"bv{s}", [P, RT, P], F32R, stack=st) for s in range(2)]
        nf = [k.sbuf(f"b_nf{s}", [P, S], stack=st) for s in range(2)]
        pf = [k.sbuf(f"b_pf{s}", [P, RT], stack=st) for s in range(2)]
        bias = [k.sbuf(f"b_bias{s}", [P, S], stack=st) for s in range(2)]
        mask = k.sbuf("b_mask", [P, P], stack=st)
        prob = [[k.sbuf(f"b_p{s}_{t}", [P, S], stack=st) for t in range(TPG)] for s in range(1)]
        mx = k.sbuf("b_mx", [P, TPG], stack=st)
        m8 = k.sbuf("b_m8", [P, 2], stack=st)
        neg_m = k.sbuf("b_neg_m", [P, 2], stack=st)
        den = k.sbuf("b_den", [P, 2, TPG], stack=st)
        rden = k.sbuf("b_rden", [P, 2, TPG], stack=st)
        pt_hi = [k.sbuf(f"b_pt_hi{s}", [P, RG], F32R, stack=st) for s in range(2)]
        pt_lo = [k.sbuf(f"b_pt_lo{s}", [P, RG], F32R, stack=st) for s in range(2)]
        ot = k.sbuf("b_ot", [P, RG], stack=st)
        y_half = k.sbuf("b_y_half", [P, TPG, HD], stack=st)
        y_sum = k.sbuf("b_y_sum", [P, TPG, HD], stack=st)
        y_out = k.sbuf("b_y_out", [P, RT, 2 * HD], stack=st)
        sc = k.banks("b_sc", SB, st)
        tp = k.banks("b_tp", TB, st)
        oacc = k.banks("b_oacc", 1, st)[0]
        yt = k.banks("b_yt", 1, st)[0]
        vt = k.banks("b_vt", 1, st)[0]
        names = ("mask_in", "sc_done", "sc_used", "bias_row", "bias_ready", "mx", "neg_m", "exp", "tp_done",
                 "hi_ready", "lo_ready", "o_done", "ot_ready", "yt_done", "half", "ysum", "y_ready", "rden")
        (mask_ld, sc_done, sc_used, bias_row, bias_ready, mx_ready, neg_ready, exp_done, tp_done, hi_ready, lo_ready,
         o_done, ot_ready, yt_done, half_ready, sum_ready, y_ready, rden_ready) = (k.sem("b_" + n) for n in names)
        y_saved = k.sem("b_y_saved")
        passed = k.sems("b_passed", 3)
        qk_ld, v_ld, nf_ld = k.sems("b_qk_in", 2), k.sems("b_v_in", 2), k.sems("b_nf_in", 2)
        qk_hi, qk_ready = k.sems("b_qk_hi", 2), k.sems("b_qk_ready", 2)
        pf_ready = k.sems("b_pf", 2)
        vt_done, v_hi, v_lo = k.sems("b_vt_done", 2), k.sems("b_v_hi", 2), k.sems("b_v_lo", 2)

        def steps(u):
            n = n_keys[u] // TPG
            return [range(a * n, (a + 1) * n) for a in range(TPG)]

        start_counts(k)
        with nc.Block() as block:
            @block.sync
            def _(sp):
                sp.dma_start(mask[:, :], mask_in).then_inc(mask_ld, 16)
                with sp.Fori(0, NP) as i:
                    for s in range(2):
                        h = i * 2 + s
                        sp.wait_ge(qk_ready[s], START + i * 2)
                        for half in range(2):
                            rows = slice(half * HD, (half + 1) * HD)
                            sp.dma_start(q_in[s][rows, :], proj[bass.ds(QB0 + h * HD, HD), :]).then_inc(qk_ld[s], 16)
                            sp.dma_start(k_in[s][rows, :], proj[bass.ds(KB0 + h * HD, HD), :]).then_inc(qk_ld[s], 16)
                        sp.wait_ge(vt_done[s], START + i * 2)
                        sp.dma_start(v_in[s][:, :], proj[bass.ds(VB0 + h * HD, HD), :]).then_inc(v_ld[s], 16)
                        sp.wait_ge(bias_ready, START + i * NT)
                        sp.dma_start(nf[s][:, :], nf_dram[bass.ds(h, 1), :].to_broadcast([P, S])).then_inc(nf_ld[s], 16)

            @block.gpsimd
            def _(pool):
                pool.wait_ge(mask_ld, START + 16)
                with pool.Fori(0, NP) as i:
                    for u, (hh, g) in enumerate(units):
                        if g == 3:
                            pool.wait_ge(nf_ld[hh], START + (i + 1) * 16)
                            pool.wait_ge(pf_ready[hh], START + i + 1)
                        for t in range(TPG):
                            n, q = u * TPG + t, g * TPG + t
                            c = C0[(n - 2) // TPG] + ((n - 2) % TPG + 1) * (units[(n - 2) // TPG][1] + 1) if n >= 2 else 0
                            wait_apart(pool, passed[0], sc_used, START + i * NC + c)
                            b = bias[n % 2]
                            nc.gpsimd.tensor_scalar(b[:, 0:(q + 1) * P], nf[hh][:, 0:(q + 1) * P], 1.0, pf[hh][:, q:q + 1],
                                                    ALU.mult, ALU.add).then_inc(bias_row, 1)
                            pool.wait_ge(bias_row, START + i * NT + n + 1)
                            last = nc.gpsimd.tensor_tensor(b[:, q * P:(q + 1) * P], b[:, q * P:(q + 1) * P], mask[:, :], ALU.add)
                            last.then_inc(bias_ready, 1)

            @block.tensor
            def _(pe):
                def scores(i, u, t):
                    hh, g = units[u]
                    q = g * TPG + t
                    for c in range(g + 1):
                        n = C0[u] + t * (g + 1) + c
                        w = RG if c < g else (t + 1) * P
                        pe.wait_ge(sc_used, START + i * NC + (n - SB + 1 if n >= SB else 0))
                        a, b = slice(q * P, (q + 1) * P), slice(c * RG, c * RG + w)
                        nc.tensor.matmul(sc[n % SB][:, 0:w], q_st[hh][:, a], k_hi[hh][:, b], start=True, stop=False)
                        nc.tensor.matmul(sc[n % SB][:, 0:w], q_st[hh][:, a], k_lo[hh][:, b], start=False, stop=True)\
                          .then_inc(sc_done, 1)

                def transposes(i, u, j):
                    g, n = units[u][1], K0[u] + j
                    if j == 0:
                        pe.wait_ge(exp_done, START + i * NT + (u + 1) * TPG)
                    pe.wait_ge(lo_ready, START + i * NK + (n - TB + 1 if n >= TB else 0))
                    for t in range(max(0, j - g * TPG), TPG):
                        last = nc.tensor.transpose(tp[n % TB][:, t * P:(t + 1) * P],
                                                   prob[0][t][:, j * P:(j + 1) * P], k.ident[:, :])
                    last.then_inc(tp_done, 1)

                def products(i, u, j):
                    hh, g = units[u]
                    n = K0[u] + j
                    c0 = max(0, j - g * TPG) * P
                    if j == 0:
                        pe.wait_ge(ot_ready, START + i * NU + u)
                    pe.wait_ge(lo_ready, START + i * NK + n + 1)
                    nc.tensor.matmul(oacc[:, c0:RG], v_st[hh][:, j, :], pt_hi[n % 2][:, c0:RG], start=(j == 0), stop=False)
                    last = nc.tensor.matmul(oacc[:, c0:RG], v_st[hh][:, j, :], pt_lo[n % 2][:, c0:RG],
                                            start=False, stop=(j == n_keys[u] - 1))
                    last.then_inc(o_done, 1)

                with pe.Fori(0, NP) as i:
                    for u, (hh, g) in enumerate(units):
                        if g == 3:
                            pe.wait_ge(v_ld[hh], START + (i + 1) * 16)
                            for b in range(2):
                                of, n = (hh, i * 2 + 1) if b else (1 - hh, i * 2 + 2 * hh)
                                wait_apart(pe, passed[2], v_lo[of], START + n)
                                for j in range(8):
                                    last = nc.tensor.transpose(vt[:, j * HD:(j + 1) * HD],
                                                               v_in[hh][:, (b * 8 + j) * P:(b * 8 + j + 1) * P],
                                                               k.ident[0:HD, 0:HD])
                                last.then_inc(vt_done[hh], 1)
                            pe.wait_ge(qk_ready[hh], START + i * 2 + 2)
                            pe.wait_ge(v_lo[hh], START + i * 2 + 2)
                        for t in range(TPG):
                            scores(i, u, t)
                        for j in range(n_keys[u]):
                            transposes(i, u, j)
                            if j:
                                products(i, u, j - 1)
                        products(i, u, n_keys[u] - 1)
                        pe.wait_ge(ot_ready, START + i * NU + u + 1)
                        pe.wait_ge(sum_ready, START + i * NU + u)
                        for t in range(TPG):
                            last = nc.tensor.transpose(yt[:, t * P:(t + 1) * P], ot[:, t * P:(t + 1) * P], k.ident[:, :])
                        last.then_inc(yt_done, 1)

            @block.scalar
            def _(act):
                with act.Fori(0, NP) as i:
                    for u, (hh, g) in enumerate(units):
                        if g == 3:
                            for b in range(2):
                                act.wait_ge(vt_done[hh], START + i * 2 + b + 1)
                                act.wait_ge(o_done, START + i * NK)
                                nc.scalar.activation(v_st[hh][:, b * 8:(b + 1) * 8, 0:HD],
                                                     vt[:, :].rearrange("p (j d) -> p j d", d=HD), ACT.Copy).then_inc(v_hi[hh], 1)
                        for t in range(TPG):
                            n, q = u * TPG + t, g * TPG + t
                            act.wait_ge(neg_ready, START + i * NT + n + 1)
                            nc.scalar.activation(prob[0][t][:, 0:(q + 1) * P], prob[0][t][:, 0:(q + 1) * P], ACT.Exp,
                                                 bias=neg_m[:, n % 2:n % 2 + 1], scale=SCALE,
                                                 accum_out=den[:, u % 2, t:t + 1]).then_inc(exp_done, 1)
                        for j in range(n_keys[u]):
                            n = K0[u] + j
                            c0 = max(0, j - g * TPG) * P
                            act.wait_ge(tp_done, START + i * NK + n + 1)
                            act.wait_ge(o_done, START + i * NK + (n - 1 if n >= 2 else 0))
                            nc.scalar.activation(pt_hi[n % 2][:, c0:RG], tp[n % TB][:, c0:RG], ACT.Copy).then_inc(hi_ready, 1)
                        act.wait_ge(o_done, START + i * NK + K0[u + 1])
                        act.wait_ge(yt_done, START + i * NU + u)
                        nc.scalar.activation(ot[:, :], oacc[:, :], ACT.Copy).then_inc(ot_ready, 1)
                        act.wait_ge(yt_done, START + i * NU + u + 1)
                        act.wait_ge(sum_ready, START + i * NU + u)
                        nc.scalar.activation(y_half[:, :, :], yt[:, :].rearrange("p (t c) -> p t c", c=P)[:, :, HD:P],
                                             ACT.Copy).then_inc(half_ready, 1)
                    act.wait_ge(y_ready, START + (i + 1) * NU)
                    act.dma_start(y[:, bass.ds(WA + i * P, P)].rearrange("(t p) c -> p t c", p=P), y_out[:, :, :])\
                       .then_inc(y_saved, 16)
                act.wait_ge(y_saved, START + NP * 16)

            @block.vector
            def _(dve):
                with dve.Fori(0, NP) as i:
                    for u, (hh, g) in enumerate(units):
                        if g == 3:
                            dve.wait_ge(qk_ld[hh], START + (i + 1) * 64)
                            dve.wait_ge(sc_done, START + i * NC)
                            for a, b in ((k_hi, k_in), (q_st, q_in)):
                                nc.vector.tensor_copy(a[hh][:, :], b[hh][:, :]).then_inc(qk_hi[hh], 1)
                            dve.wait_ge(qk_hi[hh], START + i * 2 + 2)
                            nc.vector.tensor_sub(k_lo[hh][:, :], k_in[hh][:, :], f32(k_hi[hh][:, :])).then_inc(qk_ready[hh], 1)
                            nc.vector.tensor_sub(q_st[hh][HD:P, :], q_in[hh][HD:P, :], f32(q_st[hh][HD:P, :]))\
                              .then_inc(qk_ready[hh], 1)
                            dve.wait_ge(nf_ld[hh], START + (i + 1) * 16)
                            dve.wait_ge(bias_ready, START + i * NT)
                            nc.vector.tensor_scalar(pf[hh][:, :], nf[hh][:, :].rearrange("p (t c) -> p t c", c=P)[:, :, 0],
                                                    -1.0, None, ALU.mult).then_inc(pf_ready[hh], 1)
                            for b in range(2):
                                dve.wait_ge(v_hi[hh], START + i * 2 + b + 1)
                                v = v_st[hh][:, b * 8:(b + 1) * 8, :]
                                nc.vector.tensor_sub(v[:, :, HD:P], vt[:, :].rearrange("p (j d) -> p j d", d=HD),
                                                     f32(v[:, :, 0:HD])).then_inc(v_lo[hh], 1)
                        for t in range(TPG):
                            n, q = u * TPG + t, g * TPG + t
                            dve.wait_ge(bias_ready, START + i * NT + n + 1)
                            if t == 0:
                                dve.wait_ge(tp_done, START + i * NK + K0[u])
                            for c in range(g + 1):
                                m = C0[u] + t * (g + 1) + c
                                w = RG if c < g else (t + 1) * P
                                wait_apart(dve, passed[1], sc_done, START + i * NC + m + 1)
                                cols = slice(c * RG, c * RG + w)
                                nc.vector.tensor_tensor_reduce(out=prob[0][t][:, cols], in0=sc[m % SB][:, 0:w],
                                                               in1=bias[n % 2][:, cols], scale=1.0, scalar=INV_SCALE * NEG,
                                                               op0=ALU.add, op1=ALU.max, accum_out=mx[:, c:c + 1])\
                                  .then_inc(sc_used, 1)
                            dve.wait_ge(sc_used, START + i * NC + C0[u] + (t + 1) * (g + 1))
                            nc.vector.reduce_max(m8[:, n % 2:n % 2 + 1], mx[:, 0:g + 1], AXX).then_inc(mx_ready, 1)
                            dve.wait_ge(mx_ready, START + i * NT + n + 1)
                            dve.wait_ge(exp_done, START + i * NT + (n - 1 if n >= 2 else 0))
                            nc.vector.tensor_scalar(neg_m[:, n % 2:n % 2 + 1], m8[:, n % 2:n % 2 + 1], -SCALE, None,
                                                    ALU.mult).then_inc(neg_ready, 1)
                        dve.wait_ge(exp_done, START + i * NT + (u + 1) * TPG)
                        nc.vector.reciprocal(rden[:, u % 2, :], den[:, u % 2, :]).then_inc(rden_ready, 1)
                        for j in range(n_keys[u]):
                            n = K0[u] + j
                            c0 = max(0, j - g * TPG) * P
                            dve.wait_ge(hi_ready, START + i * NK + n + 1)
                            nc.vector.tensor_sub(pt_lo[n % 2][:, c0:RG], tp[n % TB][:, c0:RG], f32(pt_hi[n % 2][:, c0:RG]))\
                              .then_inc(lo_ready, 1)
                        dve.wait_ge(half_ready, START + i * NU + u + 1)
                        nc.vector.tensor_add(y_sum[:, :, :], yt[:, :].rearrange("p (t c) -> p t c", c=P)[:, :, 0:HD],
                                             y_half[:, :, :]).then_inc(sum_ready, 1)
                        dve.wait_ge(sum_ready, START + i * NU + u + 1)
                        dve.wait_ge(rden_ready, START + i * NU + u + 1)
                        dve.wait_ge(y_saved, START + i * 16)
                        nc.vector.tensor_tensor(y_out[:, g * TPG:(g + 1) * TPG, hh * HD:(hh + 1) * HD], y_sum[:, :, :],
                                                rden[:, u % 2, :].unsqueeze(2).to_broadcast([P, TPG, HD]), ALU.mult)\
                          .then_inc(y_ready, 1)


def stage_attention_a(k, proj, band_in, sinks, y):
    nc = k.nc
    with ExitStack() as st:
        q_in = k.sbuf("aq_in", [P, GA, S], stack=st)
        q_st = k.sbuf("aq", [P, GA, S], F32R, stack=st)
        k_in = k.sbuf("ak_in", [P, S], stack=st)
        k_hi = k.sbuf("ak_hi", [P, S], F32R, stack=st)
        k_lo = k.sbuf("ak_lo", [P, S], F32R, stack=st)
        v_in = k.sbuf("av_in", [HD, S], stack=st)
        v_st = k.sbuf("av", [P, RT, P], F32R, stack=st)
        band = k.sbuf("a_band", [P, GA, BAND], stack=st)
        sink = k.sbuf("a_sink", [P, GA], stack=st)
        prob = [k.sbuf(f"a_p{s}", [P, GA, 2 * P], stack=st) for s in range(2)]
        mx = k.sbuf("a_mx", [P, 2, GA], stack=st)
        m = k.sbuf("a_m", [P, 2, GA], stack=st)
        neg_m = k.sbuf("a_neg_m", [P, 2, GA], stack=st)
        sink_m = k.sbuf("a_sink_m", [P, 2, GA], stack=st)
        sink_e = k.sbuf("a_sink_e", [P, 2, GA], stack=st)
        den = k.sbuf("a_den", [P, 2, GA], stack=st)
        den_all = k.sbuf("a_den_all", [P, 2, GA], stack=st)
        rden = k.sbuf("a_rden", [P, 2, GA], stack=st)
        pt_hi = [k.sbuf(f"a_pt_hi{s}", [P, RG], F32R, stack=st) for s in range(2)]
        pt_lo = [k.sbuf(f"a_pt_lo{s}", [P, RG], F32R, stack=st) for s in range(2)]
        ot = k.sbuf("a_ot", [P, RG], stack=st)
        y_half = k.sbuf("a_y_half", [P, GA, HD], stack=st)
        y_sum = k.sbuf("a_y_sum", [P, GA, HD], stack=st)
        y_out = [k.sbuf(f"a_y_out{s}", [P, GA, HD], stack=st) for s in range(2)]
        sc = [st.enter_context(nc.psum_tensor(f"a_sc{s}", [P, GA, 2 * P], F32)) for s in range(1)]
        tp = k.banks("a_tp", 2, st)
        oacc = k.banks("a_oacc", 1, st)[0]
        yt = k.banks("a_yt", 1, st)[0]
        vt = k.banks("a_vt", 2, st)
        qk_ld, v_ld, band_ld, qk_hi, qk_ready = (k.sem("a_" + n) for n in ("qk_in", "v_in", "band_in", "qk_hi", "qk_ready"))
        vt_done, v_hi, v_lo, zeroed = (k.sem("a_" + n) for n in ("vt_done", "v_hi", "v_lo", "zeroed"))
        names = ("sc_done", "logits", "mx", "m", "neg_m", "exp", "sink_e", "den", "rden", "tp_done",
                 "hi_ready", "lo_ready", "o_done", "ot_ready", "yt_done", "half", "ysum", "y_ready")
        (sc_done, logits, mx_ready, m_ready, neg_ready, exp_done, sink_done, den_ready, rden_ready, tp_done,
         hi_ready, lo_ready, o_done, ot_ready, yt_done, half_ready, sum_ready, y_ready) = (k.sem("a_" + n) for n in names)
        y_saved = k.sems("a_y_saved", 2)
        passed = k.sem("a_passed")
        tiles = [(j, a) for j in range(RT) for a in ((1,) if j == 0 else (0, 1))]
        T0 = [sum(1 for x, _ in tiles if x < j) for j in range(RT + 1)]
        NK = T0[-1]

        start_counts(k)
        with nc.Block() as block:
            @block.sync
            def _(sp):
                with sp.Fori(0, KVA) as i:
                    sp.wait_ge(qk_ready, START + i * 2)
                    for half in range(2):
                        rows = slice(half * HD, (half + 1) * HD)
                        sp.dma_start(k_in[rows, :], proj[bass.ds(KA0 + i * HD, HD), :]).then_inc(qk_ld, 16)
                        sp.dma_start(q_in[rows, :, :], proj[bass.ds(QA0 + i * GA * HD, GA * HD), :]
                                     .rearrange("(g d) s -> d g s", d=HD)).then_inc(qk_ld, 16)
                    sp.wait_ge(vt_done, START + i * 2)
                    sp.dma_start(v_in[:, :], proj[bass.ds(VA0 + i * HD, HD), :]).then_inc(v_ld, 16)
                    sp.wait_ge(logits, START + i * RT)
                    sp.wait_ge(sink_done, START + i * RT)
                    sp.dma_start(band[:, :, :], band_in[bass.ds(i, 1), :, :, :].rearrange("o p g c -> p (o g) c"))\
                      .then_inc(band_ld, 16)
                    sp.dma_start(sink[:, :], sinks[:, bass.ds(i * GA, GA)].to_broadcast([P, GA])).then_inc(band_ld, 16)

            @block.tensor
            def _(pe):
                with pe.Fori(0, KVA) as i:
                    for b in range(2):
                        pe.wait_ge(v_ld, START + (i + 1) * 16)
                        wait_apart(pe, passed, v_lo, START + i * 2)
                        for j in range(8):
                            last = nc.tensor.transpose(vt[b][:, j * HD:(j + 1) * HD],
                                                       v_in[:, (b * 8 + j) * P:(b * 8 + j + 1) * P], k.ident[0:HD, 0:HD])
                        last.then_inc(vt_done, 1)
                    pe.wait_ge(qk_ready, START + i * 2 + 2)

                    def scores(j):
                        pe.wait_ge(logits, START + i * RT + j)
                        c0 = HD if j else P
                        keys = slice((j - 1) * P + c0, (j + 1) * P)
                        for g in range(GA):
                            q = q_st[:, g, j * P:(j + 1) * P]
                            nc.tensor.matmul(sc[0][:, g, c0:], q, k_hi[:, keys], start=True, stop=False)
                            last = nc.tensor.matmul(sc[0][:, g, c0:], q, k_lo[:, keys], start=False, stop=True)
                        last.then_inc(sc_done, 1)

                    def products(j):
                        pe.wait_ge(exp_done, START + i * RT + j + 1)
                        pe.wait_ge(zeroed, START + 2)
                        mine = [(n, a) for n, (x, a) in enumerate(tiles) if x == j]
                        for n, a in mine:
                            pe.wait_ge(lo_ready, START + i * NK + (n - 1 if n >= 2 else 0))
                            for g in range(GA):
                                last = nc.tensor.transpose(tp[n % 2][:, g * P:(g + 1) * P],
                                                           prob[j % 2][:, g, a * P:(a + 1) * P], k.ident[:, :])
                            last.then_inc(tp_done, 1)
                        for n, a in mine:
                            if n == mine[0][0]:
                                pe.wait_ge(ot_ready, START + i * RT + j)
                            pe.wait_ge(lo_ready, START + i * NK + n + 1)
                            v = v_st[:, j - 1 + a, :]
                            nc.tensor.matmul(oacc[:, :], v, pt_hi[n % 2][:, :], start=(n == mine[0][0]), stop=False)
                            nc.tensor.matmul(oacc[:, :], v, pt_lo[n % 2][:, :], start=False, stop=(n == mine[-1][0]))\
                              .then_inc(o_done, 1)
                        pe.wait_ge(ot_ready, START + i * RT + j + 1)
                        pe.wait_ge(sum_ready, START + i * RT + j)
                        for g in range(GA):
                            last = nc.tensor.transpose(yt[:, g * P:(g + 1) * P], ot[:, g * P:(g + 1) * P], k.ident[:, :])
                        last.then_inc(yt_done, 1)

                    pe.wait_ge(v_lo, START + i * 2 + 2)
                    scores(0)
                    for j in range(RT):
                        if j + 1 < RT:
                            scores(j + 1)
                        products(j)

            @block.scalar
            def _(act):
                with act.Fori(0, KVA) as i:
                    for b in range(2):
                        act.wait_ge(vt_done, START + i * 2 + b + 1)
                        act.wait_ge(o_done, START + i * NK)
                        nc.scalar.activation(v_st[:, b * 8:(b + 1) * 8, 0:HD],
                                             vt[b][:, :].rearrange("p (j d) -> p j d", d=HD), ACT.Copy).then_inc(v_hi, 1)

                    def exps(j):
                        act.wait_ge(neg_ready, START + i * RT + j + 1)
                        c0 = HD if j else P
                        for g in range(GA):
                            p = prob[j % 2][:, g, c0:]
                            last = nc.scalar.activation(p, p, ACT.Exp, bias=neg_m[:, j % 2, g:g + 1],
                                                        accum_out=den[:, j % 2, g:g + 1])
                        last.then_inc(exp_done, 1)
                        nc.scalar.activation(sink_e[:, j % 2, :], sink_m[:, j % 2, :], ACT.Exp).then_inc(sink_done, 1)

                    def copies(j):
                        mine = [n for n, (x, _) in enumerate(tiles) if x == j]
                        for n in mine:
                            act.wait_ge(tp_done, START + i * NK + n + 1)
                            act.wait_ge(o_done, START + i * NK + (n - 1 if n >= 2 else 0))
                            nc.scalar.activation(pt_hi[n % 2][:, :], tp[n % 2][:, :], ACT.Copy).then_inc(hi_ready, 1)
                        act.wait_ge(o_done, START + i * NK + mine[-1] + 1)
                        act.wait_ge(yt_done, START + i * RT + j)
                        nc.scalar.activation(ot[:, :], oacc[:, :], ACT.Copy).then_inc(ot_ready, 1)
                        act.wait_ge(yt_done, START + i * RT + j + 1)
                        act.wait_ge(sum_ready, START + i * RT + j)
                        nc.scalar.activation(y_half[:, :, :], yt[:, :].rearrange("p (t c) -> p t c", c=P)[:, :, HD:P],
                                             ACT.Copy).then_inc(half_ready, 1)
                        act.wait_ge(y_ready, START + i * RT + j + 1)
                        act.dma_start(y[j * P:(j + 1) * P, bass.ds(i * GA * HD, GA * HD)],
                                      y_out[j % 2][:, :, :].rearrange("p g d -> p (g d)")).then_inc(y_saved[j % 2], 16)

                    exps(0)
                    for j in range(RT):
                        if j + 1 < RT:
                            exps(j + 1)
                        copies(j)
                for s in range(2):
                    act.wait_ge(y_saved[s], START + KVA * RT // 2 * 16)

            @block.vector
            def _(dve):
                for s in range(2):
                    nc.vector.memset(prob[s][:, :, 0:HD], 0.0).then_inc(zeroed, 1)
                with dve.Fori(0, KVA) as i:
                    dve.wait_ge(qk_ld, START + (i + 1) * 64)
                    dve.wait_ge(sc_done, START + i * RT)
                    nc.vector.tensor_copy(k_hi[:, :], k_in[:, :]).then_inc(qk_hi, 1)
                    nc.vector.tensor_copy(q_st[:, :, :], q_in[:, :, :]).then_inc(qk_hi, 1)
                    dve.wait_ge(qk_hi, START + i * 2 + 2)
                    nc.vector.tensor_sub(k_lo[:, :], k_in[:, :], f32(k_hi[:, :])).then_inc(qk_ready, 1)
                    nc.vector.tensor_sub(q_st[HD:P, :, :], q_in[HD:P, :, :], f32(q_st[HD:P, :, :])).then_inc(qk_ready, 1)
                    for b in range(2):
                        dve.wait_ge(v_hi, START + i * 2 + b + 1)
                        v = v_st[:, b * 8:(b + 1) * 8, :]
                        nc.vector.tensor_sub(v[:, :, HD:P], vt[b][:, :].rearrange("p (j d) -> p j d", d=HD),
                                             f32(v[:, :, 0:HD])).then_inc(v_lo, 1)

                    def maxima(j):
                        s = j % 2
                        c0 = HD if j else P
                        n = i * RT + j + 1
                        dve.wait_ge(sc_done, START + n)
                        if j == 0:
                            dve.wait_ge(band_ld, START + (i + 1) * 32)
                        dve.wait_ge(tp_done, START + i * NK + (T0[j - 1] if j >= 2 else 0))
                        nc.vector.scalar_tensor_tensor(prob[s][:, :, c0:], sc[0][:, :, c0:], SCALE, band[:, :, c0 - HD:],
                                                       ALU.mult, ALU.add).then_inc(logits, 1)
                        dve.wait_ge(logits, START + n)
                        nc.vector.reduce_max(mx[:, s, :], prob[s][:, :, c0:], AXX).then_inc(mx_ready, 1)
                        dve.wait_ge(mx_ready, START + n)
                        nc.vector.tensor_tensor(m[:, s, :], mx[:, s, :], sink[:, :], ALU.max).then_inc(m_ready, 1)
                        dve.wait_ge(m_ready, START + n)
                        dve.wait_ge(sink_done, START + i * RT + (j - 1 if j >= 2 else 0))
                        nc.vector.tensor_sub(sink_m[:, s, :], sink[:, :], m[:, s, :])
                        nc.vector.tensor_scalar(neg_m[:, s, :], m[:, s, :], -1.0, None, ALU.mult).then_inc(neg_ready, 1)

                    def outputs(j):
                        s = j % 2
                        n = i * RT + j + 1
                        dve.wait_ge(sink_done, START + n)
                        dve.wait_ge(exp_done, START + n)
                        nc.vector.tensor_add(den_all[:, s, :], den[:, s, :], sink_e[:, s, :]).then_inc(den_ready, 1)
                        dve.wait_ge(den_ready, START + n)
                        nc.vector.reciprocal(rden[:, s, :], den_all[:, s, :]).then_inc(rden_ready, 1)
                        for x in [x for x, (u, _) in enumerate(tiles) if u == j]:
                            dve.wait_ge(hi_ready, START + i * NK + x + 1)
                            nc.vector.tensor_sub(pt_lo[x % 2][:, :], tp[x % 2][:, :], f32(pt_hi[x % 2][:, :])).then_inc(lo_ready, 1)
                        dve.wait_ge(half_ready, START + n)
                        nc.vector.tensor_add(y_sum[:, :, :], yt[:, :].rearrange("p (t c) -> p t c", c=P)[:, :, 0:HD],
                                             y_half[:, :, :]).then_inc(sum_ready, 1)
                        dve.wait_ge(sum_ready, START + n)
                        dve.wait_ge(rden_ready, START + n)
                        dve.wait_ge(y_saved[s], START + i * (RT // 2 * 16) + j // 2 * 16)
                        nc.vector.tensor_tensor(y_out[s][:, :, :], y_sum[:, :, :],
                                                rden[:, s, :].unsqueeze(2).to_broadcast([P, GA, HD]), ALU.mult)\
                          .then_inc(y_ready, 1)

                    maxima(0)
                    for j in range(RT):
                        if j + 1 < RT:
                            maxima(j + 1)
                        outputs(j)


def stage_output(k, y, x, w_out, w_gate_up, w_down, eps, out):
    nc = k.nc
    NSLOT = 4
    DOWN = [(0, 8), (8, 8), (16, FT - 16)]
    with ExitStack() as st:
        raw = [k.sbuf(f"w_raw{s}", [P, DT, P], stack=st) for s in range(NSLOT)]
        hi = [k.sbuf(f"w_hi{s}", [P, DT, P], F32R, stack=st) for s in range(NSLOT)]
        lo = [k.sbuf(f"w_lo{s}", [P, DT, P], F32R, stack=st) for s in range(NSLOT)]
        act_at = nc.sbuf_base
        act_hi = k.sbuf("act_hi", [P, FT, RG], F32R, stack=st)
        act_lo = k.sbuf("act_lo", [P, FT, RG], F32R, stack=st)
        h_hi = k.sbuf("g_hi", [P, DT, RG], F32R, stack=st)
        h_lo = k.sbuf("g_lo", [P, DT, RG], F32R, stack=st)
        xt = k.sbuf("xt", [P, DT, RG], stack=st)
        assert nc.sbuf_base >= act_at + 2 * FT * RG * 4 and act_at % 32 == 0
        rows = nc.alloc_sbuf_tensor_at("rows", [P, 2 * TPG + 1, D], F32, offset=act_at)
        y_row = [rows[:, t, :] for t in range(TPG)]
        x_row = [rows[:, TPG + t, :] for t in range(TPG)]
        o_row = y_row
        junk = rows[:, 2 * TPG, :]
        tmp = [k.sbuf(f"o_tmp{s}", [P, RG], stack=st) for s in range(2)]
        sq_hi = k.sbuf("sq_hi", [P, RG], F32R, stack=st)
        sq_lo = k.sbuf("sq_lo", [P, RG], F32R, stack=st)
        rms = k.sbuf("o_rms", [P, RG], stack=st)
        rstd = k.sbuf("o_rstd", [P, RG], stack=st)
        ssq = k.sbuf("o_ssq", [P, 2 * TPG], stack=st)
        g_rms = k.sbuf("g_rms", [P, 2 * TPG], stack=st)
        g_rstd = k.sbuf("g_rstd", [P, 2 * TPG], stack=st)
        bank = k.banks("o_bank", 8, st)
        w_ld, w_hi, w_lo, w_used = (k.sems("o_" + n, NSLOT) for n in ("w_in", "w_hi", "w_lo", "w_used"))
        names = ("y_in", "x_in", "squared", "rms1", "rstd1", "scaled", "tr", "tr_copied", "h_f", "h_hi", "h_lo",
                 "resid", "sq", "sq_hi", "sq_lo", "sum", "rms", "rstd", "xn", "silu", "act_f", "act_hi",
                 "act_lo", "final", "fin_t", "o_ready")
        S_ = {n: k.sem("o_" + n) for n in names}
        saved = k.sem("o_saved")
        wo_v = w_out.rearrange("o (t p) n -> p (o t) n", p=P)
        wg_v = w_gate_up.rearrange("o (t p) n -> p (o t) n", p=P)
        wd_v = w_down.rearrange("o (t p) n -> p (o t) n", p=P)
        y_v = y.rearrange("(t p) d -> t p d", p=P)
        x_v = x.rearrange("o (t p) d -> (o t) p d", p=P)
        o_v = out.rearrange("o (t p) d -> (o t) p d", p=P)
        N_OUT, N_UP, N_DN = DT, 2 * FT, len(DOWN) * DT
        NW = N_OUT + N_UP + N_DN
        PER = NW // NSLOT
        UP0, DN0 = N_OUT // NSLOT, (N_OUT + N_UP) // NSLOT
        one = lambda v, n: v[bass.ds(n, 1), :, :].rearrange("o p d -> p (o d)")

        start_counts(k)
        with nc.Block() as block:
            @block.sync
            def _(sp):
                def load(n, dst, src):
                    s, t = n
                    sp.wait_ge(w_lo[s], START + t)
                    sp.dma_start(dst, src).then_inc(w_ld[s], 16)

                with sp.Fori(0, NRG) as r:
                    with sp.Fori(0, N_OUT // NSLOT) as a:
                        for s in range(NSLOT):
                            load((s, r * PER + a), raw[s][:, :, :], wo_v[:, :, bass.ds((a * NSLOT + s) * P, P)])
                    with sp.Fori(0, FT // 2) as a:
                        for s in range(NSLOT):
                            col = (a * 2 + s // 2) * P + (s % 2) * DFF
                            load((s, r * PER + a + N_OUT // NSLOT), raw[s][:, :, :], wg_v[:, :, bass.ds(col, P)])
                    with sp.Fori(0, DT // 4) as a:
                        for n in range(12):
                            t0, nt = DOWN[n % 3]
                            load((n % NSLOT, r * PER + (N_OUT + N_UP) // NSLOT + a * 3 + n // NSLOT),
                                 raw[n % NSLOT][:, 0:nt, :], wd_v[:, t0:t0 + nt, bass.ds((a * 4 + n // 3) * P, P)])

            @block.tensor
            def _(pe):
                def product(r, banks, use, rhs_hi, rhs_lo, nt, first, last):
                    s, t = use
                    pe.wait_ge(w_lo[s], START + t + 1)
                    for j in range(nt):
                        x_ = split_product(nc, banks, hi[s][:, j, :], lo[s][:, j, :], rhs_hi(j), rhs_lo(j),
                                           first and j == 0, last and j == nt - 1)
                    x_.then_inc(w_used[s], 1)

                def sums(r, half):
                    for t in range(DT):
                        n = half * DT + t
                        pe.wait_ge(S_["sq_lo"], START + r * (2 * DT) + n + 1)
                        nc.tensor.matmul(bank[7][:, :], k.ones_r[:, :], sq_hi[:, :], start=(t == 0), stop=False)
                        nc.tensor.matmul(bank[7][:, :], k.ones_r[:, :], sq_lo[:, :], start=False, stop=(t == DT - 1))\
                          .then_inc(S_["sum"], 1)

                with pe.Fori(0, NRG) as r:
                    pe.wait_ge(S_["scaled"], START + (r + 1) * 8)
                    for n in range(2 * DT):
                        if n == DT:
                            pe.wait_ge(S_["x_in"], START + (r + 1) * (TPG * 16))
                        pe.wait_ge(S_["tr_copied"], START + r * (2 * DT) + (n - 3 if n >= 4 else 0))
                        of = y_row if n < DT else x_row
                        for q in range(TPG):
                            last = nc.tensor.transpose(bank[n % 4][:, q * P:(q + 1) * P],
                                                       of[q][:, (n % DT) * P:(n % DT + 1) * P], k.ident[:, :])
                        last.then_inc(S_["tr"], 1)
                    pe.wait_ge(S_["h_lo"], START + r * (2 * DT) + DT)
                    for t in range(DT):
                        pe.wait_ge(S_["resid"], START + r * DT + (t - 2 if t >= 3 else 0))
                        product(r, bank[4 + t % 3][:, :], (t % NSLOT, r * PER + t // NSLOT),
                                lambda j: h_hi[:, j, :], lambda j: h_lo[:, j, :], DT, True, True)
                    sums(r, 0)
                    with pe.Fori(0, FT // 2) as a:
                        pe.wait_ge(S_["h_lo"], START + (r + 1) * (2 * DT))
                        for n in range(4):
                            if n % 2 == 0:
                                pe.wait_ge(S_["act_f"], START + r * FT + a * 2 + (0 if n == 0 else 0))
                            product(r, bank[n][:, :], (n, r * PER + a + N_OUT // NSLOT),
                                    lambda j: h_hi[:, j, :], lambda j: h_lo[:, j, :], DT, True, True)
                    with pe.Fori(0, DT // 4) as a:
                        pe.wait_ge(S_["act_lo"], START + (r + 1) * FT)
                        for n in range(12):
                            t0, nt = DOWN[n % 3]
                            if n % 3 == 0:
                                pe.wait_ge(S_["final"], START + r * DT + a * 4 + (n // 3 - 1 if n >= 6 else 0))
                            product(r, bank[4 + (n // 3) % 2][:, :],
                                         (n % NSLOT, r * PER + (N_OUT + N_UP) // NSLOT + a * 3 + n // NSLOT),
                                         lambda j: act_hi[:, t0 + j, :], lambda j: act_lo[:, t0 + j, :], nt,
                                         n % 3 == 0, n % 3 == 2)
                    sums(r, 1)
                    pe.wait_ge(S_["xn"], START + r * (2 * DT) + 2 * DT)
                    for n in range(2 * TPG):
                        q, half = n // 2, n % 2
                        pe.wait_ge(S_["o_ready"], START + r * (2 * TPG) + (n - 3 if n >= 4 else 0))
                        for t in range(4):
                            last = nc.tensor.transpose(bank[n % 4][:, t * P:(t + 1) * P],
                                                       xt[:, half * 4 + t, q * P:(q + 1) * P], k.ident[:, :])
                        last.then_inc(S_["fin_t"], 1)

            @block.scalar
            def _(act):
                def squares(r, half):
                    for t in range(DT):
                        n = half * DT + t
                        act.wait_ge(S_["final" if half else "resid"], START + r * DT + t + 1)
                        act.wait_ge(S_["sq_lo"], START + r * (2 * DT) + (n - 1 if n >= 2 else 0))
                        nc.scalar.activation(tmp[t % 2][:, :], xt[:, t, :], ACT.Square).then_inc(S_["sq"], 1)
                    act.wait_ge(S_["sum"], START + r * (2 * DT) + (half + 1) * DT)
                    nc.scalar.activation(rms[:, :], bank[7][:, :], ACT.Sqrt, bias=eps[:, 0:1], scale=1.0 / D)\
                      .then_inc(S_["rms"], 1)

                with act.Fori(0, NRG) as r:
                    act.wait_ge(saved, START + r * (TPG * 16))
                    for t in range(TPG):
                        act.dma_start(y_row[t], one(y_v, r * TPG + t)).then_inc(S_["y_in"], 16)
                    for t in range(TPG):
                        act.dma_start(x_row[t], one(x_v, r * TPG + t)).then_inc(S_["x_in"], 16)
                    act.wait_ge(S_["y_in"], START + (r + 1) * (TPG * 16))
                    act.wait_ge(S_["rstd1"], START + r)
                    for t in range(TPG):
                        for a in range(2):
                            act.wait_ge(S_["squared"], START + r * 8 + 2 * t)
                            nc.scalar.activation(junk[:, a * WA:(a + 1) * WA], y_row[t][:, a * WA:(a + 1) * WA], ACT.Square,
                                                 accum_out=ssq[:, 2 * t + a:2 * t + a + 1]).then_inc(S_["squared"], 1)
                    act.wait_ge(S_["squared"], START + (r + 1) * 8)
                    nc.scalar.activation(g_rms[:, :], ssq[:, :], ACT.Sqrt, bias=eps[:, 0:1], scale=1.0 / WA)\
                      .then_inc(S_["rms1"], 1)
                    for n in range(2 * DT):
                        t = n % DT
                        act.wait_ge(S_["tr"], START + r * (2 * DT) + n + 1)
                        if n < DT:
                            act.wait_ge(S_["h_lo"], START + r * (2 * DT) + (n - 1 if n >= 2 else 0))
                            nc.scalar.activation(tmp[n % 2][:, :], bank[n % 4][:, :], ACT.Copy,
                                                 scale=k.cols[:, V_GGRP + t:V_GGRP + t + 1]).then_inc(S_["tr_copied"], 1)
                        else:
                            nc.scalar.activation(xt[:, t, :], bank[n % 4][:, :], ACT.Copy).then_inc(S_["tr_copied"], 1)
                    squares(r, 0)
                    for t in range(DT):
                        act.wait_ge(S_["xn"], START + r * (2 * DT) + t + 1)
                        nc.scalar.activation(tmp[t % 2][:, :], tmp[t % 2][:, :], ACT.Identity,
                                             bias=k.mod[:, 3 * DT + t:3 * DT + t + 1], scale=k.a_ffn[:, t:t + 1])\
                          .then_inc(S_["h_f"], 1)
                    with act.Fori(0, FT // 2) as a:
                        for n in range(2):
                            act.wait_ge(w_used[2 * n], START + r * PER + UP0 + a + 1)
                            act.wait_ge(S_["act_lo"], START + r * FT + a * 2)
                            nc.scalar.activation(tmp[n][:, :], bank[2 * n][:, :], ACT.Silu).then_inc(S_["silu"], 1)
                    squares(r, 1)
                    for n in range(2 * TPG):
                        q, half = n // 2, n % 2
                        act.wait_ge(S_["fin_t"], START + r * (2 * TPG) + n + 1)
                        nc.scalar.activation(o_row[q][:, half * RG:(half + 1) * RG], bank[n % 4][:, :], ACT.Copy)\
                          .then_inc(S_["o_ready"], 1)
                        if half:
                            act.wait_ge(S_["o_ready"], START + r * (2 * TPG) + n + 1)
                            act.dma_start(one(o_v, r * TPG + q), o_row[q]).then_inc(saved, 16)
                act.wait_ge(saved, START + NRG * TPG * 16)

            @block.vector
            def _(dve):
                def split(use, nt=DT):
                    s, t = use
                    dve.wait_ge(w_ld[s], START + (t + 1) * 16)
                    dve.wait_ge(w_used[s], START + t)
                    nc.vector.tensor_copy(hi[s][:, 0:nt, :], raw[s][:, 0:nt, :]).then_inc(w_hi[s], 1)
                    dve.wait_ge(w_hi[s], START + t + 1)
                    nc.vector.tensor_sub(lo[s][:, 0:nt, :], raw[s][:, 0:nt, :], f32(hi[s][:, 0:nt, :])).then_inc(w_lo[s], 1)

                def square_parts(r, half):
                    for t in range(DT):
                        n = half * DT + t
                        dve.wait_ge(S_["sq"], START + r * (2 * DT) + n + 1)
                        dve.wait_ge(S_["sum"], START + r * (2 * DT) + n)
                        nc.vector.tensor_copy(sq_hi[:, :], tmp[t % 2][:, :]).then_inc(S_["sq_hi"], 1)
                        dve.wait_ge(S_["sq_hi"], START + r * (2 * DT) + n + 1)
                        nc.vector.tensor_sub(sq_lo[:, :], tmp[t % 2][:, :], f32(sq_hi[:, :])).then_inc(S_["sq_lo"], 1)
                    dve.wait_ge(S_["rms"], START + r * 2 + half + 1)
                    nc.vector.reciprocal(rstd[:, :], rms[:, :]).then_inc(S_["rstd"], 1)
                    dve.wait_ge(S_["rstd"], START + r * 2 + half + 1)

                def h_parts(r, n, t):
                    nc.vector.tensor_copy(h_hi[:, t, :], tmp[t % 2][:, :]).then_inc(S_["h_hi"], 1)
                    dve.wait_ge(S_["h_hi"], START + r * (2 * DT) + n + 1)
                    nc.vector.tensor_sub(h_lo[:, t, :], tmp[t % 2][:, :], f32(h_hi[:, t, :])).then_inc(S_["h_lo"], 1)

                with dve.Fori(0, NRG) as r:
                    dve.wait_ge(S_["rms1"], START + r + 1)
                    nc.vector.reciprocal(g_rstd[:, :], g_rms[:, :]).then_inc(S_["rstd1"], 1)
                    dve.wait_ge(S_["rstd1"], START + r + 1)
                    for t in range(TPG):
                        for a in range(2):
                            c = slice(a * WA, (a + 1) * WA)
                            nc.vector.tensor_scalar(y_row[t][:, c], y_row[t][:, c], g_rstd[:, 2 * t + a:2 * t + a + 1], None,
                                                    ALU.mult).then_inc(S_["scaled"], 1)
                    for t in range(DT):
                        dve.wait_ge(S_["tr_copied"], START + r * (2 * DT) + t + 1)
                        h_parts(r, t, t)
                    for s in range(NSLOT):
                        split((s, r * PER))
                    dve.wait_ge(S_["tr_copied"], START + (r + 1) * (2 * DT))
                    for t in range(DT):
                        if t < NSLOT:
                            split((t, r * PER + 1))
                        dve.wait_ge(w_used[t % NSLOT], START + r * PER + t // NSLOT + 1)
                        nc.vector.scalar_tensor_tensor(xt[:, t, :], bank[4 + t % 3][:, :], k.mod[:, 2 * DT + t:2 * DT + t + 1],
                                                       xt[:, t, :], ALU.mult, ALU.add).then_inc(S_["resid"], 1)
                    for s in range(NSLOT):
                        split((s, r * PER + UP0))
                    square_parts(r, 0)
                    for t in range(DT):
                        dve.wait_ge(S_["h_lo"], START + r * (2 * DT) + DT + (t - 1 if t >= 2 else 0))
                        nc.vector.tensor_tensor(tmp[t % 2][:, :], xt[:, t, :], rstd[:, :], ALU.mult).then_inc(S_["xn"], 1)
                        dve.wait_ge(S_["h_f"], START + r * DT + t + 1)
                        h_parts(r, DT + t, t)

                    def gated(a, n):
                        f = r * FT + a * 2 + n
                        ft = a * 2 + n
                        dve.wait_ge(S_["silu"], START + f + 1)
                        dve.wait_ge(w_used[2 * n + 1], START + r * PER + UP0 + a + 1)
                        nc.vector.tensor_tensor(tmp[n][:, :], bank[2 * n + 1][:, :], tmp[n][:, :], ALU.mult).then_inc(S_["act_f"], 1)
                        dve.wait_ge(S_["act_f"], START + f + 1)
                        nc.vector.tensor_copy(act_hi[:, bass.ds(ft, 1), :].rearrange("p o n -> p (o n)"), tmp[n][:, :])\
                          .then_inc(S_["act_hi"], 1)
                        dve.wait_ge(S_["act_hi"], START + f + 1)
                        nc.vector.tensor_sub(act_lo[:, bass.ds(ft, 1), :].rearrange("p o n -> p (o n)"), tmp[n][:, :],
                                             f32(act_hi[:, bass.ds(ft, 1), :].rearrange("p o n -> p (o n)")))\
                           .then_inc(S_["act_lo"], 1)

                    with dve.Fori(0, FT // 2 - 1) as a:
                        for n in range(2):
                            gated(a, n)
                            for s in (2 * n, 2 * n + 1):
                                split((s, r * PER + UP0 + a + 1))
                    for n in range(2):
                        gated(FT // 2 - 1, n)
                        for s in (2 * n, 2 * n + 1):
                            split((s, r * PER + DN0), DOWN[s % 3][1])
                    def finish(a, t):
                        dve.wait_ge(w_used[(3 * t + 2) % NSLOT], START + r * PER + DN0 + a * 3 + (3 * t + 2) // NSLOT + 1)
                        col = bass.ds(a * 4 + t, 1)
                        nc.vector.scalar_tensor_tensor(xt[:, col, :].rearrange("p o n -> p (o n)"), bank[4 + t % 2][:, :],
                                                       k.mod[:, bass.ds(a * 4 + t + 5 * DT, 1)],
                                                       xt[:, col, :].rearrange("p o n -> p (o n)"),
                                                       ALU.mult, ALU.add).then_inc(S_["final"], 1)
                    for a in range(DT // 4):
                        for n in range(12):
                            m = a * 12 + n + NSLOT
                            if m < N_DN:
                                split((m % NSLOT, r * PER + DN0 + m // NSLOT), DOWN[m % 3][1])
                            if n % 3 == 2:
                                finish(a, n // 3)
                    square_parts(r, 1)
                    for t in range(DT):
                        nc.vector.scalar_tensor_tensor(xt[:, t, :], xt[:, t, :], k.cols[:, V_GFIN + t:V_GFIN + t + 1],
                                                       rstd[:, :], ALU.mult, ALU.mult).then_inc(S_["xn"], 1)


def build(nc, x, c, w_ada, b_ada, g_norm_mix, w_in, b_forget, sinks, g_grp_a, g_grp_b, w_out, g_norm_ffn,
          w_gate_up, w_down, g_final, ident, ones, mask, band, out):
    proj = nc.dram_tensor("proj_t", (PT * P, S), F32, kind="Internal").ap()
    nf = nc.dram_tensor("neg_f8", (HB, S), F32, kind="Internal").ap()
    y = nc.dram_tensor("y_heads", (S, WA + WB), F32, kind="Internal").ap()
    as_rows = lambda v: v.rearrange("o (t p) -> (o t) p", p=P)
    vectors = [(V_BADA, as_rows(b_ada)), (V_GMIX, as_rows(g_norm_mix)), (V_GFFN, as_rows(g_norm_ffn)),
               (V_GFIN, g_final.rearrange("(t p) -> t p", p=P)), (V_GGRP, as_rows(g_grp_a)),
               (V_GGRP + WA // P, as_rows(g_grp_b))]
    with ExitStack() as stack:
        k = Core(nc, stack)
        eps = k.sbuf("eps", [P, 1])
        eps_set = k.sem("eps_set")
        with nc.Block() as block:
            @block.vector
            def _(dve):
                nc.vector.memset(eps[:, :], EPS).then_inc(eps_set, 1)
                dve.wait_ge(eps_set, 1)
        stage_modulation(k, c, w_ada, vectors, ident, ones)
        k.end_stage()
        with ExitStack() as st:
            h_hi = k.sbuf("h_hi", [P, DT, S], F32R, stack=st)
            h_lo = k.sbuf("h_lo", [P, DT, S], F32R, stack=st)
            stage_input_norm(k, x, eps, h_hi, h_lo, st)
            k.end_stage()
            stage_projection(k, w_in, b_forget, h_hi, h_lo, proj, nf)
            k.end_stage()
        stage_attention_b(k, proj, nf, mask, y)
        k.end_stage()
        stage_attention_a(k, proj, band, sinks, y)
        k.end_stage()
        stage_output(k, y, x, w_out, w_gate_up, w_down, eps, out)


_INS = ["x", "c", "w_ada", "b_ada", "g_norm_mix", "w_in", "b_forget", "sinks", "g_grp_a", "g_grp_b", "w_out",
        "g_norm_ffn", "w_gate_up", "w_down", "g_final"]


def _constants():
    import numpy as np
    q, key = np.arange(P)[:, None], np.arange(P)[None, :]
    mask = np.where(key <= q, 0.0, INV_SCALE * NEG).astype(np.float32)
    chunk = 64
    kb = np.arange(BAND)[None, :]
    dist = np.abs(q - (kb - chunk)).astype(np.float32)
    seen = (kb // chunk >= q // chunk) & (kb // chunk <= q // chunk + 1)
    slopes = np.exp2(-8.0 * (np.arange(HA, dtype=np.float32) + 1.0) / HA).astype(np.float32)
    band = np.where(seen[None], -slopes[:, None, None] * dist[None], np.float32(NEG)).astype(np.float32)
    band = np.ascontiguousarray(band.reshape(KVA, GA, P, BAND).transpose(0, 2, 1, 3))
    return {"ident": np.eye(P, dtype=np.float32), "ones": np.ones((P, P), np.float32), "mask": mask, "band": band}


def kernel(**inputs):
    import numpy as np
    import concourse.bacc as bacc
    from concourse.bass_utils import run_bass_kernel_spmd as run

    nc = bacc.Bacc("TRN2", target_bir_lowering=False, num_devices=1)
    arrays, args = {}, []
    for name, a in [(n, np.ascontiguousarray(inputs[n])) for n in _INS] + list(_constants().items()):
        arrays[f"in_{name}"] = a
        args.append(nc.dram_tensor(f"in_{name}", a.shape, mybir.dt.from_np(a.dtype), kind="ExternalInput").ap())
    args.append(nc.dram_tensor("out", (1, S, D), F32, kind="ExternalOutput").ap())
    build(nc, *args)
    r = run(nc, [arrays], core_ids=[0])
    return r.results[0]["out"]
```

```python
from contextlib import ExitStack

import concourse.bass as bass
from concourse import mybir
from concourse.alu_op_type import AluOpType as ALU

F32 = mybir.dt.float32
F32R = mybir.dt.float32r
ACT = mybir.ActivationFunctionType
AXX = mybir.AxisListType.X

P = 128
D = 1024
S = 2048
HD = 64
HA, KVA, HB = 8, 2, 8
GA = HA // KVA
WA, WB = HA * HD, HB * HD
DFF = 2816
EPS = 1e-6
START = 128
SCALE = HD ** -0.5
INV_SCALE = 8.0
NEG = -1e30
DT = D // P
RT = S // P
RG = 512
NRG = S // RG
TPG = RG // P
FT = DFF // P
QA0, KA0, VA0 = 0, WA, WA + KVA * HD
QB0 = VA0 + KVA * HD
KB0, VB0, FG0 = QB0 + WB, QB0 + 2 * WB, QB0 + 3 * WB
IN_COLS = FG0 + HB
PT = FG0 // P
BAND = 192
V_BADA, V_GMIX, V_GFFN, V_GFIN, V_GGRP = 0, 48, 56, 64, 72
V_ROWS = 80


class Core:

    def __init__(self, nc, stack):
        self.nc, self.stack, self.stage_sems = nc, stack, []
        self.ident = self.sbuf("ident", [P, P])
        self.ones_r = self.sbuf("ones_r", [P, P], F32R)
        self.cols = self.sbuf("cols", [P, V_ROWS])
        self.mod = self.sbuf("mod", [P, 48])
        self.a_mix = self.sbuf("a_mix", [P, DT])
        self.a_ffn = self.sbuf("a_ffn", [P, DT])

    def sbuf(self, name, shape, dt=F32, stack=None):
        return (stack or self.stack).enter_context(self.nc.sbuf_tensor(name, shape, dt))

    def banks(self, name, n, stack):
        return [stack.enter_context(self.nc.psum_tensor(f"{name}{i}", [P, RG], F32)) for i in range(n)]

    def sem(self, name):
        self.stage_sems.append(self.nc.alloc_semaphore(name=name))
        return self.stage_sems[-1]

    def end_stage(self):
        self.nc.clear_and_free_semaphores(self.stage_sems)
        self.stage_sems = []
        self.nc.all_engine_barrier()

    def sems(self, name, n):
        return [self.sem(f"{name}{i}") for i in range(n)]


def start_counts(k):
    with k.nc.Block() as block:
        @block.gpsimd
        def _(pool):
            for sem in k.stage_sems:
                pool.sem_inc(sem, START)


def wait_apart(eng, passed, sem, value):
    eng.wait_ge(sem, value)
    eng.sem_inc(passed, 1)


def f32(ap):
    return ap.bitcast(F32)


def stage_modulation(k, c, w_ada, vectors, ident_in, ones_in):
    nc = k.nc
    CH, SL = 12, 4
    with ExitStack() as st:
        c_col = k.sbuf("c_col", [P, DT], stack=st)
        c_act = k.sbuf("c_act", [P, DT], stack=st)
        table = k.sbuf("table", [V_ROWS, P], stack=st)
        ones = k.sbuf("ones_raw", [P, P], stack=st)
        w = [k.sbuf(f"w_ada{s}", [P, DT, RG], stack=st) for s in range(SL)]
        row = k.sbuf("mod_row", [1, CH * RG], stack=st)
        acc = k.banks("mod_acc", SL, st)
        small = k.banks("mod_col", 2, st)
        const_in, c_in = k.sem("const_in"), k.sem("c_in")
        w_in = k.sems("w_ada_in", SL)
        c_ready, ones_ready = k.sem("c_ready"), k.sem("ones_ready")
        table_t, table_used = k.sem("table_t"), k.sem("table_used")
        prod = k.sems("ada_product", SL)
        row_ready = k.sems("ada_row", SL)
        mod_t, mod_ready = k.sem("mod_t"), k.sem("mod_ready")
        w_view = w_ada.rearrange("o (p t) n -> p (o t) n", t=DT)

        start_counts(k)
        with nc.Block() as block:
            @block.sync
            def _(sp):
                sp.dma_start(c_col[:, :], c.rearrange("o (p t) -> p (o t)", t=DT)).then_inc(c_in, 16)
                sp.dma_start(k.ident[:, :], ident_in).then_inc(const_in, 16)
                sp.dma_start(ones[:, :], ones_in).then_inc(const_in, 16)
                for at, v in vectors:
                    n = v.shape[0]
                    sp.dma_start(table[at:at + n, :], v).then_inc(const_in, 16)
                with sp.Fori(0, CH // SL) as i:
                    for s in range(SL):
                        sp.wait_ge(prod[s], START + i)
                        sp.dma_start(w[s][:, :, :], w_view[:, :, bass.ds((i * SL + s) * RG, RG)]).then_inc(w_in[s], 16)

            @block.scalar
            def _(act):
                act.wait_ge(c_in, START + 16)
                nc.scalar.activation(c_act[:, :], c_col[:, :], ACT.Silu).then_inc(c_ready, 1)

            @block.tensor
            def _(pe):
                pe.wait_ge(const_in, START + 16 * (2 + len(vectors)))
                nc.tensor.transpose(small[0][:, 0:V_ROWS], table[:, :], k.ident[0:V_ROWS, 0:V_ROWS]).then_inc(table_t, 1)
                pe.wait_ge(c_ready, START + 1)
                with pe.Fori(0, CH // SL) as i:
                    for s in range(SL):
                        pe.wait_ge(w_in[s], START + (i + 1) * 16)
                        pe.wait_ge(row_ready[s], START + i)
                        for t in range(DT):
                            last = nc.tensor.matmul(acc[s][0:1, :], c_act[:, t:t + 1], w[s][:, t, :],
                                                    start=(t == 0), stop=(t == DT - 1))
                        last.then_inc(prod[s], 1)
                for s in range(SL):
                    pe.wait_ge(row_ready[s], START + CH // SL)
                for j in range(48):
                    last = nc.tensor.matmul(small[1][:, j:j + 1], row[0:1, j * P:(j + 1) * P], k.ident[0:1, 0:1],
                                            start=True, stop=True)
                last.then_inc(mod_t, 1)

            @block.vector
            def _(dve):
                dve.wait_ge(const_in, START + 16 * (2 + len(vectors)))
                nc.vector.tensor_copy(k.ones_r[:, :], ones[:, :]).then_inc(ones_ready, 1)
                dve.wait_ge(table_t, START + 1)
                nc.vector.tensor_copy(k.cols[:, :], small[0][:, 0:V_ROWS]).then_inc(table_used, 1)
                with dve.Fori(0, CH // SL) as i:
                    for s in range(SL):
                        dve.wait_ge(prod[s], START + i + 1)
                        nc.vector.tensor_copy(row[0:1, bass.ds((i * SL + s) * RG, RG)], acc[s][0:1, :]).then_inc(row_ready[s], 1)
                dve.wait_ge(mod_t, START + 1)
                dve.wait_ge(table_used, START + 1)
                nc.vector.tensor_add(k.mod[:, :], small[1][:, 0:48], k.cols[:, V_BADA:V_BADA + 48]).then_inc(mod_ready, 1)
                dve.wait_ge(mod_ready, START + 1)
                for a, g, j in ((k.a_mix, V_GMIX, 1), (k.a_ffn, V_GFFN, 4)):
                    nc.vector.scalar_tensor_tensor(a[:, :], k.mod[:, DT * j:DT * (j + 1)], 1.0, k.cols[:, g:g + DT],
                                                   ALU.add, ALU.mult).then_inc(mod_ready, 1)


def stage_input_norm(k, x, eps, h_hi, h_lo, stack):
    nc = k.nc
    NS = 2 * TPG
    with ExitStack() as st:
        xs = [k.sbuf(f"x_in{s}", [P, D], stack=st) for s in range(NS)]
        junk = k.sbuf("squares", [P, D], stack=st)
        ssq = k.sbuf("ssq", [P, NS], stack=st)
        rms = k.sbuf("rms", [P, NS], stack=st)
        rstd = k.sbuf("rstd", [P, NS], stack=st)
        h = [k.sbuf(f"h_f32{s}", [P, RG], stack=st) for s in range(2)]
        tr = k.banks("x_t", 4, st)
        x_in = k.sems("n_x_in", NS)
        squared, rms_ready, rstd_ready, x_scaled = (k.sem("n_" + n) for n in ("squared", "rms", "rstd", "scaled"))
        tr_done, h_ready, hi_ready, lo_ready = (k.sem("n_" + n) for n in ("t", "h", "hi", "lo"))
        x_rows = x.rearrange("o (t p) d -> (o t) p d", p=P)

        start_counts(k)
        with nc.Block() as block:
            @block.sync
            def _(sp):
                with sp.Fori(0, NRG // 2) as i:
                    for s in range(NS):
                        sp.wait_ge(tr_done, START + i * 2 * DT)
                        sp.dma_start(xs[s][:, :], x_rows[bass.ds(i * NS + s, 1), :, :].rearrange("o p d -> p (o d)"))\
                          .then_inc(x_in[s], 16)

            @block.scalar
            def _(act):
                with act.Fori(0, NRG // 2) as i:
                    for r in range(2):
                        for s in range(r * TPG, (r + 1) * TPG):
                            act.wait_ge(x_in[s], START + (i + 1) * 16)
                            if s % TPG == 0:
                                act.wait_ge(rstd_ready, START + i * 2 + r)
                            act.wait_ge(squared, START + i * NS + s)
                            nc.scalar.activation(junk[:, :], xs[s][:, :], ACT.Square, accum_out=ssq[:, s:s + 1])\
                              .then_inc(squared, 1)
                        g = slice(r * TPG, (r + 1) * TPG)
                        act.wait_ge(squared, START + i * NS + (r + 1) * TPG)
                        nc.scalar.activation(rms[:, g], ssq[:, g], ACT.Sqrt, bias=eps[:, 0:1], scale=1.0 / D)\
                          .then_inc(rms_ready, 1)
                        for t in range(DT):
                            n = r * DT + t
                            act.wait_ge(tr_done, START + i * 2 * DT + n + 1)
                            act.wait_ge(lo_ready, START + i * 2 * DT + (n - 1 if n >= 2 else 0))
                            nc.scalar.activation(h[n % 2][:, :], tr[n % 4][:, :], ACT.Identity,
                                                 bias=k.mod[:, t:t + 1], scale=k.a_mix[:, t:t + 1]).then_inc(h_ready, 1)

            @block.tensor
            def _(pe):
                with pe.Fori(0, NRG // 2) as i:
                    for r in range(2):
                        pe.wait_ge(x_scaled, START + i * NS + (r + 1) * TPG)
                        for t in range(DT):
                            n = r * DT + t
                            pe.wait_ge(h_ready, START + i * 2 * DT + (n - 3 if n >= 4 else 0))
                            for q in range(TPG):
                                last = nc.tensor.transpose(tr[n % 4][:, q * P:(q + 1) * P],
                                                           xs[r * TPG + q][:, t * P:(t + 1) * P], k.ident[:, :])
                            last.then_inc(tr_done, 1)

            @block.vector
            def _(dve):
                with dve.Fori(0, NRG // 2) as i:
                    for r in range(2):
                        g = slice(r * TPG, (r + 1) * TPG)
                        dve.wait_ge(rms_ready, START + i * 2 + r + 1)
                        nc.vector.reciprocal(rstd[:, g], rms[:, g]).then_inc(rstd_ready, 1)
                        dve.wait_ge(rstd_ready, START + i * 2 + r + 1)
                        for s in range(r * TPG, (r + 1) * TPG):
                            nc.vector.tensor_scalar(xs[s][:, :], xs[s][:, :], rstd[:, s:s + 1], None, ALU.mult)\
                              .then_inc(x_scaled, 1)
                        rows = bass.ds((i * 2 + r) * RG, RG)
                        for t in range(DT):
                            n = r * DT + t
                            dve.wait_ge(h_ready, START + i * 2 * DT + n + 1)
                            nc.vector.tensor_copy(h_hi[:, t, rows], h[n % 2][:, :]).then_inc(hi_ready, 1)
                            dve.wait_ge(hi_ready, START + i * 2 * DT + n + 1)
                            nc.vector.tensor_sub(h_lo[:, t, rows], h[n % 2][:, :], f32(h_hi[:, t, rows]))\
                              .then_inc(lo_ready, 1)


def split_product(nc, out, w_hi, w_lo, a_hi, a_lo, first, last):
    nc.tensor.matmul(out, w_hi, a_hi, start=first, stop=False)
    nc.tensor.matmul(out, w_hi, a_lo, start=False, stop=False)
    return nc.tensor.matmul(out, w_lo, a_hi, start=False, stop=last)


def stage_projection(k, w_in, b_forget, h_hi, h_lo, proj, nf_dram):
    nc = k.nc
    with ExitStack() as st:
        raw = [k.sbuf(f"wp_raw{s}", [P, DT, P], stack=st) for s in range(2)]
        hi = [k.sbuf(f"wp_hi{s}", [P, DT, P], F32R, stack=st) for s in range(2)]
        lo = [k.sbuf(f"wp_lo{s}", [P, DT, P], F32R, stack=st) for s in range(2)]
        f_raw = k.sbuf("wf_raw", [P, DT, HB], stack=st)
        f_hi = k.sbuf("wf_hi", [P, DT, HB], F32R, stack=st)
        f_lo = k.sbuf("wf_lo", [P, DT, HB], F32R, stack=st)
        b_f = k.sbuf("b_f", [HB, 1], stack=st)
        out = [k.sbuf(f"proj_out{s}", [P, S], stack=st) for s in range(2)]
        acc = [k.banks(f"proj_acc{s}_", NRG, st) for s in range(2)]
        logit, soft = out[0][0:HB, :], out[1][0:HB, :]
        one = k.sbuf("one_f", [HB, S], stack=st)
        f_in, f_split, f_acc, f_chain = (k.sem("p_" + n) for n in ("f_in", "f_split", "f_acc", "f_chain"))
        f_dve, f_saved = k.sem("p_f_dve"), k.sem("p_f_saved")
        w_ld, w_hi, w_lo = k.sems("p_w_in", 2), k.sems("p_w_hi", 2), k.sems("p_w_lo", 2)
        done, copied, saved = k.sems("p_done", 2), k.sems("p_copied", 2), k.sems("p_saved", 2)
        w_view = w_in.rearrange("o (t p) n -> p (o t) n", p=P)

        start_counts(k)
        with nc.Block() as block:
            @block.sync
            def _(sp):
                with nc.allow_non_contiguous_dma(reason="eight columns of forget gates"):
                    sp.dma_start(f_raw[:, :, :], w_view[:, :, FG0:IN_COLS]).then_inc(f_in, 16)
                    sp.dma_start(b_f[:, :], b_forget.rearrange("o h -> h o")).then_inc(f_in, 16)
                with sp.Fori(0, PT // 2) as i:
                    for s in range(2):
                        sp.wait_ge(w_lo[s], START + i)
                        sp.dma_start(raw[s][:, :, :], w_view[:, :, bass.ds((i * 2 + s) * P, P)]).then_inc(w_ld[s], 16)

            @block.tensor
            def _(pe):
                pe.wait_ge(f_split, START + 2)
                for r in range(NRG):
                    for t in range(DT):
                        a = slice(r * RG, (r + 1) * RG)
                        last = split_product(nc, acc[1][r][0:HB, :], f_hi[:, t, :], f_lo[:, t, :],
                                             h_hi[:, t, a], h_lo[:, t, a], t == 0, t == DT - 1)
                    last.then_inc(f_acc, 1)
                with pe.Fori(0, PT // 2) as i:
                    for s in range(2):
                        pe.wait_ge(w_lo[s], START + i + 1)
                        if s == 1:
                            pe.wait_ge(f_chain, START + NRG)
                        pe.wait_ge(copied[s], START + i * NRG)
                        for r in range(NRG):
                            a = slice(r * RG, (r + 1) * RG)
                            for t in range(DT):
                                last = split_product(nc, acc[s][r][:, :], hi[s][:, t, :], lo[s][:, t, :],
                                                     h_hi[:, t, a], h_lo[:, t, a], t == 0, t == DT - 1)
                            last.then_inc(done[s], 1)

            @block.scalar
            def _(act):
                act.wait_ge(f_in, START + 32)
                for r in range(NRG):
                    act.wait_ge(f_acc, START + r + 1)
                    nc.scalar.activation(logit[:, r * RG:(r + 1) * RG], acc[1][r][0:HB, :], ACT.Identity,
                                         bias=b_f[:, 0:1]).then_inc(f_chain, 1)
                act.wait_ge(f_chain, START + NRG)
                nc.scalar.activation(soft, logit, ACT.Abs).then_inc(f_chain, 1)
                act.wait_ge(f_chain, START + NRG + 1)
                nc.scalar.activation(soft, soft, ACT.Exp, scale=-1.0).then_inc(f_chain, 1)
                act.wait_ge(f_chain, START + NRG + 2)
                nc.scalar.activation(soft, soft, ACT.Ln, bias=1.0).then_inc(f_chain, 1)
                act.wait_ge(f_dve, START + 4)
                act.dma_start(nf_dram, logit).then_inc(f_saved, 16)
                act.wait_ge(f_saved, START + 16)
                with act.Fori(0, PT // 2) as i:
                    for s in range(2):
                        act.wait_ge(saved[s], START + i * 16)
                        for r in range(NRG):
                            act.wait_ge(done[s], START + i * NRG + r + 1)
                            nc.scalar.activation(out[s][:, r * RG:(r + 1) * RG], acc[s][r][:, :], ACT.Copy)\
                              .then_inc(copied[s], 1)
                        act.wait_ge(copied[s], START + (i + 1) * NRG)
                        act.dma_start(proj[bass.ds((i * 2 + s) * P, P), :], out[s][:, :]).then_inc(saved[s], 16)
                for s in range(2):
                    act.wait_ge(saved[s], START + PT // 2 * 16)

            @block.vector
            def _(dve):
                dve.wait_ge(f_in, START + 32)
                nc.vector.tensor_copy(f_hi[:, :, :], f_raw[:, :, :]).then_inc(f_split, 1)
                nc.vector.memset(one[:, :], 1.0).then_inc(f_dve, 1)
                dve.wait_ge(f_split, START + 1)
                nc.vector.tensor_sub(f_lo[:, :, :], f_raw[:, :, :], f32(f_hi[:, :, :])).then_inc(f_split, 1)

                def split(i, s):
                    dve.wait_ge(w_ld[s], START + (i + 1) * 16)
                    dve.wait_ge(done[s], START + i * NRG)
                    nc.vector.tensor_copy(hi[s][:, :, :], raw[s][:, :, :]).then_inc(w_hi[s], 1)
                    dve.wait_ge(w_hi[s], START + i + 1)
                    nc.vector.tensor_sub(lo[s][:, :, :], raw[s][:, :, :], f32(hi[s][:, :, :])).then_inc(w_lo[s], 1)

                split(0, 0)
                split(0, 1)
                dve.wait_ge(f_chain, START + NRG + 3)
                nc.vector.scalar_tensor_tensor(soft, logit, 0.0, soft, ALU.min, ALU.subtract).then_inc(f_dve, 1)
                dve.wait_ge(f_dve, START + 2)
                nc.vector.tensor_tensor_scan(logit, one[:, :], soft, 0.0, ALU.mult, ALU.add).then_inc(f_dve, 1)
                dve.wait_ge(f_dve, START + 3)
                nc.vector.tensor_scalar(logit, logit, -INV_SCALE, None, ALU.mult).then_inc(f_dve, 1)
                with dve.Fori(1, PT // 2) as i:
                    for s in range(2):
                        split(i, s)


def stage_attention_b(k, proj, nf_dram, mask_in, y):
    nc = k.nc
    NP = HB // 2
    units = [(hh, g) for hh in range(2) for g in (3, 2, 1, 0)]
    NU, UH = len(units), len(units) // 2
    n_tiles = [TPG * (g + 1) for _, g in units]
    K0 = [sum(n_tiles[:u]) for u in range(NU + 1)]
    NK, NT = K0[-1], NU * TPG
    SB, TB = 3, 3
    PIECES = 6
    with ExitStack() as st:
        qk_in = k.sbuf("bqk_in", [P, S], stack=st)
        v_in = k.sbuf("bv_in", [HD, S], stack=st)
        q_st = [k.sbuf(f"bq{s}", [P, S], F32R, stack=st) for s in range(2)]
        k_hi = [k.sbuf(f"bk_hi{s}", [P, S], F32R, stack=st) for s in range(2)]
        k_lo = [k.sbuf(f"bk_lo{s}", [P, S], F32R, stack=st) for s in range(2)]
        v_st = [k.sbuf(f"bv{s}", [P, RT, P], F32R, stack=st) for s in range(2)]
        nf = [k.sbuf(f"b_nf{s}", [P, S], stack=st) for s in range(2)]
        pf = [k.sbuf(f"b_pf{s}", [P, RT], stack=st) for s in range(2)]
        bias = [k.sbuf(f"b_bias{s}", [P, S], stack=st) for s in range(2)]
        mask = k.sbuf("b_mask", [P, P], stack=st)
        prob = [[k.sbuf(f"b_p{s}_{t}", [P, S], stack=st) for t in range(TPG)] for s in range(2)]
        mx = k.sbuf("b_mx", [P, TPG], stack=st)
        m8 = k.sbuf("b_m8", [P, 2], stack=st)
        neg_m = k.sbuf("b_neg_m", [P, 2], stack=st)
        den = k.sbuf("b_den", [P, 2, TPG], stack=st)
        rden = k.sbuf("b_rden", [P, TPG], stack=st)
        pt_hi = [k.sbuf(f"b_pt_hi{s}", [P, RG], F32R, stack=st) for s in range(TB)]
        pt_lo = [k.sbuf(f"b_pt_lo{s}", [P, RG], F32R, stack=st) for s in range(TB)]
        ot = k.sbuf("b_ot", [P, RG], stack=st)
        y_half = k.sbuf("b_y_half", [P, TPG, HD], stack=st)
        y_sum = k.sbuf("b_y_sum", [P, TPG, HD], stack=st)
        y_out = k.sbuf("b_y_out", [P, RT, 2 * HD], stack=st)
        sc = k.banks("b_sc", SB, st)
        tp = k.banks("b_tp", TB, st)
        oacc = k.banks("b_oacc", 1, st)[0]
        yt = k.banks("b_yt", 1, st)[0]
        vt = yt
        names = ("mask_in", "sc_done", "sc_used", "bias_row", "bias_ready", "mx", "neg_m", "exp", "tp_done",
                 "hi_ready", "lo_ready", "o_done", "ot_ready", "yt_done", "half", "ysum", "y_ready", "rden")
        (mask_ld, sc_done, sc_used, bias_row, bias_ready, mx_ready, neg_ready, exp_done, tp_done, hi_ready, lo_ready,
         o_done, ot_ready, yt_done, half_ready, sum_ready, y_ready, rden_ready) = (k.sem("b_" + n) for n in names)
        y_saved = k.sem("b_y_saved")
        passed = k.sems("b_passed", 3)
        nf_ld = k.sems("b_nf_in", 2)
        names = ("qk_in", "v_in", "qk_hi", "qk_ready", "pf", "vt_done", "v_hi", "v_lo")
        qk_ld, v_ld, qk_hi, qk_ready, pf_ready, vt_done, v_hi, v_lo = (k.sem("b_" + n) for n in names)

        def tiles_to(u):
            return K0[u + 1] if u >= 0 else K0[u + 1 + NU] - NK

        def turn(i, prepare, step, end):
            for u in range(NU):
                for m in range(n_tiles[u]):
                    step(i, u, m)
                    if u % UH == 1 and 1 <= m < 1 + PIECES:
                        hh = 1 - u // UH
                        prepare(i * 2 + (1 if hh else 2), hh, m - 1, i * NK + (0 if hh else K0[UH]),
                                i * NT + (0 if hh else UH * TPG), i + (1 if hh else 2), i * NU + (0 if hh else UH))
            end(i)

        def share(u, m):
            if not u:
                return range(0)
            lag = 1 if n_tiles[u] == TPG else 2
            n, of = n_tiles[u - 1], n_tiles[u] - lag
            return range(max(0, m - lag) * n // of, max(0, m + 1 - lag) * n // of)

        start_counts(k)
        with nc.Block() as block:
            @block.sync
            def _(sp):
                def load(h, m, hh, biases):
                    for n, row in enumerate((KB0, QB0)):
                        sp.wait_ge(qk_ready, START + m * 2 + n)
                        for half in range(2):
                            sp.dma_start(qk_in[half * HD:(half + 1) * HD, :], proj[bass.ds(row + h * HD, HD), :])\
                              .then_inc(qk_ld, 16)
                    sp.wait_ge(vt_done, START + m * 2)
                    sp.dma_start(v_in[:, :], proj[bass.ds(VB0 + h * HD, HD), :]).then_inc(v_ld, 16)
                    sp.wait_ge(bias_ready, START + biases)
                    sp.dma_start(nf[hh][:, :], nf_dram[bass.ds(h, 1), :].to_broadcast([P, S])).then_inc(nf_ld[hh], 16)

                sp.dma_start(mask[:, :], mask_in).then_inc(mask_ld, 16)
                load(0, 0, 0, 0)
                with sp.Fori(0, NP) as i:
                    load(i * 2 + 1, i * 2 + 1, 1, i * NT)
                    load((i * 2 + 2) % HB, i * 2 + 2, 0, i * NT + UH * TPG)

            @block.gpsimd
            def _(pool):
                pool.wait_ge(mask_ld, START + 16)
                with pool.Fori(0, NP) as i:
                    for u, (hh, g) in enumerate(units):
                        if u % UH == 0:
                            pool.wait_ge(nf_ld[hh], START + (i + 1) * 16)
                            pool.wait_ge(pf_ready, START + i * 2 + hh + 1)
                        for t in range(TPG):
                            n, q = u * TPG + t, g * TPG + t
                            ub, tb = (n - 2) // TPG, (n - 2) % TPG
                            c = tiles_to(ub - 1) + (tb + 1) * (units[ub][1] + 1)
                            wait_apart(pool, passed[0], sc_used, START + i * NK + c)
                            b = bias[n % 2]
                            nc.gpsimd.tensor_scalar(b[:, 0:(q + 1) * P], nf[hh][:, 0:(q + 1) * P], 1.0, pf[hh][:, q:q + 1],
                                                    ALU.mult, ALU.add).then_inc(bias_row, 1)
                            pool.wait_ge(bias_row, START + i * NT + n + 1)
                            nc.gpsimd.tensor_tensor(b[:, q * P:(q + 1) * P], b[:, q * P:(q + 1) * P], mask[:, :], ALU.add)\
                              .then_inc(bias_ready, 1)

            @block.tensor
            def _(pe):
                def prepare(m, hh, piece, tiles, biases, loads, outputs):
                    b = piece - 2 if piece in (2, 3) else -1
                    """v of the m-th head as rows, eight key tiles."""
                    if b < 0:
                        return
                    pe.wait_ge(v_ld, START + (m + 1) * 16)
                    pe.wait_ge(sum_ready, START + outputs)
                    wait_apart(pe, passed[2], v_lo, START + m * 2 + b)
                    for j in range(8):
                        last = nc.tensor.transpose(vt[:, j * HD:(j + 1) * HD], v_in[:, (b * 8 + j) * P:(b * 8 + j + 1) * P],
                                                   k.ident[0:HD, 0:HD])
                    last.then_inc(vt_done, 1)

                def scores(i, u, m):
                    hh, g = units[u]
                    t, c = m // (g + 1), m % (g + 1)
                    q, n = g * TPG + t, K0[u] + m
                    if u % UH == 0 and m == 0:
                        pe.wait_ge(qk_ready, START + i * 4 + hh * 2 + 2)
                    w = RG if c < g else (t + 1) * P
                    pe.wait_ge(sc_used, START + i * NK + (n - SB + 1 if n >= SB else 0))
                    a, b = slice(q * P, (q + 1) * P), slice(c * RG, c * RG + w)
                    nc.tensor.matmul(sc[n % SB][:, 0:w], q_st[hh][:, a], k_hi[hh][:, b], start=True, stop=False)
                    nc.tensor.matmul(sc[n % SB][:, 0:w], q_st[hh][:, a], k_lo[hh][:, b], start=False, stop=True)\
                      .then_inc(sc_done, 1)

                def transposes(i, u, j):
                    g, n = units[u][1], K0[u] + j
                    if j == 0:
                        pe.wait_ge(exp_done, START + i * NT + (u + 1) * TPG)
                    pe.wait_ge(lo_ready, START + i * NK + n - TB + 1)
                    for t in range(max(0, j - g * TPG), TPG):
                        last = nc.tensor.transpose(tp[n % TB][:, t * P:(t + 1) * P],
                                                   prob[u % 2][t][:, j * P:(j + 1) * P], k.ident[:, :])
                    last.then_inc(tp_done, 1)

                def products(i, u, j):
                    hh, g = units[u]
                    n = K0[u] + j
                    c0 = max(0, j - g * TPG) * P
                    if j == 0:
                        pe.wait_ge(ot_ready, START + i * NU + u)
                        if u % UH == 0:
                            pe.wait_ge(v_lo, START + i * 4 + hh * 2 + 2)
                    pe.wait_ge(lo_ready, START + i * NK + n + 1)
                    nc.tensor.matmul(oacc[:, c0:RG], v_st[hh][:, j, :], pt_hi[n % TB][:, c0:RG], start=(j == 0), stop=False)
                    nc.tensor.matmul(oacc[:, c0:RG], v_st[hh][:, j, :], pt_lo[n % TB][:, c0:RG],
                                     start=False, stop=(j == n_tiles[u] - 1)).then_inc(o_done, 1)

                def finish(i, u):
                    pe.wait_ge(ot_ready, START + i * NU + u + 1)
                    pe.wait_ge(sum_ready, START + i * NU + u)
                    pe.wait_ge(v_lo, START + i * 4 + (4 if u < UH else 6))
                    for t in range(TPG):
                        last = nc.tensor.transpose(yt[:, t * P:(t + 1) * P], ot[:, t * P:(t + 1) * P], k.ident[:, :])
                    last.then_inc(yt_done, 1)

                waiting = []

                def part(i, u, js):
                    for j in js:
                        transposes(i, u, j)
                        waiting.append((u, j))
                        if len(waiting) > 2:
                            products(i, *waiting.pop(0))
                    if not js and waiting:
                        products(i, *waiting.pop(0))

                def step(i, u, m):
                    if u == 0 and m == 0:
                        scores(i, u, m)
                    if m + 1 < n_tiles[u]:
                        scores(i, u, m + 1)
                    elif u + 1 < NU:
                        scores(i, u + 1, 0)
                    if m == 3 and u >= 2:
                        finish(i, u - 2)
                    part(i, u - 1, share(u, m))

                def end(i):
                    part(i, NU - 1, range(n_tiles[NU - 1]))
                    while waiting:
                        part(i, NU - 1, ())
                    finish(i, NU - 2)
                    finish(i, NU - 1)

                for piece in range(PIECES):
                    prepare(0, 0, piece, 0, 0, 1, 0)
                with pe.Fori(0, NP) as i:
                    turn(i, prepare, step, end)

            @block.scalar
            def _(act):
                def prepare(m, hh, piece, tiles, biases, loads, outputs):
                    b = piece - 2 if piece in (2, 3) else -1
                    if b < 0:
                        return
                    act.wait_ge(vt_done, START + m * 2 + b + 1)
                    act.wait_ge(o_done, START + tiles)
                    nc.scalar.activation(v_st[hh][:, b * 8:(b + 1) * 8, 0:HD],
                                         vt[:, :].rearrange("p (j d) -> p j d", d=HD), ACT.Copy).then_inc(v_hi, 1)

                def exps(i, n):
                    u, t = n // TPG, n % TPG
                    w = (units[u][1] * TPG + t + 1) * P
                    if t == 0:
                        act.wait_ge(rden_ready, START + i * NU + u - 1)
                    act.wait_ge(neg_ready, START + i * NT + n + 1)
                    nc.scalar.activation(prob[u % 2][t][:, 0:w], prob[u % 2][t][:, 0:w], ACT.Exp,
                                         bias=neg_m[:, n % 2:n % 2 + 1], scale=SCALE,
                                         accum_out=den[:, u % 2, t:t + 1]).then_inc(exp_done, 1)

                def part(i, u, js):
                    g = units[u][1]
                    for j in js:
                        n = K0[u] + j
                        c0 = max(0, j - g * TPG) * P
                        act.wait_ge(tp_done, START + i * NK + n + 1)
                        act.wait_ge(o_done, START + i * NK + n - 1)
                        nc.scalar.activation(pt_hi[n % TB][:, c0:RG], tp[n % TB][:, c0:RG], ACT.Copy).then_inc(hi_ready, 1)

                def copy_out(i, u):
                    act.wait_ge(o_done, START + i * NK + K0[u + 1])
                    act.wait_ge(yt_done, START + i * NU + u)
                    nc.scalar.activation(ot[:, :], oacc[:, :], ACT.Copy).then_inc(ot_ready, 1)

                def finish(i, u):
                    act.wait_ge(yt_done, START + i * NU + u + 1)
                    act.wait_ge(sum_ready, START + i * NU + u)
                    nc.scalar.activation(y_half[:, :, :], yt[:, :].rearrange("p (t c) -> p t c", c=P)[:, :, HD:P],
                                         ACT.Copy).then_inc(half_ready, 1)

                def step(i, u, m):
                    t, c = m // (units[u][1] + 1), m % (units[u][1] + 1)
                    if c == 0 and (u or t):
                        exps(i, u * TPG + t - 1)
                    if m == 2 and u >= 2:
                        copy_out(i, u - 2)
                    part(i, u - 1, share(u, m))
                    if m == 3 and u >= 2:
                        finish(i, u - 2)

                def end(i):
                    exps(i, NT - 1)
                    part(i, NU - 1, range(2))
                    copy_out(i, NU - 2)
                    part(i, NU - 1, range(2, n_tiles[NU - 1]))
                    finish(i, NU - 2)
                    copy_out(i, NU - 1)
                    finish(i, NU - 1)
                    act.wait_ge(y_ready, START + (i + 1) * NU)
                    act.dma_start(y[:, bass.ds(WA + i * P, P)].rearrange("(t p) c -> p t c", p=P), y_out[:, :, :])\
                       .then_inc(y_saved, 16)

                for piece in range(PIECES):
                    prepare(0, 0, piece, 0, 0, 1, 0)
                with act.Fori(0, NP) as i:
                    turn(i, prepare, step, end)
                act.wait_ge(y_saved, START + NP * 16)

            @block.vector
            def _(dve):
                def prepare(m, hh, piece, tiles, biases, loads, outputs):
                    b = piece - 2 if piece in (2, 3) else -1
                    if piece == 0:
                        dve.wait_ge(qk_ld, START + m * 64 + 32)
                        dve.wait_ge(sc_done, START + tiles)
                        nc.vector.tensor_copy(k_hi[hh][:, :], qk_in[:, :]).then_inc(qk_hi, 1)
                    if piece == 1:
                        dve.wait_ge(qk_hi, START + m * 2 + 1)
                        nc.vector.tensor_sub(k_lo[hh][:, :], qk_in[:, :], f32(k_hi[hh][:, :])).then_inc(qk_ready, 1)
                    if piece == 4:
                        dve.wait_ge(qk_ld, START + m * 64 + 64)
                        nc.vector.tensor_copy(q_st[hh][:, :], qk_in[:, :]).then_inc(qk_hi, 1)
                    if piece == 5:
                        dve.wait_ge(qk_hi, START + m * 2 + 2)
                        nc.vector.tensor_sub(q_st[hh][HD:P, :], qk_in[HD:P, :], f32(q_st[hh][HD:P, :])).then_inc(qk_ready, 1)
                        dve.wait_ge(nf_ld[hh], START + loads * 16)
                        dve.wait_ge(bias_ready, START + biases)
                        nc.vector.tensor_scalar(pf[hh][:, :], nf[hh][:, :].rearrange("p (t c) -> p t c", c=P)[:, :, 0],
                                                -1.0, None, ALU.mult).then_inc(pf_ready, 1)
                    if b >= 0:
                        dve.wait_ge(v_hi, START + m * 2 + b + 1)
                        v = v_st[hh][:, b * 8:(b + 1) * 8, :]
                        nc.vector.tensor_sub(v[:, :, HD:P], vt[:, :].rearrange("p (j d) -> p j d", d=HD),
                                             f32(v[:, :, 0:HD])).then_inc(v_lo, 1)

                def logits(i, u, m):
                    g = units[u][1]
                    t, c = m // (g + 1), m % (g + 1)
                    n, x = u * TPG + t, K0[u] + m
                    if c == 0:
                        dve.wait_ge(bias_ready, START + i * NT + n + 1)
                    if m == 0:
                        dve.wait_ge(tp_done, START + i * NK + tiles_to(u - 2))
                    w = RG if c < g else (t + 1) * P
                    cols = slice(c * RG, c * RG + w)
                    wait_apart(dve, passed[1], sc_done, START + i * NK + x + 1)
                    nc.vector.tensor_tensor_reduce(out=prob[u % 2][t][:, cols], in0=sc[x % SB][:, 0:w],
                                                   in1=bias[n % 2][:, cols], scale=1.0, scalar=INV_SCALE * NEG,
                                                   op0=ALU.add, op1=ALU.max, accum_out=mx[:, c:c + 1]).then_inc(sc_used, 1)
                    if c == g:
                        dve.wait_ge(sc_used, START + i * NK + x + 1)
                        nc.vector.reduce_max(m8[:, n % 2:n % 2 + 1], mx[:, 0:g + 1], AXX).then_inc(mx_ready, 1)
                        dve.wait_ge(mx_ready, START + i * NT + n + 1)
                        dve.wait_ge(exp_done, START + i * NT + n - 1)
                        nc.vector.tensor_scalar(neg_m[:, n % 2:n % 2 + 1], m8[:, n % 2:n % 2 + 1], -SCALE, None,
                                                ALU.mult).then_inc(neg_ready, 1)

                def part(i, u, js):
                    g = units[u][1]
                    for j in js:
                        n = K0[u] + j
                        c0 = max(0, j - g * TPG) * P
                        dve.wait_ge(hi_ready, START + i * NK + n + 1)
                        nc.vector.tensor_sub(pt_lo[n % TB][:, c0:RG], tp[n % TB][:, c0:RG], f32(pt_hi[n % TB][:, c0:RG]))\
                          .then_inc(lo_ready, 1)

                def inverse(i, u):
                    dve.wait_ge(exp_done, START + i * NT + (u + 1) * TPG)
                    dve.wait_ge(y_ready, START + i * NU + u)
                    nc.vector.reciprocal(rden[:, :], den[:, u % 2, :]).then_inc(rden_ready, 1)

                def finish(i, u):
                    hh, g = units[u]
                    dve.wait_ge(half_ready, START + i * NU + u + 1)
                    nc.vector.tensor_add(y_sum[:, :, :], yt[:, :].rearrange("p (t c) -> p t c", c=P)[:, :, 0:HD],
                                         y_half[:, :, :]).then_inc(sum_ready, 1)
                    dve.wait_ge(sum_ready, START + i * NU + u + 1)
                    dve.wait_ge(rden_ready, START + i * NU + u + 1)
                    if u == 0:
                        dve.wait_ge(y_saved, START + i * 16)
                    nc.vector.tensor_tensor(y_out[:, g * TPG:(g + 1) * TPG, hh * HD:(hh + 1) * HD], y_sum[:, :, :],
                                            rden[:, :].unsqueeze(2).to_broadcast([P, TPG, HD]), ALU.mult)\
                      .then_inc(y_ready, 1)

                waiting = []

                def step(i, u, m):
                    if m == 0 and u >= 2:
                        inverse(i, u - 2)
                    logits(i, u, m)
                    js = share(u, m)
                    while waiting:
                        part(i, *waiting.pop(0))
                    part(i, u - 1, js[:-1])
                    waiting.append((u - 1, js[-1:]))
                    if m == 3 and u >= 2:
                        finish(i, u - 2)

                def end(i):
                    inverse(i, NU - 2)
                    while waiting:
                        part(i, *waiting.pop(0))
                    part(i, NU - 1, range(n_tiles[NU - 1]))
                    finish(i, NU - 2)
                    inverse(i, NU - 1)
                    finish(i, NU - 1)

                for piece in range(PIECES):
                    prepare(0, 0, piece, 0, 0, 1, 0)
                with dve.Fori(0, NP) as i:
                    turn(i, prepare, step, end)


def stage_attention_a(k, proj, band_in, sinks, y):
    nc = k.nc
    with ExitStack() as st:
        q_in = k.sbuf("aq_in", [P, GA, S], stack=st)
        q_st = k.sbuf("aq", [P, GA, S], F32R, stack=st)
        k_in = k.sbuf("ak_in", [P, S], stack=st)
        k_hi = k.sbuf("ak_hi", [P, S], F32R, stack=st)
        k_lo = k.sbuf("ak_lo", [P, S], F32R, stack=st)
        v_in = k.sbuf("av_in", [HD, S], stack=st)
        v_st = k.sbuf("av", [P, RT, P], F32R, stack=st)
        band = k.sbuf("a_band", [P, GA, BAND], stack=st)
        sink = k.sbuf("a_sink", [P, GA], stack=st)
        prob = [k.sbuf(f"a_p{s}", [P, GA, 2 * P], stack=st) for s in range(2)]
        mx = k.sbuf("a_mx", [P, 2, GA], stack=st)
        m = k.sbuf("a_m", [P, 2, GA], stack=st)
        neg_m = k.sbuf("a_neg_m", [P, 2, GA], stack=st)
        sink_m = k.sbuf("a_sink_m", [P, 2, GA], stack=st)
        sink_e = k.sbuf("a_sink_e", [P, 2, GA], stack=st)
        den = k.sbuf("a_den", [P, 2, GA], stack=st)
        den_all = k.sbuf("a_den_all", [P, 2, GA], stack=st)
        rden = k.sbuf("a_rden", [P, 2, GA], stack=st)
        pt_hi = [k.sbuf(f"a_pt_hi{s}", [P, RG], F32R, stack=st) for s in range(2)]
        pt_lo = [k.sbuf(f"a_pt_lo{s}", [P, RG], F32R, stack=st) for s in range(2)]
        ot = k.sbuf("a_ot", [P, RG], stack=st)
        y_half = k.sbuf("a_y_half", [P, GA, HD], stack=st)
        y_sum = k.sbuf("a_y_sum", [P, GA, HD], stack=st)
        y_out = [k.sbuf(f"a_y_out{s}", [P, GA, HD], stack=st) for s in range(2)]
        sc = [st.enter_context(nc.psum_tensor(f"a_sc{s}", [P, GA, 2 * P], F32)) for s in range(1)]
        tp = k.banks("a_tp", 2, st)
        oacc = k.banks("a_oacc", 1, st)[0]
        yt = k.banks("a_yt", 1, st)[0]
        vt = k.banks("a_vt", 2, st)
        qk_ld, v_ld, band_ld, qk_hi, qk_ready = (k.sem("a_" + n) for n in ("qk_in", "v_in", "band_in", "qk_hi", "qk_ready"))
        vt_done, v_hi, v_lo, zeroed = (k.sem("a_" + n) for n in ("vt_done", "v_hi", "v_lo", "zeroed"))
        names = ("sc_done", "logits", "mx", "m", "neg_m", "exp", "sink_e", "den", "rden", "tp_done",
                 "hi_ready", "lo_ready", "o_done", "ot_ready", "yt_done", "half", "ysum", "y_ready")
        (sc_done, logits, mx_ready, m_ready, neg_ready, exp_done, sink_done, den_ready, rden_ready, tp_done,
         hi_ready, lo_ready, o_done, ot_ready, yt_done, half_ready, sum_ready, y_ready) = (k.sem("a_" + n) for n in names)
        y_saved = k.sems("a_y_saved", 2)
        passed = k.sem("a_passed")
        tiles = [(j, a) for j in range(RT) for a in ((1,) if j == 0 else (0, 1))]
        T0 = [sum(1 for x, _ in tiles if x < j) for j in range(RT + 1)]
        NK = T0[-1]

        start_counts(k)
        with nc.Block() as block:
            @block.sync
            def _(sp):
                with sp.Fori(0, KVA) as i:
                    sp.wait_ge(qk_ready, START + i * 2)
                    for half in range(2):
                        rows = slice(half * HD, (half + 1) * HD)
                        sp.dma_start(k_in[rows, :], proj[bass.ds(KA0 + i * HD, HD), :]).then_inc(qk_ld, 16)
                        sp.dma_start(q_in[rows, :, :], proj[bass.ds(QA0 + i * GA * HD, GA * HD), :]
                                     .rearrange("(g d) s -> d g s", d=HD)).then_inc(qk_ld, 16)
                    sp.wait_ge(vt_done, START + i * 2)
                    sp.dma_start(v_in[:, :], proj[bass.ds(VA0 + i * HD, HD), :]).then_inc(v_ld, 16)
                    sp.wait_ge(logits, START + i * RT)
                    sp.wait_ge(sink_done, START + i * RT)
                    sp.dma_start(band[:, :, :], band_in[bass.ds(i, 1), :, :, :].rearrange("o p g c -> p (o g) c"))\
                      .then_inc(band_ld, 16)
                    sp.dma_start(sink[:, :], sinks[:, bass.ds(i * GA, GA)].to_broadcast([P, GA])).then_inc(band_ld, 16)

            @block.tensor
            def _(pe):
                with pe.Fori(0, KVA) as i:
                    for b in range(2):
                        pe.wait_ge(v_ld, START + (i + 1) * 16)
                        wait_apart(pe, passed, v_lo, START + i * 2)
                        for j in range(8):
                            last = nc.tensor.transpose(vt[b][:, j * HD:(j + 1) * HD],
                                                       v_in[:, (b * 8 + j) * P:(b * 8 + j + 1) * P], k.ident[0:HD, 0:HD])
                        last.then_inc(vt_done, 1)
                    pe.wait_ge(qk_ready, START + i * 2 + 2)

                    def scores(j):
                        pe.wait_ge(logits, START + i * RT + j)
                        c0 = HD if j else P
                        keys = slice((j - 1) * P + c0, (j + 1) * P)
                        for g in range(GA):
                            q = q_st[:, g, j * P:(j + 1) * P]
                            nc.tensor.matmul(sc[0][:, g, c0:], q, k_hi[:, keys], start=True, stop=False)
                            last = nc.tensor.matmul(sc[0][:, g, c0:], q, k_lo[:, keys], start=False, stop=True)
                        last.then_inc(sc_done, 1)

                    def products(j):
                        pe.wait_ge(exp_done, START + i * RT + j + 1)
                        pe.wait_ge(zeroed, START + 2)
                        mine = [(n, a) for n, (x, a) in enumerate(tiles) if x == j]
                        for n, a in mine:
                            pe.wait_ge(lo_ready, START + i * NK + (n - 1 if n >= 2 else 0))
                            for g in range(GA):
                                last = nc.tensor.transpose(tp[n % 2][:, g * P:(g + 1) * P],
                                                           prob[j % 2][:, g, a * P:(a + 1) * P], k.ident[:, :])
                            last.then_inc(tp_done, 1)
                        for n, a in mine:
                            if n == mine[0][0]:
                                pe.wait_ge(ot_ready, START + i * RT + j)
                            pe.wait_ge(lo_ready, START + i * NK + n + 1)
                            v = v_st[:, j - 1 + a, :]
                            nc.tensor.matmul(oacc[:, :], v, pt_hi[n % 2][:, :], start=(n == mine[0][0]), stop=False)
                            nc.tensor.matmul(oacc[:, :], v, pt_lo[n % 2][:, :], start=False, stop=(n == mine[-1][0]))\
                              .then_inc(o_done, 1)
                        pe.wait_ge(ot_ready, START + i * RT + j + 1)
                        pe.wait_ge(sum_ready, START + i * RT + j)
                        for g in range(GA):
                            last = nc.tensor.transpose(yt[:, g * P:(g + 1) * P], ot[:, g * P:(g + 1) * P], k.ident[:, :])
                        last.then_inc(yt_done, 1)

                    pe.wait_ge(v_lo, START + i * 2 + 2)
                    scores(0)
                    for j in range(RT):
                        if j + 1 < RT:
                            scores(j + 1)
                        products(j)

            @block.scalar
            def _(act):
                with act.Fori(0, KVA) as i:
                    for b in range(2):
                        act.wait_ge(vt_done, START + i * 2 + b + 1)
                        act.wait_ge(o_done, START + i * NK)
                        nc.scalar.activation(v_st[:, b * 8:(b + 1) * 8, 0:HD],
                                             vt[b][:, :].rearrange("p (j d) -> p j d", d=HD), ACT.Copy).then_inc(v_hi, 1)

                    def exps(j):
                        act.wait_ge(neg_ready, START + i * RT + j + 1)
                        c0 = HD if j else P
                        for g in range(GA):
                            p = prob[j % 2][:, g, c0:]
                            last = nc.scalar.activation(p, p, ACT.Exp, bias=neg_m[:, j % 2, g:g + 1],
                                                        accum_out=den[:, j % 2, g:g + 1])
                        last.then_inc(exp_done, 1)
                        nc.scalar.activation(sink_e[:, j % 2, :], sink_m[:, j % 2, :], ACT.Exp).then_inc(sink_done, 1)

                    def copies(j):
                        mine = [n for n, (x, _) in enumerate(tiles) if x == j]
                        for n in mine:
                            act.wait_ge(tp_done, START + i * NK + n + 1)
                            act.wait_ge(o_done, START + i * NK + (n - 1 if n >= 2 else 0))
                            nc.scalar.activation(pt_hi[n % 2][:, :], tp[n % 2][:, :], ACT.Copy).then_inc(hi_ready, 1)
                        act.wait_ge(o_done, START + i * NK + mine[-1] + 1)
                        act.wait_ge(yt_done, START + i * RT + j)
                        nc.scalar.activation(ot[:, :], oacc[:, :], ACT.Copy).then_inc(ot_ready, 1)
                        act.wait_ge(yt_done, START + i * RT + j + 1)
                        act.wait_ge(sum_ready, START + i * RT + j)
                        nc.scalar.activation(y_half[:, :, :], yt[:, :].rearrange("p (t c) -> p t c", c=P)[:, :, HD:P],
                                             ACT.Copy).then_inc(half_ready, 1)
                        act.wait_ge(y_ready, START + i * RT + j + 1)
                        act.dma_start(y[j * P:(j + 1) * P, bass.ds(i * GA * HD, GA * HD)],
                                      y_out[j % 2][:, :, :].rearrange("p g d -> p (g d)")).then_inc(y_saved[j % 2], 16)

                    exps(0)
                    for j in range(RT):
                        if j + 1 < RT:
                            exps(j + 1)
                        copies(j)
                for s in range(2):
                    act.wait_ge(y_saved[s], START + KVA * RT // 2 * 16)

            @block.vector
            def _(dve):
                for s in range(2):
                    nc.vector.memset(prob[s][:, :, 0:HD], 0.0).then_inc(zeroed, 1)
                with dve.Fori(0, KVA) as i:
                    dve.wait_ge(qk_ld, START + (i + 1) * 64)
                    dve.wait_ge(sc_done, START + i * RT)
                    nc.vector.tensor_copy(k_hi[:, :], k_in[:, :]).then_inc(qk_hi, 1)
                    nc.vector.tensor_copy(q_st[:, :, :], q_in[:, :, :]).then_inc(qk_hi, 1)
                    dve.wait_ge(qk_hi, START + i * 2 + 2)
                    nc.vector.tensor_sub(k_lo[:, :], k_in[:, :], f32(k_hi[:, :])).then_inc(qk_ready, 1)
                    nc.vector.tensor_sub(q_st[HD:P, :, :], q_in[HD:P, :, :], f32(q_st[HD:P, :, :])).then_inc(qk_ready, 1)
                    for b in range(2):
                        dve.wait_ge(v_hi, START + i * 2 + b + 1)
                        v = v_st[:, b * 8:(b + 1) * 8, :]
                        nc.vector.tensor_sub(v[:, :, HD:P], vt[b][:, :].rearrange("p (j d) -> p j d", d=HD),
                                             f32(v[:, :, 0:HD])).then_inc(v_lo, 1)

                    def maxima(j):
                        s = j % 2
                        c0 = HD if j else P
                        n = i * RT + j + 1
                        dve.wait_ge(sc_done, START + n)
                        if j == 0:
                            dve.wait_ge(band_ld, START + (i + 1) * 32)
                        dve.wait_ge(tp_done, START + i * NK + (T0[j - 1] if j >= 2 else 0))
                        nc.vector.scalar_tensor_tensor(prob[s][:, :, c0:], sc[0][:, :, c0:], SCALE, band[:, :, c0 - HD:],
                                                       ALU.mult, ALU.add).then_inc(logits, 1)
                        dve.wait_ge(logits, START + n)
                        nc.vector.reduce_max(mx[:, s, :], prob[s][:, :, c0:], AXX).then_inc(mx_ready, 1)
                        dve.wait_ge(mx_ready, START + n)
                        nc.vector.tensor_tensor(m[:, s, :], mx[:, s, :], sink[:, :], ALU.max).then_inc(m_ready, 1)
                        dve.wait_ge(m_ready, START + n)
                        dve.wait_ge(sink_done, START + i * RT + (j - 1 if j >= 2 else 0))
                        nc.vector.tensor_sub(sink_m[:, s, :], sink[:, :], m[:, s, :])
                        nc.vector.tensor_scalar(neg_m[:, s, :], m[:, s, :], -1.0, None, ALU.mult).then_inc(neg_ready, 1)

                    def outputs(j):
                        s = j % 2
                        n = i * RT + j + 1
                        dve.wait_ge(sink_done, START + n)
                        dve.wait_ge(exp_done, START + n)
                        nc.vector.tensor_add(den_all[:, s, :], den[:, s, :], sink_e[:, s, :]).then_inc(den_ready, 1)
                        dve.wait_ge(den_ready, START + n)
                        nc.vector.reciprocal(rden[:, s, :], den_all[:, s, :]).then_inc(rden_ready, 1)
                        for x in [x for x, (u, _) in enumerate(tiles) if u == j]:
                            dve.wait_ge(hi_ready, START + i * NK + x + 1)
                            nc.vector.tensor_sub(pt_lo[x % 2][:, :], tp[x % 2][:, :], f32(pt_hi[x % 2][:, :])).then_inc(lo_ready, 1)
                        dve.wait_ge(half_ready, START + n)
                        nc.vector.tensor_add(y_sum[:, :, :], yt[:, :].rearrange("p (t c) -> p t c", c=P)[:, :, 0:HD],
                                             y_half[:, :, :]).then_inc(sum_ready, 1)
                        dve.wait_ge(sum_ready, START + n)
                        dve.wait_ge(rden_ready, START + n)
                        dve.wait_ge(y_saved[s], START + i * (RT // 2 * 16) + j // 2 * 16)
                        nc.vector.tensor_tensor(y_out[s][:, :, :], y_sum[:, :, :],
                                                rden[:, s, :].unsqueeze(2).to_broadcast([P, GA, HD]), ALU.mult)\
                          .then_inc(y_ready, 1)

                    maxima(0)
                    for j in range(RT):
                        if j + 1 < RT:
                            maxima(j + 1)
                        outputs(j)


def stage_mix_output(k, y, x, w_out, eps, x1_t, h2_t):
    nc = k.nc
    HALF = DT // 2
    with ExitStack() as st:
        w_hi = [k.sbuf(f"wo_hi{o}", [P, DT, P], F32R, stack=st) for o in range(DT)]
        w_lo = [k.sbuf(f"wo_lo{o}", [P, DT, P], F32R, stack=st) for o in range(DT)]
        y_row = [k.sbuf(f"y_row{b}", [P, TPG, D], stack=st) for b in range(2)]
        x_row = k.sbuf("x_row", [P, TPG, D], stack=st)
        y_hi = k.sbuf("y_hi", [P, DT, RG], F32R, stack=st)
        y_lo = k.sbuf("y_lo", [P, DT, RG], F32R, stack=st)
        xt = [k.sbuf(f"x1_{b}", [P, DT, RG], stack=st) for b in range(2)]
        w_raw = [xt[o // HALF][:, 2 * (o % HALF):2 * (o % HALF) + 2, :].rearrange("p a (b c) -> p (a b) c", c=P)
                 for o in range(DT)]
        y_tmp = [k.sbuf(f"y_tmp{s}", [P, RG], stack=st) for s in range(2)]
        sq = [k.sbuf(f"m_sq{s}", [P, RG], stack=st) for s in range(2)]
        sq_hi = [k.sbuf(f"m_sq_hi{s}", [P, RG], F32R, stack=st) for s in range(2)]
        sq_lo = [k.sbuf(f"m_sq_lo{s}", [P, RG], F32R, stack=st) for s in range(2)]
        rms = k.sbuf("m_rms", [P, RG], stack=st)
        rstd = k.sbuf("m_rstd", [P, RG], stack=st)
        ssq, g_rms, g_rstd = (k.sbuf("m_" + n, [P, 2 * TPG], stack=st) for n in ("ssq", "g_rms", "g_rstd"))
        acc = k.banks("m_acc", HALF, st)
        tr = k.banks("m_tr", 2, st)
        total = k.banks("m_total", 1, st)[0]
        junk = k.banks("m_junk", 1, st)[0]
        w_ld = k.sems("m_w_in", DT)
        y_in = k.sems("m_y_in", 2)
        names = ("w_hi", "w_lo", "x_in", "squared", "g_rms", "g_rstd", "scaled", "tr", "copied", "y_hi", "y_lo",
                 "k_done", "acc", "resid", "sq", "sq_hi", "sq_lo", "sum", "rms", "rstd", "xn", "h2")
        S_ = {n: k.sem("m_" + n) for n in names}
        x1_saved, h2_saved = k.sems("m_x1_saved", 2), k.sems("m_h2_saved", 2)
        wo_v = w_out.rearrange("o (t p) n -> p (o t) n", p=P)
        rows_of = lambda v, r: v[bass.ds(r, 1), :, :, :].rearrange("o p t d -> p (o t) d")
        y_v = y.rearrange("(r t p) d -> r p t d", p=P, t=TPG)
        x_v = x.rearrange("o (r t p) d -> (o r) p t d", p=P, t=TPG)
        x1_v, h2_v = (v.rearrange("(t p) n -> p t n", p=P) for v in (x1_t, h2_t))
        TR = 4 * DT
        Y_AT, X_AT = (0, 2 * DT), (DT, 3 * DT)

        start_counts(k)
        with nc.Block() as block:
            def store_x1(sp, i, b):
                for half in range(2):
                    o = slice(half * HALF, (half + 1) * HALF)
                    sp.wait_ge(S_["resid"], START + (i * 2 + b) * DT + (half + 1) * HALF)
                    sp.dma_start(x1_v[:, o, bass.ds((i * 2 + b) * RG, RG)], xt[b][:, o, :]).then_inc(x1_saved[b], 16)

            def store_h2(sp, i, b):
                sp.wait_ge(S_["h2"], START + (i * 2 + b + 1) * DT)
                sp.dma_start(h2_v[:, :, bass.ds((i * 2 + b) * RG, RG)], xt[b][:, :, :]).then_inc(h2_saved[b], 16)

            @block.sync
            def _(sp):
                for o in range(DT):
                    sp.dma_start(w_raw[o], wo_v[:, :, o * P:(o + 1) * P]).then_inc(w_ld[o], 16)
                with sp.Fori(0, NRG // 2) as i:
                    for b in range(2):
                        sp.wait_ge(S_["tr"], START + i * TR + Y_AT[b] + DT - TR)
                        sp.dma_start(y_row[b][:, :, :], rows_of(y_v, i * 2 + b)).then_inc(y_in[b], 16)
                    for b in range(2):
                        sp.wait_ge(S_["tr"], START + i * TR + X_AT[b - 1] + DT - (TR if b == 0 else 0))
                        sp.dma_start(x_row[:, :, :], rows_of(x_v, i * 2 + b)).then_inc(S_["x_in"], 16)
                        if b == 1:
                            store_h2(sp, i, 0)
                        store_x1(sp, i, b)
                    store_h2(sp, i, 1)
                for b in range(2):
                    sp.wait_ge(x1_saved[b], START + NRG // 2 * 32)
                    sp.wait_ge(h2_saved[b], START + NRG // 2 * 16)

            @block.tensor
            def _(pe):
                def transposes(i, n, rows, t):
                    pe.wait_ge(S_["copied"], START + i * TR + n - 1)
                    for q in range(TPG):
                        last = nc.tensor.transpose(tr[n % 2][:, q * P:(q + 1) * P], rows[:, q, t * P:(t + 1) * P],
                                                   k.ident[:, :])
                    last.then_inc(S_["tr"], 1)

                def products(r, half, j):
                    for o in range(HALF):
                        if j == 0:
                            pe.wait_ge(S_["resid"], START + r * DT + (half - 1) * HALF + o + 1)
                        out = half * HALF + o
                        last = split_product(nc, acc[o][:, :], w_hi[out][:, j, :], w_lo[out][:, j, :],
                                             y_hi[:, j, :], y_lo[:, j, :], j == 0, j == DT - 1)
                        if j == DT - 1:
                            last.then_inc(S_["acc"], 1)
                    if j < DT - 1:
                        last.then_inc(S_["k_done"], 1)

                def sums(r, t):
                    pe.wait_ge(S_["sq_lo"], START + r * DT + t + 1)
                    if t == 0:
                        pe.wait_ge(S_["rms"], START + r)
                    nc.tensor.matmul(total[:, :], k.ones_r[:, :], sq_hi[t % 2][:, :], start=(t == 0), stop=False)
                    nc.tensor.matmul(total[:, :], k.ones_r[:, :], sq_lo[t % 2][:, :], start=False, stop=(t == DT - 1))\
                      .then_inc(S_["sum"], 1)

                pe.wait_ge(S_["w_lo"], START + DT)
                with pe.Fori(0, NRG // 2) as i:
                    pe.wait_ge(S_["scaled"], START + (i * 2 + 1) * 2 * TPG)
                    for t in range(DT):
                        transposes(i, Y_AT[0] + t, y_row[0], t)
                    for b in range(2):
                        r = i * 2 + b
                        for j in range(DT):
                            if j == 0:
                                pe.wait_ge(S_["x_in"], START + (r + 1) * 16)
                            transposes(i, X_AT[b] + j, x_row, j)
                            pe.wait_ge(S_["y_lo"], START + r * DT + j + 1)
                            products(r, 0, j)
                            if b == 1 and j > 0:
                                sums(r - 1, j - 1)
                        if b == 1:
                            sums(r - 1, DT - 1)
                        for j in range(DT):
                            products(r, 1, j)
                            if b == 0:
                                if j == 0:
                                    pe.wait_ge(S_["scaled"], START + (r + 2) * 2 * TPG)
                                transposes(i, Y_AT[1] + j, y_row[1], j)
                            elif j >= HALF:
                                sums(r, j - HALF)
                    for t in range(HALF, DT):
                        sums(i * 2 + 1, t)

            @block.scalar
            def _(act):
                def y_squares(i, b, n):
                    r = i * 2 + b
                    if n == 0:
                        act.wait_ge(y_in[b], START + (i + 1) * 16)
                        act.wait_ge(S_["g_rms"], START + r)
                    act.wait_ge(S_["squared"], START + r * 2 * TPG + n)
                    q, a = n // 2, n % 2
                    nc.scalar.activation(junk[:, :], y_row[b][:, q, a * WA:(a + 1) * WA], ACT.Square,
                                         accum_out=ssq[:, n:n + 1]).then_inc(S_["squared"], 1)

                def y_root(r):
                    act.wait_ge(S_["squared"], START + (r + 1) * 2 * TPG)
                    act.wait_ge(S_["g_rstd"], START + r)
                    nc.scalar.activation(g_rms[:, :], ssq[:, :], ACT.Sqrt, bias=eps[:, 0:1], scale=1.0 / WA)\
                      .then_inc(S_["g_rms"], 1)

                def y_copy(i, b, t):
                    n = Y_AT[b] + t
                    act.wait_ge(S_["tr"], START + i * TR + n + 1)
                    act.wait_ge(S_["y_lo"], START + (i * 2 + b) * DT + t - 1)
                    nc.scalar.activation(y_tmp[t % 2][:, :], tr[n % 2][:, :], ACT.Copy,
                                         scale=k.cols[:, V_GGRP + t:V_GGRP + t + 1]).then_inc(S_["copied"], 1)

                def x_copy(i, b, t):
                    n = X_AT[b] + t
                    if t == 0:
                        act.wait_ge(h2_saved[b], START + i * 16)
                    act.wait_ge(S_["tr"], START + i * TR + n + 1)
                    nc.scalar.activation(xt[b][:, t, :], tr[n % 2][:, :], ACT.Copy).then_inc(S_["copied"], 1)

                def square(i, b, t):
                    r = i * 2 + b
                    act.wait_ge(S_["resid"], START + r * DT + t + 1)
                    act.wait_ge(S_["sq_lo"], START + r * DT + t - 1)
                    nc.scalar.activation(sq[t % 2][:, :], xt[b][:, t, :], ACT.Square).then_inc(S_["sq"], 1)

                def root(r):
                    act.wait_ge(S_["sum"], START + (r + 1) * DT)
                    act.wait_ge(S_["rstd"], START + r)
                    nc.scalar.activation(rms[:, :], total[:, :], ACT.Sqrt, bias=eps[:, 0:1], scale=1.0 / D)\
                      .then_inc(S_["rms"], 1)

                def affine(i, b, t):
                    act.wait_ge(S_["xn"], START + (i * 2 + b) * DT + t + 1)
                    nc.scalar.activation(xt[b][:, t, :], xt[b][:, t, :], ACT.Identity,
                                         bias=k.mod[:, 3 * DT + t:3 * DT + t + 1], scale=k.a_ffn[:, t:t + 1])\
                      .then_inc(S_["h2"], 1)

                with act.Fori(0, NRG // 2) as i:
                    for n in range(2 * TPG):
                        y_squares(i, 0, n)
                    y_root(i * 2)
                    for t in range(DT):
                        y_copy(i, 0, t)
                    for t in range(DT):
                        x_copy(i, 0, t)
                        if t < TPG:
                            y_squares(i, 1, 2 * t)
                            y_squares(i, 1, 2 * t + 1)
                        if t == TPG:
                            y_root(i * 2 + 1)
                    for t in range(DT):
                        y_copy(i, 1, t)
                    for t in range(DT):
                        x_copy(i, 1, t)
                        square(i, 0, t)
                    root(i * 2)
                    for t in range(DT):
                        affine(i, 0, t)
                    for t in range(DT):
                        square(i, 1, t)
                    root(i * 2 + 1)
                    for t in range(DT):
                        affine(i, 1, t)

            @block.vector
            def _(dve):
                for o in range(DT):
                    dve.wait_ge(w_ld[o], START + 16)
                    nc.vector.tensor_copy(w_hi[o][:, :, :], w_raw[o]).then_inc(S_["w_hi"], 1)
                    dve.wait_ge(S_["w_hi"], START + o + 1)
                    nc.vector.tensor_sub(w_lo[o][:, :, :], w_raw[o], f32(w_hi[o][:, :, :])).then_inc(S_["w_lo"], 1)

                def y_scale(r, b):
                    dve.wait_ge(S_["g_rms"], START + r + 1)
                    nc.vector.reciprocal(g_rstd[:, :], g_rms[:, :]).then_inc(S_["g_rstd"], 1)
                    dve.wait_ge(S_["g_rstd"], START + r + 1)
                    for n in range(2 * TPG):
                        part = y_row[b][:, n // 2, (n % 2) * WA:(n % 2 + 1) * WA]
                        nc.vector.tensor_scalar(part, part, g_rstd[:, n:n + 1], None, ALU.mult).then_inc(S_["scaled"], 1)

                def y_split(i, b, t):
                    r = i * 2 + b
                    dve.wait_ge(S_["copied"], START + i * TR + Y_AT[b] + t + 1)
                    if t < DT - 1:
                        dve.wait_ge(S_["k_done"], START + r * 2 * (DT - 1) - (DT - 1) + t + 1)
                    else:
                        dve.wait_ge(S_["acc"], START + r * DT)
                    nc.vector.tensor_copy(y_hi[:, t, :], y_tmp[t % 2][:, :]).then_inc(S_["y_hi"], 1)
                    dve.wait_ge(S_["y_hi"], START + r * DT + t + 1)
                    nc.vector.tensor_sub(y_lo[:, t, :], y_tmp[t % 2][:, :], f32(y_hi[:, t, :])).then_inc(S_["y_lo"], 1)

                def residual(i, b, half):
                    for t in range(half * HALF, (half + 1) * HALF):
                        if t == half * HALF:
                            dve.wait_ge(S_["copied"], START + i * TR + X_AT[b] + DT)
                        dve.wait_ge(S_["acc"], START + (i * 2 + b) * DT + t + 1)
                        nc.vector.scalar_tensor_tensor(xt[b][:, t, :], acc[t % HALF][:, :],
                                                       k.mod[:, 2 * DT + t:2 * DT + t + 1], xt[b][:, t, :],
                                                       ALU.mult, ALU.add).then_inc(S_["resid"], 1)

                def square_split(r, t):
                    dve.wait_ge(S_["sq"], START + r * DT + t + 1)
                    dve.wait_ge(S_["sum"], START + r * DT + t - 1)
                    nc.vector.tensor_copy(sq_hi[t % 2][:, :], sq[t % 2][:, :]).then_inc(S_["sq_hi"], 1)
                    dve.wait_ge(S_["sq_hi"], START + r * DT + t + 1)
                    nc.vector.tensor_sub(sq_lo[t % 2][:, :], sq[t % 2][:, :], f32(sq_hi[t % 2][:, :]))\
                      .then_inc(S_["sq_lo"], 1)

                def normalise(i, b):
                    r = i * 2 + b
                    dve.wait_ge(S_["rms"], START + r + 1)
                    nc.vector.reciprocal(rstd[:, :], rms[:, :]).then_inc(S_["rstd"], 1)
                    dve.wait_ge(S_["rstd"], START + r + 1)
                    dve.wait_ge(x1_saved[b], START + (i + 1) * 32)
                    for t in range(DT):
                        nc.vector.tensor_tensor(xt[b][:, t, :], xt[b][:, t, :], rstd[:, :], ALU.mult)\
                          .then_inc(S_["xn"], 1)

                with dve.Fori(0, NRG // 2) as i:
                    y_scale(i * 2, 0)
                    for t in range(DT):
                        y_split(i, 0, t)
                    y_scale(i * 2 + 1, 1)
                    residual(i, 0, 0)
                    for t in range(DT):
                        y_split(i, 1, t)
                    residual(i, 0, 1)
                    for t in range(DT):
                        square_split(i * 2, t)
                    residual(i, 1, 0)
                    normalise(i, 0)
                    for t in range(HALF):
                        square_split(i * 2 + 1, t)
                    residual(i, 1, 1)
                    for t in range(HALF, DT):
                        square_split(i * 2 + 1, t)
                    normalise(i, 1)


def stage_ffn(k, x1_t, h2_t, w_gate_up, w_down, g_final, eps, out):
    nc = k.nc
    NSLOT = 4
    DOWN = [(0, 8), (8, 8), (16, FT - 16)]
    NX = 4
    with ExitStack() as st:
        raw = [k.sbuf(f"w_raw{s}", [P, DT, P], stack=st) for s in range(NSLOT)]
        hi = [k.sbuf(f"w_hi{s}", [P, DT, P], F32R, stack=st) for s in range(NSLOT)]
        lo = [k.sbuf(f"w_lo{s}", [P, DT, P], F32R, stack=st) for s in range(NSLOT)]
        act_hi = k.sbuf("act_hi", [P, FT, RG], F32R, stack=st)
        act_lo = k.sbuf("act_lo", [P, FT, RG], F32R, stack=st)
        h_hi = k.sbuf("f_h_hi", [P, DT, RG], F32R, stack=st)
        h_lo = k.sbuf("f_h_lo", [P, DT, RG], F32R, stack=st)
        h_raw = [k.sbuf(f"f_h_raw{s}", [P, RG], stack=st) for s in range(2)]
        x1 = [k.sbuf(f"f_x1_{s}", [P, RG], stack=st) for s in range(NX)]
        tmp = [k.sbuf(f"f_tmp{s}", [P, RG], stack=st) for s in range(2)]
        rows = k.sbuf("f_rows", [P, TPG, D], stack=st)
        g_fin = k.sbuf("f_g_final", [P, D], stack=st)
        ssq = k.sbuf("f_ssq", [P, 2 * TPG], stack=st)
        mean, rms, rstd = (k.sbuf("f_" + n, [P, TPG], stack=st) for n in ("mean", "rms", "rstd"))
        bank = k.banks("f_bank", 8, st)
        w_ld, w_hi, w_lo, w_used = (k.sems("f_" + n, NSLOT) for n in ("w_in", "w_hi", "w_lo", "w_used"))
        names = ("g_in", "h_hi", "h_lo", "silu", "act_f", "act_hi", "act_lo", "final", "fin_t", "copied",
                 "squared", "ssq", "rms", "rstd", "o_ready", "saved")
        S_ = {n: k.sem("f_" + n) for n in names}
        h_in, x1_in = k.sems("f_h_in", 2), k.sems("f_x1_in", NX)
        wg_v = w_gate_up.rearrange("o (t p) n -> p (o t) n", p=P)
        wd_v = w_down.rearrange("o (t p) n -> p (o t) n", p=P)
        o_v = out.rearrange("o (r t p) d -> (o r) p t d", p=P, t=TPG)
        N_UP, N_DN = 2 * FT, len(DOWN) * DT
        PER = (N_UP + N_DN) // NSLOT
        DN0 = N_UP // NSLOT

        start_counts(k)
        with nc.Block() as block:
            @block.sync
            def _(sp):
                def load(s, t, dst, src):
                    sp.wait_ge(w_lo[s], START + t)
                    sp.dma_start(dst, src).then_inc(w_ld[s], 16)

                sp.dma_start(g_fin[:, :], g_final.partition_broadcast(P)).then_inc(S_["g_in"], 16)
                with sp.Fori(0, NRG) as r:
                    with sp.Fori(0, FT // 2) as a:
                        for s in range(NSLOT):
                            col = (a * 2 + s // 2) * P + (s % 2) * DFF
                            load(s, r * PER + a, raw[s][:, :, :], wg_v[:, :, bass.ds(col, P)])
                    with sp.Fori(0, DT // 4) as a:
                        for n in range(12):
                            t0, nt = DOWN[n % 3]
                            load(n % NSLOT, r * PER + DN0 + a * 3 + n // NSLOT,
                                 raw[n % NSLOT][:, 0:nt, :], wd_v[:, t0:t0 + nt, bass.ds((a * 4 + n // 3) * P, P)])

            @block.tensor
            def _(pe):
                def product(out_bank, s, t, rhs_hi, rhs_lo, nt, first, last):
                    pe.wait_ge(w_lo[s], START + t + 1)
                    for j in range(nt):
                        x_ = split_product(nc, out_bank, hi[s][:, j, :], lo[s][:, j, :], rhs_hi(j), rhs_lo(j),
                                           first and j == 0, last and j == nt - 1)
                    x_.then_inc(w_used[s], 1)

                def to_rows(r, a, i):
                    pe.wait_ge(S_["final"], START + r * DT + a * 4 + i + 1)
                    pe.wait_ge(S_["copied"], START + r * DT + a * 4 + i - 1)
                    for q in range(TPG):
                        last = nc.tensor.transpose(bank[6 + i % 2][:, q * P:(q + 1) * P], x1[i % NX][:, q * P:(q + 1) * P],
                                                   k.ident[:, :])
                    last.then_inc(S_["fin_t"], 1)

                with pe.Fori(0, NRG) as r:
                    with pe.Fori(0, FT // 2) as a:
                        pe.wait_ge(S_["h_lo"], START + (r + 1) * DT)
                        for n in range(4):
                            if n % 2 == 0:
                                pe.wait_ge(S_["act_f"], START + r * FT + a * 2 + (n // 2 - 1))
                            product(bank[n][:, :], n, r * PER + a,
                                    lambda j: h_hi[:, j, :], lambda j: h_lo[:, j, :], DT, True, True)
                    with pe.Fori(0, DT // 4) as a:
                        pe.wait_ge(S_["act_lo"], START + (r + 1) * FT)
                        for n in range(12):
                            t0, nt = DOWN[n % 3]
                            if n % 3 == 0:
                                pe.wait_ge(S_["final"], START + r * DT + a * 4 + (n // 3 - 1))
                            product(bank[4 + (n // 3) % 2][:, :], n % NSLOT, r * PER + DN0 + a * 3 + n // NSLOT,
                                    lambda j: act_hi[:, t0 + j, :], lambda j: act_lo[:, t0 + j, :], nt,
                                    n % 3 == 0, n % 3 == 2)
                            if n % 3 == 0 and n > 0:
                                to_rows(r, a, n // 3 - 1)
                        to_rows(r, a, 3)

            @block.scalar
            def _(act):
                def load_h(r, t):
                    act.wait_ge(S_["h_lo"], START + r * DT + t - 1)
                    act.dma_start(h_raw[t % 2][:, :], h2_t[t * P:(t + 1) * P, bass.ds(r * RG, RG)]).then_inc(h_in[t % 2], 16)

                def load_x1(r, t):
                    act.dma_start(x1[t % NX][:, :], x1_t[t * P:(t + 1) * P, bass.ds(r * RG, RG)]).then_inc(x1_in[t % NX], 16)

                def group(r, more):
                    with act.Fori(0, FT // 2) as a:
                        for n in range(2):
                            act.wait_ge(w_used[2 * n], START + r * PER + a + 1)
                            act.wait_ge(S_["act_lo"], START + r * FT + a * 2 + n - 1)
                            nc.scalar.activation(tmp[n][:, :], bank[2 * n][:, :], ACT.Silu).then_inc(S_["silu"], 1)
                    for t in range(NX - 1):
                        load_x1(r, t)
                    if more:
                        act.wait_ge(S_["act_lo"], START + (r + 1) * FT)
                        load_h(r + 1, 0)
                        load_h(r + 1, 1)
                    act.wait_ge(S_["saved"], START + r * 16)
                    for t in range(DT):
                        act.wait_ge(S_["fin_t"], START + r * DT + t + 1)
                        nc.scalar.activation(rows[:, :, t * P:(t + 1) * P],
                                             bank[6 + t % 2][:, :].rearrange("p (q c) -> p q c", c=P), ACT.Copy)\
                          .then_inc(S_["copied"], 1)
                        if t + NX - 1 < DT:
                            load_x1(r, t + NX - 1)
                        if more and t + 2 < DT:
                            load_h(r + 1, t + 2)
                    act.wait_ge(S_["copied"], START + (r + 1) * DT)
                    for n in range(2 * TPG):
                        q, half = n // 2, n % 2
                        act.wait_ge(S_["squared"], START + r * 2 * TPG + n)
                        nc.scalar.activation(bank[6][:, :], rows[:, q, half * RG:(half + 1) * RG], ACT.Square,
                                             accum_out=ssq[:, half * TPG + q:half * TPG + q + 1]).then_inc(S_["squared"], 1)
                    act.wait_ge(S_["ssq"], START + r + 1)
                    nc.scalar.activation(rms[:, :], mean[:, :], ACT.Sqrt, bias=eps[:, 0:1], scale=1.0 / D)\
                      .then_inc(S_["rms"], 1)
                    act.wait_ge(S_["o_ready"], START + (r + 1) * TPG)
                    act.dma_start(o_v[bass.ds(r, 1), :, :, :].rearrange("o p t d -> p (o t) d"), rows[:, :, :])\
                       .then_inc(S_["saved"], 16)

                for t in range(DT):
                    load_h(0, t)
                with act.Fori(0, NRG - 1) as r:
                    group(r, True)
                group(NRG - 1, False)
                act.wait_ge(S_["saved"], START + NRG * 16)

            @block.vector
            def _(dve):
                def split(s, t, nt=DT):
                    dve.wait_ge(w_ld[s], START + (t + 1) * 16)
                    dve.wait_ge(w_used[s], START + t)
                    nc.vector.tensor_copy(hi[s][:, 0:nt, :], raw[s][:, 0:nt, :]).then_inc(w_hi[s], 1)
                    dve.wait_ge(w_hi[s], START + t + 1)
                    nc.vector.tensor_sub(lo[s][:, 0:nt, :], raw[s][:, 0:nt, :], f32(hi[s][:, 0:nt, :])).then_inc(w_lo[s], 1)

                def h_split(r, t):
                    dve.wait_ge(h_in[t % 2], START + (r * (DT // 2) + t // 2 + 1) * 16)
                    nc.vector.tensor_copy(h_hi[:, t, :], h_raw[t % 2][:, :]).then_inc(S_["h_hi"], 1)
                    dve.wait_ge(S_["h_hi"], START + r * DT + t + 1)
                    nc.vector.tensor_sub(h_lo[:, t, :], h_raw[t % 2][:, :], f32(h_hi[:, t, :])).then_inc(S_["h_lo"], 1)

                def gated(r, a, n):
                    ft = a * 2 + n
                    f = r * FT + ft
                    part = lambda v: v[:, bass.ds(ft, 1), :].rearrange("p o n -> p (o n)")
                    dve.wait_ge(S_["silu"], START + f + 1)
                    dve.wait_ge(w_used[2 * n + 1], START + r * PER + a + 1)
                    nc.vector.tensor_tensor(tmp[n][:, :], bank[2 * n + 1][:, :], tmp[n][:, :], ALU.mult).then_inc(S_["act_f"], 1)
                    dve.wait_ge(S_["act_f"], START + f + 1)
                    nc.vector.tensor_copy(part(act_hi), tmp[n][:, :]).then_inc(S_["act_hi"], 1)
                    dve.wait_ge(S_["act_hi"], START + f + 1)
                    nc.vector.tensor_sub(part(act_lo), tmp[n][:, :], f32(part(act_hi))).then_inc(S_["act_lo"], 1)

                def finish(r, t):
                    u = 3 * t + 2
                    dve.wait_ge(x1_in[t % NX], START + (r * (DT // NX) + t // NX + 1) * 16)
                    dve.wait_ge(w_used[u % NSLOT], START + r * PER + DN0 + u // NSLOT + 1)
                    nc.vector.scalar_tensor_tensor(x1[t % NX][:, :], bank[4 + t % 2][:, :], k.mod[:, 5 * DT + t:5 * DT + t + 1],
                                                   x1[t % NX][:, :], ALU.mult, ALU.add).then_inc(S_["final"], 1)

                def final_norm(r):
                    dve.wait_ge(S_["squared"], START + (r + 1) * 2 * TPG)
                    nc.vector.tensor_tensor(mean[:, :], ssq[:, 0:TPG], ssq[:, TPG:2 * TPG], ALU.add).then_inc(S_["ssq"], 1)
                    dve.wait_ge(S_["rms"], START + r + 1)
                    nc.vector.reciprocal(rstd[:, :], rms[:, :]).then_inc(S_["rstd"], 1)
                    dve.wait_ge(S_["rstd"], START + r + 1)
                    for q in range(TPG):
                        nc.vector.scalar_tensor_tensor(rows[:, q, :], rows[:, q, :], rstd[:, q:q + 1], g_fin[:, :],
                                                       ALU.mult, ALU.mult).then_inc(S_["o_ready"], 1)

                def group(r, more):
                    with dve.Fori(0, FT // 2 - 1) as a:
                        for n in range(2):
                            gated(r, a, n)
                            for s in (2 * n, 2 * n + 1):
                                split(s, r * PER + a + 1)
                    for n in range(2):
                        gated(r, FT // 2 - 1, n)
                        for s in (2 * n, 2 * n + 1):
                            split(s, r * PER + DN0, DOWN[s % 3][1])
                    for n in range(N_DN):
                        m = n + NSLOT
                        if m < N_DN:
                            split(m % NSLOT, r * PER + DN0 + m // NSLOT, DOWN[m % 3][1])
                        elif more:
                            split(m % NSLOT, r * PER + DN0 + m // NSLOT)
                        if n % 3 == 1 and more:
                            h_split(r + 1, n // 3)
                        if n % 3 == 2:
                            finish(r, n // 3)
                    final_norm(r)

                for t in range(DT):
                    h_split(0, t)
                    if t % 2:
                        split(t // 2, 0)
                dve.wait_ge(S_["g_in"], START + 16)
                with dve.Fori(0, NRG - 1) as r:
                    group(r, True)
                group(NRG - 1, False)


def build(nc, x, c, w_ada, b_ada, g_norm_mix, w_in, b_forget, sinks, g_grp_a, g_grp_b, w_out, g_norm_ffn,
          w_gate_up, w_down, g_final, ident, ones, mask, band, out):
    proj = nc.dram_tensor("proj_t", (PT * P, S), F32, kind="Internal").ap()
    nf = nc.dram_tensor("neg_f8", (HB, S), F32, kind="Internal").ap()
    y = nc.dram_tensor("y_heads", (S, WA + WB), F32, kind="Internal").ap()
    x1 = nc.dram_tensor("x1_t", (D, S), F32, kind="Internal").ap()
    h2 = nc.dram_tensor("h2_t", (D, S), F32, kind="Internal").ap()
    as_rows = lambda v: v.rearrange("o (t p) -> (o t) p", p=P)
    vectors = [(V_BADA, as_rows(b_ada)), (V_GMIX, as_rows(g_norm_mix)), (V_GFFN, as_rows(g_norm_ffn)),
               (V_GFIN, g_final.rearrange("(t p) -> t p", p=P)), (V_GGRP, as_rows(g_grp_a)),
               (V_GGRP + WA // P, as_rows(g_grp_b))]
    with ExitStack() as stack:
        k = Core(nc, stack)
        eps = k.sbuf("eps", [P, 1])
        eps_set = k.sem("eps_set")
        with nc.Block() as block:
            @block.vector
            def _(dve):
                nc.vector.memset(eps[:, :], EPS).then_inc(eps_set, 1)
                dve.wait_ge(eps_set, 1)
        stage_modulation(k, c, w_ada, vectors, ident, ones)
        k.end_stage()
        with ExitStack() as st:
            h_hi = k.sbuf("h_hi", [P, DT, S], F32R, stack=st)
            h_lo = k.sbuf("h_lo", [P, DT, S], F32R, stack=st)
            stage_input_norm(k, x, eps, h_hi, h_lo, st)
            k.end_stage()
            stage_projection(k, w_in, b_forget, h_hi, h_lo, proj, nf)
            k.end_stage()
        stage_attention_b(k, proj, nf, mask, y)
        k.end_stage()
        stage_attention_a(k, proj, band, sinks, y)
        k.end_stage()
        stage_mix_output(k, y, x, w_out, eps, x1, h2)
        k.end_stage()
        stage_ffn(k, x1, h2, w_gate_up, w_down, g_final, eps, out)


_INS = ["x", "c", "w_ada", "b_ada", "g_norm_mix", "w_in", "b_forget", "sinks", "g_grp_a", "g_grp_b", "w_out",
        "g_norm_ffn", "w_gate_up", "w_down", "g_final"]


def _constants():
    import numpy as np
    q, key = np.arange(P)[:, None], np.arange(P)[None, :]
    mask = np.where(key <= q, 0.0, INV_SCALE * NEG).astype(np.float32)
    chunk = 64
    kb = np.arange(BAND)[None, :]
    dist = np.abs(q - (kb - chunk)).astype(np.float32)
    seen = (kb // chunk >= q // chunk) & (kb // chunk <= q // chunk + 1)
    slopes = np.exp2(-8.0 * (np.arange(HA, dtype=np.float32) + 1.0) / HA).astype(np.float32)
    band = np.where(seen[None], -slopes[:, None, None] * dist[None], np.float32(NEG)).astype(np.float32)
    band = np.ascontiguousarray(band.reshape(KVA, GA, P, BAND).transpose(0, 2, 1, 3))
    return {"ident": np.eye(P, dtype=np.float32), "ones": np.ones((P, P), np.float32), "mask": mask, "band": band}


def kernel(**inputs):
    import numpy as np
    import concourse.bacc as bacc
    from concourse.bass_utils import run_bass_kernel_spmd as run

    nc = bacc.Bacc("TRN2", target_bir_lowering=False, num_devices=1)
    arrays, args = {}, []
    for name, a in [(n, np.ascontiguousarray(inputs[n])) for n in _INS] + list(_constants().items()):
        arrays[f"in_{name}"] = a
        args.append(nc.dram_tensor(f"in_{name}", a.shape, mybir.dt.from_np(a.dtype), kind="ExternalInput").ap())
    args.append(nc.dram_tensor("out", (1, S, D), F32, kind="ExternalOutput").ap())
    build(nc, *args)
    r = run(nc, [arrays], core_ids=[0])
    return r.results[0]["out"]
```

```python
from contextlib import ExitStack

import concourse.bass as bass
from concourse import mybir
from concourse.alu_op_type import AluOpType as ALU

F32 = mybir.dt.float32
F32R = mybir.dt.float32r
ACT = mybir.ActivationFunctionType
AXX = mybir.AxisListType.X

P = 128
D = 1024
S = 2048
HD = 64
HA, KVA, HB = 8, 2, 8
GA = HA // KVA
WA, WB = HA * HD, HB * HD
DFF = 2816
EPS = 1e-6
START = 128
SCALE = HD ** -0.5
INV_SCALE = 8.0
NEG = -1e30
DT = D // P
RT = S // P
RG = 512
NRG = S // RG
TPG = RG // P
FT = DFF // P
QA0, KA0, VA0 = 0, WA, WA + KVA * HD
QB0 = VA0 + KVA * HD
KB0, VB0, FG0 = QB0 + WB, QB0 + 2 * WB, QB0 + 3 * WB
IN_COLS = FG0 + HB
PT = FG0 // P
NOW = 2
BAND = 192
V_BADA, V_GMIX, V_GFFN, V_GFIN, V_GGRP = 0, 48, 56, 64, 72
V_ROWS = 80


class Core:

    def __init__(self, nc, stack):
        self.nc, self.stack, self.stage_sems = nc, stack, []
        self.ident = self.sbuf("ident", [P, P])
        self.ones_r = self.sbuf("ones_r", [P, P], F32R)
        self.cols = self.sbuf("cols", [P, V_ROWS])
        self.mod = self.sbuf("mod", [P, 48])
        self.c_act = self.sbuf("c_act", [P, DT])
        self.a_mix = self.sbuf("a_mix", [P, DT])
        self.a_ffn = self.sbuf("a_ffn", [P, DT])

    def sbuf(self, name, shape, dt=F32, stack=None):
        return (stack or self.stack).enter_context(self.nc.sbuf_tensor(name, shape, dt))

    def banks(self, name, n, stack):
        return [stack.enter_context(self.nc.psum_tensor(f"{name}{i}", [P, RG], F32)) for i in range(n)]

    def sem(self, name):
        self.stage_sems.append(self.nc.alloc_semaphore(name=name))
        return self.stage_sems[-1]

    def end_stage(self):
        self.nc.clear_and_free_semaphores(self.stage_sems)
        self.stage_sems = []
        self.nc.all_engine_barrier()

    def sems(self, name, n):
        return [self.sem(f"{name}{i}") for i in range(n)]


def start_counts(k):
    with k.nc.Block() as block:
        @block.gpsimd
        def _(pool):
            for sem in k.stage_sems:
                pool.sem_inc(sem, START)


def wait_apart(eng, passed, sem, value):
    eng.wait_ge(sem, value)
    eng.sem_inc(passed, 1)


def f32(ap):
    return ap.bitcast(F32)


def stage_modulation(k, c, w_ada, vectors, ident_in, ones_in):
    nc = k.nc
    CH = NOW * D // RG
    with ExitStack() as st:
        c_col = k.sbuf("c_col", [P, DT], stack=st)
        table = k.sbuf("table", [V_ROWS, P], stack=st)
        ones = k.sbuf("ones_raw", [P, P], stack=st)
        w = [k.sbuf(f"w_ada{s}", [P, DT, RG], stack=st) for s in range(CH)]
        row = k.sbuf("mod_row", [1, CH * RG], stack=st)
        acc = k.banks("mod_acc", CH, st)
        small = k.banks("mod_col", 2, st)
        const_in, c_in = k.sem("const_in"), k.sem("c_in")
        w_in = k.sems("w_ada_in", CH)
        c_ready, ones_ready = k.sem("c_ready"), k.sem("ones_ready")
        table_t, table_used = k.sem("table_t"), k.sem("table_used")
        prod = k.sems("ada_product", CH)
        row_ready, mod_t, mod_ready = k.sem("ada_row"), k.sem("mod_t"), k.sem("mod_ready")
        w_view = w_ada.rearrange("o (p t) n -> p (o t) n", t=DT)

        start_counts(k)
        with nc.Block() as block:
            @block.sync
            def _(sp):
                sp.dma_start(c_col[:, :], c.rearrange("o (p t) -> p (o t)", t=DT)).then_inc(c_in, 16)
                for s in range(CH):
                    sp.dma_start(w[s][:, :, :], w_view[:, :, s * RG:(s + 1) * RG]).then_inc(w_in[s], 16)

            @block.scalar
            def _(act):
                act.dma_start(k.ident[:, :], ident_in).then_inc(const_in, 16)
                act.dma_start(ones[:, :], ones_in).then_inc(const_in, 16)
                for at, v in vectors:
                    act.dma_start(table[at:at + v.shape[0], :], v).then_inc(const_in, 16)
                act.wait_ge(c_in, START + 16)
                nc.scalar.activation(k.c_act[:, :], c_col[:, :], ACT.Silu).then_inc(c_ready, 1)

            @block.tensor
            def _(pe):
                pe.wait_ge(const_in, START + 16 * (2 + len(vectors)))
                nc.tensor.transpose(small[0][:, 0:V_ROWS], table[:, :], k.ident[0:V_ROWS, 0:V_ROWS]).then_inc(table_t, 1)
                pe.wait_ge(c_ready, START + 1)
                for s in range(CH):
                    pe.wait_ge(w_in[s], START + 16)
                    for t in range(DT):
                        last = nc.tensor.matmul(acc[s][0:1, :], k.c_act[:, t:t + 1], w[s][:, t, :],
                                                start=(t == 0), stop=(t == DT - 1))
                    last.then_inc(prod[s], 1)
                pe.wait_ge(row_ready, START + CH)
                for j in range(NOW * DT):
                    last = nc.tensor.matmul(small[1][:, j:j + 1], row[0:1, j * P:(j + 1) * P], k.ident[0:1, 0:1],
                                            start=True, stop=True)
                last.then_inc(mod_t, 1)

            @block.vector
            def _(dve):
                dve.wait_ge(const_in, START + 16 * (2 + len(vectors)))
                nc.vector.tensor_copy(k.ones_r[:, :], ones[:, :]).then_inc(ones_ready, 1)
                dve.wait_ge(table_t, START + 1)
                nc.vector.tensor_copy(k.cols[:, :], small[0][:, 0:V_ROWS]).then_inc(table_used, 1)
                for s in range(CH):
                    dve.wait_ge(prod[s], START + 1)
                    nc.vector.tensor_copy(row[0:1, s * RG:(s + 1) * RG], acc[s][0:1, :]).then_inc(row_ready, 1)
                dve.wait_ge(mod_t, START + 1)
                dve.wait_ge(table_used, START + 1)
                n = NOW * DT
                nc.vector.tensor_add(k.mod[:, 0:n], small[1][:, 0:n], k.cols[:, V_BADA:V_BADA + n]).then_inc(mod_ready, 1)
                dve.wait_ge(mod_ready, START + 1)
                nc.vector.scalar_tensor_tensor(k.a_mix[:, :], k.mod[:, DT:2 * DT], 1.0, k.cols[:, V_GMIX:V_GMIX + DT],
                                               ALU.add, ALU.mult).then_inc(mod_ready, 1)


def stage_input_norm(k, x, eps, h_hi, h_lo, stack):
    nc = k.nc
    NS = 2 * TPG
    with ExitStack() as st:
        xs = [k.sbuf(f"x_in{s}", [P, D], stack=st) for s in range(NS)]
        junk = k.sbuf("squares", [P, D], stack=st)
        ssq = k.sbuf("ssq", [P, NS], stack=st)
        rms = k.sbuf("rms", [P, NS], stack=st)
        rstd = k.sbuf("rstd", [P, NS], stack=st)
        h = [k.sbuf(f"h_f32{s}", [P, RG], stack=st) for s in range(2)]
        tr = k.banks("x_t", 4, st)
        x_in = k.sems("n_x_in", NS)
        squared, rms_ready, rstd_ready, x_scaled = (k.sem("n_" + n) for n in ("squared", "rms", "rstd", "scaled"))
        tr_done, h_ready, hi_ready, lo_ready = (k.sem("n_" + n) for n in ("t", "h", "hi", "lo"))
        x_rows = x.rearrange("o (t p) d -> (o t) p d", p=P)

        start_counts(k)
        with nc.Block() as block:
            @block.sync
            def _(sp):
                with sp.Fori(0, NRG // 2) as i:
                    for s in range(NS):
                        sp.wait_ge(tr_done, START + i * 2 * DT)
                        sp.dma_start(xs[s][:, :], x_rows[bass.ds(i * NS + s, 1), :, :].rearrange("o p d -> p (o d)"))\
                          .then_inc(x_in[s], 16)

            @block.scalar
            def _(act):
                with act.Fori(0, NRG // 2) as i:
                    for r in range(2):
                        for s in range(r * TPG, (r + 1) * TPG):
                            act.wait_ge(x_in[s], START + (i + 1) * 16)
                            if s % TPG == 0:
                                act.wait_ge(rstd_ready, START + i * 2 + r)
                            act.wait_ge(squared, START + i * NS + s)
                            nc.scalar.activation(junk[:, :], xs[s][:, :], ACT.Square, accum_out=ssq[:, s:s + 1])\
                              .then_inc(squared, 1)
                        g = slice(r * TPG, (r + 1) * TPG)
                        act.wait_ge(squared, START + i * NS + (r + 1) * TPG)
                        nc.scalar.activation(rms[:, g], ssq[:, g], ACT.Sqrt, bias=eps[:, 0:1], scale=1.0 / D)\
                          .then_inc(rms_ready, 1)
                        for t in range(DT):
                            n = r * DT + t
                            act.wait_ge(tr_done, START + i * 2 * DT + n + 1)
                            act.wait_ge(lo_ready, START + i * 2 * DT + (n - 1 if n >= 2 else 0))
                            nc.scalar.activation(h[n % 2][:, :], tr[n % 4][:, :], ACT.Identity,
                                                 bias=k.mod[:, t:t + 1], scale=k.a_mix[:, t:t + 1]).then_inc(h_ready, 1)

            @block.tensor
            def _(pe):
                with pe.Fori(0, NRG // 2) as i:
                    for r in range(2):
                        pe.wait_ge(x_scaled, START + i * NS + (r + 1) * TPG)
                        for t in range(DT):
                            n = r * DT + t
                            pe.wait_ge(h_ready, START + i * 2 * DT + (n - 3 if n >= 4 else 0))
                            for q in range(TPG):
                                last = nc.tensor.transpose(tr[n % 4][:, q * P:(q + 1) * P],
                                                           xs[r * TPG + q][:, t * P:(t + 1) * P], k.ident[:, :])
                            last.then_inc(tr_done, 1)

            @block.vector
            def _(dve):
                with dve.Fori(0, NRG // 2) as i:
                    for r in range(2):
                        g = slice(r * TPG, (r + 1) * TPG)
                        dve.wait_ge(rms_ready, START + i * 2 + r + 1)
                        nc.vector.reciprocal(rstd[:, g], rms[:, g]).then_inc(rstd_ready, 1)
                        dve.wait_ge(rstd_ready, START + i * 2 + r + 1)
                        for s in range(r * TPG, (r + 1) * TPG):
                            nc.vector.tensor_scalar(xs[s][:, :], xs[s][:, :], rstd[:, s:s + 1], None, ALU.mult)\
                              .then_inc(x_scaled, 1)
                        rows = bass.ds((i * 2 + r) * RG, RG)
                        for t in range(DT):
                            n = r * DT + t
                            dve.wait_ge(h_ready, START + i * 2 * DT + n + 1)
                            nc.vector.tensor_copy(h_hi[:, t, rows], h[n % 2][:, :]).then_inc(hi_ready, 1)
                            dve.wait_ge(hi_ready, START + i * 2 * DT + n + 1)
                            nc.vector.tensor_sub(h_lo[:, t, rows], h[n % 2][:, :], f32(h_hi[:, t, rows]))\
                              .then_inc(lo_ready, 1)


def split_product(nc, out, w_hi, w_lo, a_hi, a_lo, first, last):
    nc.tensor.matmul(out, w_hi, a_hi, start=first, stop=False)
    nc.tensor.matmul(out, w_hi, a_lo, start=False, stop=False)
    return nc.tensor.matmul(out, w_lo, a_hi, start=False, stop=last)


def stage_projection(k, w_in, b_forget, w_ada, h_hi, h_lo, proj, nf_dram):
    nc = k.nc
    with ExitStack() as st:
        raw = [k.sbuf(f"wp_raw{s}", [P, DT, P], stack=st) for s in range(2)]
        hi = [k.sbuf(f"wp_hi{s}", [P, DT, P], F32R, stack=st) for s in range(2)]
        lo = [k.sbuf(f"wp_lo{s}", [P, DT, P], F32R, stack=st) for s in range(2)]
        f_raw = k.sbuf("wf_raw", [P, DT, HB], stack=st)
        f_hi = k.sbuf("wf_hi", [P, DT, HB], F32R, stack=st)
        f_lo = k.sbuf("wf_lo", [P, DT, HB], F32R, stack=st)
        b_f = k.sbuf("b_f", [HB, 1], stack=st)
        out = [k.sbuf(f"proj_out{s}", [P, S], stack=st) for s in range(2)]
        acc = [k.banks(f"proj_acc{s}_", NRG, st) for s in range(2)]
        logit, soft = out[0][0:HB, :], out[1][0:HB, :]
        one = f32(k.ones_r[0:HB, 0:1]).to_broadcast([HB, S])
        CH = (6 - NOW) * D // (2 * (PT // 2 - 1))
        w_a = [k.sbuf(f"w_ada_late{s}", [P, DT, CH], stack=st) for s in range(2)]
        part = k.sbuf("mod_parts", [P, (6 - NOW) * D], stack=st)
        a_ld, a_used, a_col, a_mod = k.sems("p_ada_in", 2), k.sem("p_ada_used"), k.sem("p_ada_col"), k.sem("p_ada_mod")
        a_view = w_ada.rearrange("o (p t) n -> p (o t) n", t=DT)
        f_in, f_split, f_acc, f_chain = (k.sem("p_" + n) for n in ("f_in", "f_split", "f_acc", "f_chain"))
        f_dve, f_saved = k.sem("p_f_dve"), k.sem("p_f_saved")
        w_ld, w_hi, w_lo = k.sems("p_w_in", 2), k.sems("p_w_hi", 2), k.sems("p_w_lo", 2)
        done, copied, saved = k.sems("p_done", 2), k.sems("p_copied", 2), k.sems("p_saved", 2)
        w_view = w_in.rearrange("o (t p) n -> p (o t) n", p=P)

        start_counts(k)
        with nc.Block() as block:
            @block.sync
            def _(sp):
                with nc.allow_non_contiguous_dma(reason="eight columns of forget gates"):
                    sp.dma_start(f_raw[:, :, :], w_view[:, :, FG0:IN_COLS]).then_inc(f_in, 16)
                    sp.dma_start(b_f[:, :], b_forget.rearrange("o h -> h o")).then_inc(f_in, 16)

                def loads(i, more):
                    for s in range(2):
                        sp.wait_ge(w_lo[s], START + i)
                        sp.dma_start(raw[s][:, :, :], w_view[:, :, bass.ds((i * 2 + s) * P, P)]).then_inc(w_ld[s], 16)
                        if more:
                            sp.wait_ge(a_used, START + (i * 2 + s - 1) * DT)
                            sp.dma_start(w_a[s][:, :, :], a_view[:, :, bass.ds(NOW * D + (i * 2 + s) * CH, CH)])\
                              .then_inc(a_ld[s], 16)

                with sp.Fori(0, PT // 2 - 1) as i:
                    loads(i, True)
                loads(PT // 2 - 1, False)

            @block.tensor
            def _(pe):
                pe.wait_ge(f_split, START + 2)
                for r in range(NRG):
                    for t in range(DT):
                        a = slice(r * RG, (r + 1) * RG)
                        last = split_product(nc, acc[1][r][0:HB, :], f_hi[:, t, :], f_lo[:, t, :],
                                             h_hi[:, t, a], h_lo[:, t, a], t == 0, t == DT - 1)
                    last.then_inc(f_acc, 1)
                with pe.Fori(0, PT // 2) as i:
                    for s in range(2):
                        pe.wait_ge(w_lo[s], START + i + 1)
                        if s == 1:
                            pe.wait_ge(f_chain, START + NRG)
                        pe.wait_ge(copied[s], START + i * NRG)
                        for r in range(NRG):
                            a = slice(r * RG, (r + 1) * RG)
                            for t in range(DT):
                                last = split_product(nc, acc[s][r][:, :], hi[s][:, t, :], lo[s][:, t, :],
                                                     h_hi[:, t, a], h_lo[:, t, a], t == 0, t == DT - 1)
                            last.then_inc(done[s], 1)
                pe.wait_ge(copied[0], START + PT // 2 * NRG)
                pe.wait_ge(a_used, START + 2 * (PT // 2 - 1) * DT)
                for j in range((6 - NOW) * DT):
                    last = nc.tensor.matmul(acc[0][0][:, j:j + 1], part[:, j * P:(j + 1) * P], f32(k.ones_r[:, 0:1]),
                                            start=True, stop=True)
                last.then_inc(a_col, 1)

            @block.scalar
            def _(act):
                act.wait_ge(f_in, START + 32)
                for r in range(NRG):
                    act.wait_ge(f_acc, START + r + 1)
                    nc.scalar.activation(logit[:, r * RG:(r + 1) * RG], acc[1][r][0:HB, :], ACT.Identity,
                                         bias=b_f[:, 0:1]).then_inc(f_chain, 1)
                act.wait_ge(f_chain, START + NRG)
                nc.scalar.activation(soft, logit, ACT.Abs).then_inc(f_chain, 1)
                act.wait_ge(f_chain, START + NRG + 1)
                nc.scalar.activation(soft, soft, ACT.Exp, scale=-1.0).then_inc(f_chain, 1)
                act.wait_ge(f_chain, START + NRG + 2)
                nc.scalar.activation(soft, soft, ACT.Ln, bias=1.0).then_inc(f_chain, 1)
                act.wait_ge(f_dve, START + 3)
                act.dma_start(nf_dram, logit).then_inc(f_saved, 16)
                act.wait_ge(f_saved, START + 16)
                with act.Fori(0, PT // 2) as i:
                    for s in range(2):
                        act.wait_ge(saved[s], START + i * 16)
                        for r in range(NRG):
                            act.wait_ge(done[s], START + i * NRG + r + 1)
                            nc.scalar.activation(out[s][:, r * RG:(r + 1) * RG], acc[s][r][:, :], ACT.Copy)\
                              .then_inc(copied[s], 1)
                        act.wait_ge(copied[s], START + (i + 1) * NRG)
                        act.dma_start(proj[bass.ds((i * 2 + s) * P, P), :], out[s][:, :]).then_inc(saved[s], 16)
                for s in range(2):
                    act.wait_ge(saved[s], START + PT // 2 * 16)

            @block.vector
            def _(dve):
                dve.wait_ge(f_in, START + 32)
                nc.vector.tensor_copy(f_hi[:, :, :], f_raw[:, :, :]).then_inc(f_split, 1)
                dve.wait_ge(f_split, START + 1)
                nc.vector.tensor_sub(f_lo[:, :, :], f_raw[:, :, :], f32(f_hi[:, :, :])).then_inc(f_split, 1)

                def split(i, s):
                    dve.wait_ge(w_ld[s], START + (i + 1) * 16)
                    dve.wait_ge(done[s], START + i * NRG)
                    nc.vector.tensor_copy(hi[s][:, :, :], raw[s][:, :, :]).then_inc(w_hi[s], 1)
                    dve.wait_ge(w_hi[s], START + i + 1)
                    nc.vector.tensor_sub(lo[s][:, :, :], raw[s][:, :, :], f32(hi[s][:, :, :])).then_inc(w_lo[s], 1)

                split(0, 0)
                split(0, 1)
                dve.wait_ge(f_chain, START + NRG + 3)
                nc.vector.scalar_tensor_tensor(soft, logit, 0.0, soft, ALU.min, ALU.subtract).then_inc(f_dve, 1)
                dve.wait_ge(f_dve, START + 1)
                nc.vector.tensor_tensor_scan(logit, one, soft, 0.0, ALU.mult, ALU.add).then_inc(f_dve, 1)
                dve.wait_ge(f_dve, START + 2)
                nc.vector.tensor_scalar(logit, logit, -INV_SCALE, None, ALU.mult).then_inc(f_dve, 1)

                def multiply(i, s):
                    n = i * 2 + s
                    to = part[:, bass.ds(n * CH, CH)]
                    dve.wait_ge(a_ld[s], START + (i + 1) * 16)
                    nc.vector.tensor_scalar(to, w_a[s][:, 0, :], k.c_act[:, 0:1], None, ALU.mult).then_inc(a_used, 1)
                    for t in range(1, DT):
                        dve.wait_ge(a_used, START + n * DT + t)
                        nc.vector.scalar_tensor_tensor(to, w_a[s][:, t, :], k.c_act[:, t:t + 1], to, ALU.mult, ALU.add)\
                          .then_inc(a_used, 1)

                with dve.Fori(1, PT // 2) as i:
                    for s in range(2):
                        split(i, s)
                        multiply(i - 1, s)
                dve.wait_ge(a_col, START + 1)
                n, late = NOW * DT, (6 - NOW) * DT
                nc.vector.tensor_add(k.mod[:, n:n + late], acc[0][0][:, 0:late], k.cols[:, V_BADA + n:V_BADA + n + late])\
                  .then_inc(a_mod, 1)
                dve.wait_ge(a_mod, START + 1)
                nc.vector.scalar_tensor_tensor(k.a_ffn[:, :], k.mod[:, 4 * DT:5 * DT], 1.0, k.cols[:, V_GFFN:V_GFFN + DT],
                                               ALU.add, ALU.mult).then_inc(a_mod, 1)


def stage_attention_b(k, proj, nf_dram, mask_in, y):
    nc = k.nc
    NP = HB // 2
    units = [(hh, g) for hh in range(2) for g in (3, 2, 1, 0)]
    NU, UH = len(units), len(units) // 2
    n_tiles = [TPG * (g + 1) for _, g in units]
    K0 = [sum(n_tiles[:u]) for u in range(NU + 1)]
    NK, NT = K0[-1], NU * TPG
    SB, TB, PS = 3, 3, 4
    PIECES = 6
    with ExitStack() as st:
        qk_in = k.sbuf("bqk_in", [P, S], stack=st)
        v_in = k.sbuf("bv_in", [HD, S], stack=st)
        q_st = [k.sbuf(f"bq{s}", [P, S], F32R, stack=st) for s in range(2)]
        k_hi = [k.sbuf(f"bk_hi{s}", [P, S], F32R, stack=st) for s in range(2)]
        k_lo = [k.sbuf(f"bk_lo{s}", [P, S], F32R, stack=st) for s in range(2)]
        v_st = [k.sbuf(f"bv{s}", [P, RT, P], F32R, stack=st) for s in range(2)]
        nf = [k.sbuf(f"b_nf{s}", [P, S], stack=st) for s in range(2)]
        pf = [k.sbuf(f"b_pf{s}", [P, RT], stack=st) for s in range(2)]
        bias = [k.sbuf(f"b_bias{s}", [P, S], stack=st) for s in range(2)]
        mask = k.sbuf("b_mask", [P, P], stack=st)
        prob = [[k.sbuf(f"b_p{s}_{t}", [P, S], stack=st) for t in range(TPG)] for s in range(2)]
        mx = k.sbuf("b_mx", [P, TPG], stack=st)
        m8 = k.sbuf("b_m8", [P, 2], stack=st)
        neg_m = k.sbuf("b_neg_m", [P, 2], stack=st)
        den = k.sbuf("b_den", [P, 2, TPG], stack=st)
        rden = k.sbuf("b_rden", [P, TPG], stack=st)
        pt_hi = [k.sbuf(f"b_pt_hi{s}", [P, RG], F32R, stack=st) for s in range(PS)]
        pt_lo = [k.sbuf(f"b_pt_lo{s}", [P, RG], F32R, stack=st) for s in range(PS)]
        ot = k.sbuf("b_ot", [P, RG], stack=st)
        y_half = k.sbuf("b_y_half", [P, TPG, HD], stack=st)
        y_sum = k.sbuf("b_y_sum", [P, TPG, HD], stack=st)
        y_out = k.sbuf("b_y_out", [P, RT, 2 * HD], stack=st)
        sc = k.banks("b_sc", SB, st)
        tp = k.banks("b_tp", TB, st)
        oacc = k.banks("b_oacc", 1, st)[0]
        yt = k.banks("b_yt", 1, st)[0]
        vt = yt
        names = ("mask_in", "sc_done", "sc_used", "bias_row", "bias_ready", "mx", "neg_m", "exp", "tp_done",
                 "hi_ready", "lo_ready", "o_done", "ot_ready", "yt_done", "half", "ysum", "y_ready", "rden")
        (mask_ld, sc_done, sc_used, bias_row, bias_ready, mx_ready, neg_ready, exp_done, tp_done, hi_ready, lo_ready,
         o_done, ot_ready, yt_done, half_ready, sum_ready, y_ready, rden_ready) = (k.sem("b_" + n) for n in names)
        y_saved = k.sem("b_y_saved")
        passed = k.sems("b_passed", 3)
        nf_ld = k.sems("b_nf_in", 2)
        names = ("qk_in", "v_in", "qk_hi", "qk_ready", "pf", "vt_done", "v_hi", "v_lo")
        qk_ld, v_ld, qk_hi, qk_ready, pf_ready, vt_done, v_hi, v_lo = (k.sem("b_" + n) for n in names)

        def tiles_to(u):
            return K0[u + 1] if u >= 0 else K0[u + 1 + NU] - NK

        def turn(i, prepare, step, end):
            for u in range(NU):
                for m in range(n_tiles[u]):
                    step(i, u, m)
                    if u % UH == 1 and 1 <= m < 1 + PIECES:
                        hh = 1 - u // UH
                        prepare(i * 2 + (1 if hh else 2), hh, m - 1, i * NK + (0 if hh else K0[UH]),
                                i * NT + (0 if hh else UH * TPG), i + (1 if hh else 2), i * NU + (0 if hh else UH))
            end(i)

        def share(u, m):
            if not u:
                return range(0)
            lag = 1 if n_tiles[u] == TPG else 2
            n, of = n_tiles[u - 1], n_tiles[u] - lag
            return range(max(0, m - lag) * n // of, max(0, m + 1 - lag) * n // of)

        start_counts(k)
        with nc.Block() as block:
            @block.sync
            def _(sp):
                def load(h, m, hh, biases):
                    for n, row in enumerate((KB0, QB0)):
                        sp.wait_ge(qk_ready, START + m * 2 + n)
                        for half in range(2):
                            sp.dma_start(qk_in[half * HD:(half + 1) * HD, :], proj[bass.ds(row + h * HD, HD), :])\
                              .then_inc(qk_ld, 16)
                    sp.wait_ge(vt_done, START + m * 2)
                    sp.dma_start(v_in[:, :], proj[bass.ds(VB0 + h * HD, HD), :]).then_inc(v_ld, 16)
                    sp.wait_ge(bias_ready, START + biases)
                    sp.dma_start(nf[hh][:, :], nf_dram[bass.ds(h, 1), :].to_broadcast([P, S])).then_inc(nf_ld[hh], 16)

                sp.dma_start(mask[:, :], mask_in).then_inc(mask_ld, 16)
                load(0, 0, 0, 0)
                with sp.Fori(0, NP) as i:
                    load(i * 2 + 1, i * 2 + 1, 1, i * NT)
                    load((i * 2 + 2) % HB, i * 2 + 2, 0, i * NT + UH * TPG)

            @block.gpsimd
            def _(pool):
                pool.wait_ge(mask_ld, START + 16)
                with pool.Fori(0, NP) as i:
                    for u, (hh, g) in enumerate(units):
                        if u % UH == 0:
                            pool.wait_ge(nf_ld[hh], START + (i + 1) * 16)
                            pool.wait_ge(pf_ready, START + i * 2 + hh + 1)
                        for t in range(TPG):
                            n, q = u * TPG + t, g * TPG + t
                            ub, tb = (n - 2) // TPG, (n - 2) % TPG
                            c = tiles_to(ub - 1) + (tb + 1) * (units[ub][1] + 1)
                            wait_apart(pool, passed[0], sc_used, START + i * NK + c)
                            b = bias[n % 2]
                            nc.gpsimd.tensor_scalar(b[:, 0:(q + 1) * P], nf[hh][:, 0:(q + 1) * P], 1.0, pf[hh][:, q:q + 1],
                                                    ALU.mult, ALU.add).then_inc(bias_row, 1)
                            pool.wait_ge(bias_row, START + i * NT + n + 1)
                            nc.gpsimd.tensor_tensor(b[:, q * P:(q + 1) * P], b[:, q * P:(q + 1) * P], mask[:, :], ALU.add)\
                              .then_inc(bias_ready, 1)

            @block.tensor
            def _(pe):
                def prepare(m, hh, piece, tiles, biases, loads, outputs):
                    b = piece - 2 if piece in (2, 3) else -1
                    """v of the m-th head as rows, eight key tiles."""
                    if b < 0:
                        return
                    pe.wait_ge(v_ld, START + (m + 1) * 16)
                    pe.wait_ge(sum_ready, START + outputs)
                    wait_apart(pe, passed[2], v_lo, START + m * 2 + b)
                    for j in range(8):
                        last = nc.tensor.transpose(vt[:, j * HD:(j + 1) * HD], v_in[:, (b * 8 + j) * P:(b * 8 + j + 1) * P],
                                                   k.ident[0:HD, 0:HD])
                    last.then_inc(vt_done, 1)

                def scores(i, u, m):
                    hh, g = units[u]
                    t, c = m // (g + 1), m % (g + 1)
                    q, n = g * TPG + t, K0[u] + m
                    if u % UH == 0 and m == 0:
                        pe.wait_ge(qk_ready, START + i * 4 + hh * 2 + 2)
                    w = RG if c < g else (t + 1) * P
                    pe.wait_ge(sc_used, START + i * NK + (n - SB + 1 if n >= SB else 0))
                    a, b = slice(q * P, (q + 1) * P), slice(c * RG, c * RG + w)
                    nc.tensor.matmul(sc[n % SB][:, 0:w], q_st[hh][:, a], k_hi[hh][:, b], start=True, stop=False)
                    nc.tensor.matmul(sc[n % SB][:, 0:w], q_st[hh][:, a], k_lo[hh][:, b], start=False, stop=True)\
                      .then_inc(sc_done, 1)

                def transposes(i, u, j):
                    g, n = units[u][1], K0[u] + j
                    if j == 0:
                        pe.wait_ge(exp_done, START + i * NT + (u + 1) * TPG)
                    pe.wait_ge(lo_ready, START + i * NK + n - TB + 1)
                    for t in range(max(0, j - g * TPG), TPG):
                        last = nc.tensor.transpose(tp[n % TB][:, t * P:(t + 1) * P],
                                                   prob[u % 2][t][:, j * P:(j + 1) * P], k.ident[:, :])
                    last.then_inc(tp_done, 1)

                def products(i, u, j):
                    hh, g = units[u]
                    n = K0[u] + j
                    c0 = max(0, j - g * TPG) * P
                    if j == 0:
                        pe.wait_ge(ot_ready, START + i * NU + u)
                        if u % UH == 0:
                            pe.wait_ge(v_lo, START + i * 4 + hh * 2 + 2)
                    pe.wait_ge(lo_ready, START + i * NK + n + 1)
                    nc.tensor.matmul(oacc[:, c0:RG], v_st[hh][:, j, :], pt_hi[n % PS][:, c0:RG], start=(j == 0), stop=False)
                    nc.tensor.matmul(oacc[:, c0:RG], v_st[hh][:, j, :], pt_lo[n % PS][:, c0:RG],
                                     start=False, stop=(j == n_tiles[u] - 1)).then_inc(o_done, 1)

                def finish(i, u):
                    pe.wait_ge(ot_ready, START + i * NU + u + 1)
                    pe.wait_ge(sum_ready, START + i * NU + u)
                    pe.wait_ge(v_lo, START + i * 4 + (4 if u < UH else 6))
                    for t in range(TPG):
                        last = nc.tensor.transpose(yt[:, t * P:(t + 1) * P], ot[:, t * P:(t + 1) * P], k.ident[:, :])
                    last.then_inc(yt_done, 1)

                waiting = []

                def part(i, u, js):
                    for j in js:
                        transposes(i, u, j)
                        waiting.append((u, j))
                        if len(waiting) > 2:
                            products(i, *waiting.pop(0))
                    if not js and waiting:
                        products(i, *waiting.pop(0))

                def step(i, u, m):
                    if u == 0 and m == 0:
                        scores(i, u, m)
                    if m + 1 < n_tiles[u]:
                        scores(i, u, m + 1)
                    elif u + 1 < NU:
                        scores(i, u + 1, 0)
                    if m == 3 and u >= 2:
                        finish(i, u - 2)
                    part(i, u - 1, share(u, m))

                def end(i):
                    part(i, NU - 1, range(n_tiles[NU - 1]))
                    while waiting:
                        part(i, NU - 1, ())
                    finish(i, NU - 2)
                    finish(i, NU - 1)

                for piece in range(PIECES):
                    prepare(0, 0, piece, 0, 0, 1, 0)
                with pe.Fori(0, NP) as i:
                    turn(i, prepare, step, end)

            @block.scalar
            def _(act):
                def prepare(m, hh, piece, tiles, biases, loads, outputs):
                    b = piece - 2 if piece in (2, 3) else -1
                    if b < 0:
                        return
                    act.wait_ge(vt_done, START + m * 2 + b + 1)
                    act.wait_ge(o_done, START + tiles)
                    nc.scalar.activation(v_st[hh][:, b * 8:(b + 1) * 8, 0:HD],
                                         vt[:, :].rearrange("p (j d) -> p j d", d=HD), ACT.Copy).then_inc(v_hi, 1)

                def exps(i, n):
                    u, t = n // TPG, n % TPG
                    w = (units[u][1] * TPG + t + 1) * P
                    if t == 0:
                        act.wait_ge(rden_ready, START + i * NU + u - 1)
                    act.wait_ge(neg_ready, START + i * NT + n + 1)
                    nc.scalar.activation(prob[u % 2][t][:, 0:w], prob[u % 2][t][:, 0:w], ACT.Exp,
                                         bias=neg_m[:, n % 2:n % 2 + 1], scale=SCALE,
                                         accum_out=den[:, u % 2, t:t + 1]).then_inc(exp_done, 1)

                def part(i, u, js):
                    g = units[u][1]
                    for j in js:
                        n = K0[u] + j
                        c0 = max(0, j - g * TPG) * P
                        act.wait_ge(tp_done, START + i * NK + n + 1)
                        act.wait_ge(o_done, START + i * NK + n - PS + 1)
                        nc.scalar.activation(pt_hi[n % PS][:, c0:RG], tp[n % TB][:, c0:RG], ACT.Copy).then_inc(hi_ready, 1)

                def copy_out(i, u):
                    act.wait_ge(o_done, START + i * NK + K0[u + 1])
                    act.wait_ge(yt_done, START + i * NU + u)
                    nc.scalar.activation(ot[:, :], oacc[:, :], ACT.Copy).then_inc(ot_ready, 1)

                def finish(i, u):
                    act.wait_ge(yt_done, START + i * NU + u + 1)
                    act.wait_ge(sum_ready, START + i * NU + u)
                    nc.scalar.activation(y_half[:, :, :], yt[:, :].rearrange("p (t c) -> p t c", c=P)[:, :, HD:P],
                                         ACT.Copy).then_inc(half_ready, 1)

                def step(i, u, m):
                    t, c = m // (units[u][1] + 1), m % (units[u][1] + 1)
                    if m == 2 and u >= 2:
                        copy_out(i, u - 2)
                    part(i, u - 1, share(u, m))
                    if c == 0 and (u or t):
                        exps(i, u * TPG + t - 1)
                    if m == 3 and u >= 2:
                        finish(i, u - 2)

                def end(i):
                    exps(i, NT - 1)
                    part(i, NU - 1, range(2))
                    copy_out(i, NU - 2)
                    part(i, NU - 1, range(2, n_tiles[NU - 1]))
                    finish(i, NU - 2)
                    copy_out(i, NU - 1)
                    finish(i, NU - 1)
                    act.wait_ge(y_ready, START + (i + 1) * NU)
                    act.dma_start(y[:, bass.ds(WA + i * P, P)].rearrange("(t p) c -> p t c", p=P), y_out[:, :, :])\
                       .then_inc(y_saved, 16)

                for piece in range(PIECES):
                    prepare(0, 0, piece, 0, 0, 1, 0)
                with act.Fori(0, NP) as i:
                    turn(i, prepare, step, end)
                act.wait_ge(y_saved, START + NP * 16)

            @block.vector
            def _(dve):
                def prepare(m, hh, piece, tiles, biases, loads, outputs):
                    b = piece - 2 if piece in (2, 3) else -1
                    if piece == 0:
                        dve.wait_ge(qk_ld, START + m * 64 + 32)
                        dve.wait_ge(sc_done, START + tiles)
                        nc.vector.tensor_copy(k_hi[hh][:, :], qk_in[:, :]).then_inc(qk_hi, 1)
                    if piece == 1:
                        dve.wait_ge(qk_hi, START + m * 2 + 1)
                        nc.vector.tensor_sub(k_lo[hh][:, :], qk_in[:, :], f32(k_hi[hh][:, :])).then_inc(qk_ready, 1)
                    if piece == 4:
                        dve.wait_ge(qk_ld, START + m * 64 + 64)
                        nc.vector.tensor_copy(q_st[hh][:, :], qk_in[:, :]).then_inc(qk_hi, 1)
                    if piece == 5:
                        dve.wait_ge(qk_hi, START + m * 2 + 2)
                        nc.vector.tensor_sub(q_st[hh][HD:P, :], qk_in[HD:P, :], f32(q_st[hh][HD:P, :])).then_inc(qk_ready, 1)
                        dve.wait_ge(nf_ld[hh], START + loads * 16)
                        dve.wait_ge(bias_ready, START + biases)
                        nc.vector.tensor_scalar(pf[hh][:, :], nf[hh][:, :].rearrange("p (t c) -> p t c", c=P)[:, :, 0],
                                                -1.0, None, ALU.mult).then_inc(pf_ready, 1)
                    if b >= 0:
                        dve.wait_ge(v_hi, START + m * 2 + b + 1)
                        v = v_st[hh][:, b * 8:(b + 1) * 8, :]
                        nc.vector.tensor_sub(v[:, :, HD:P], vt[:, :].rearrange("p (j d) -> p j d", d=HD),
                                             f32(v[:, :, 0:HD])).then_inc(v_lo, 1)

                def logits(i, u, m):
                    g = units[u][1]
                    t, c = m // (g + 1), m % (g + 1)
                    n, x = u * TPG + t, K0[u] + m
                    if c == 0:
                        dve.wait_ge(bias_ready, START + i * NT + n + 1)
                    if m == 0:
                        dve.wait_ge(tp_done, START + i * NK + tiles_to(u - 2))
                    w = RG if c < g else (t + 1) * P
                    cols = slice(c * RG, c * RG + w)
                    wait_apart(dve, passed[1], sc_done, START + i * NK + x + 1)
                    nc.vector.tensor_tensor_reduce(out=prob[u % 2][t][:, cols], in0=sc[x % SB][:, 0:w],
                                                   in1=bias[n % 2][:, cols], scale=1.0, scalar=INV_SCALE * NEG,
                                                   op0=ALU.add, op1=ALU.max, accum_out=mx[:, c:c + 1]).then_inc(sc_used, 1)
                    if c == g:
                        dve.wait_ge(sc_used, START + i * NK + x + 1)
                        nc.vector.reduce_max(m8[:, n % 2:n % 2 + 1], mx[:, 0:g + 1], AXX).then_inc(mx_ready, 1)
                        dve.wait_ge(mx_ready, START + i * NT + n + 1)
                        dve.wait_ge(exp_done, START + i * NT + n - 1)
                        nc.vector.tensor_scalar(neg_m[:, n % 2:n % 2 + 1], m8[:, n % 2:n % 2 + 1], -SCALE, None,
                                                ALU.mult).then_inc(neg_ready, 1)

                def part(i, u, js):
                    g = units[u][1]
                    for j in js:
                        n = K0[u] + j
                        c0 = max(0, j - g * TPG) * P
                        dve.wait_ge(hi_ready, START + i * NK + n + 1)
                        nc.vector.tensor_sub(pt_lo[n % PS][:, c0:RG], tp[n % TB][:, c0:RG], f32(pt_hi[n % PS][:, c0:RG]))\
                          .then_inc(lo_ready, 1)

                def inverse(i, u):
                    dve.wait_ge(exp_done, START + i * NT + (u + 1) * TPG)
                    dve.wait_ge(y_ready, START + i * NU + u)
                    nc.vector.reciprocal(rden[:, :], den[:, u % 2, :]).then_inc(rden_ready, 1)

                def finish(i, u):
                    hh, g = units[u]
                    dve.wait_ge(half_ready, START + i * NU + u + 1)
                    nc.vector.tensor_add(y_sum[:, :, :], yt[:, :].rearrange("p (t c) -> p t c", c=P)[:, :, 0:HD],
                                         y_half[:, :, :]).then_inc(sum_ready, 1)
                    dve.wait_ge(sum_ready, START + i * NU + u + 1)
                    dve.wait_ge(rden_ready, START + i * NU + u + 1)
                    if u == 0:
                        dve.wait_ge(y_saved, START + i * 16)
                    nc.vector.tensor_tensor(y_out[:, g * TPG:(g + 1) * TPG, hh * HD:(hh + 1) * HD], y_sum[:, :, :],
                                            rden[:, :].unsqueeze(2).to_broadcast([P, TPG, HD]), ALU.mult)\
                      .then_inc(y_ready, 1)

                waiting = []

                def step(i, u, m):
                    if m == 0 and u >= 2:
                        inverse(i, u - 2)
                    js = share(u, m)
                    while waiting:
                        part(i, *waiting.pop(0))
                    logits(i, u, m)
                    part(i, u - 1, js[:-1])
                    waiting.append((u - 1, js[-1:]))
                    if m == 3 and u >= 2:
                        finish(i, u - 2)

                def end(i):
                    inverse(i, NU - 2)
                    while waiting:
                        part(i, *waiting.pop(0))
                    part(i, NU - 1, range(n_tiles[NU - 1]))
                    finish(i, NU - 2)
                    inverse(i, NU - 1)
                    finish(i, NU - 1)

                for piece in range(PIECES):
                    prepare(0, 0, piece, 0, 0, 1, 0)
                with dve.Fori(0, NP) as i:
                    turn(i, prepare, step, end)


def stage_attention_a(k, proj, band_in, sinks, y):
    nc = k.nc
    NC, NL = 8, 4
    with ExitStack() as st:
        q_in = k.sbuf("aq_in", [P, GA, S], stack=st)
        q_st = k.sbuf("aq", [P, GA, S], F32R, stack=st)
        k_in = k.sbuf("ak_in", [P, S], stack=st)
        k_hi = k.sbuf("ak_hi", [P, S], F32R, stack=st)
        k_lo = k.sbuf("ak_lo", [P, S], F32R, stack=st)
        v_in = k.sbuf("av_in", [HD, S], stack=st)
        v_st = k.sbuf("av", [P, RT, P], F32R, stack=st)
        band = k.sbuf("a_band", [P, GA, BAND], stack=st)
        sink = k.sbuf("a_sink", [P, GA], stack=st)
        prob = [k.sbuf(f"a_p{s}", [P, GA, 2 * P], stack=st) for s in range(2)]
        mx, m, neg_m, sink_m, sink_e, den, den_all = (k.sbuf("a_" + n, [P, 2, GA], stack=st) for n in
                                                      ("mx", "m", "neg_m", "sink_m", "sink_e", "den", "den_all"))
        rden = k.sbuf("a_rden", [P, 4, GA], stack=st)
        pt_hi = [k.sbuf(f"a_pt_hi{s}", [P, RG], F32R, stack=st) for s in range(4)]
        pt_lo = [k.sbuf(f"a_pt_lo{s}", [P, RG], F32R, stack=st) for s in range(4)]
        ot = [k.sbuf(f"a_ot{s}", [P, RG], stack=st) for s in range(2)]
        y_half = k.sbuf("a_y_half", [P, GA, HD], stack=st)
        y_sum = k.sbuf("a_y_sum", [P, GA, HD], stack=st)
        y_out = [k.sbuf(f"a_y_out{s}", [P, GA, HD], stack=st) for s in range(2)]
        sc = [st.enter_context(nc.psum_tensor(f"a_sc{s}", [P, GA, 2 * P], F32)) for s in range(2)]
        tp = k.banks("a_tp", 2, st)
        oacc = k.banks("a_oacc", 1, st)[0]
        yt = k.banks("a_yt", 1, st)[0]
        vt = tp
        qk_ld = k.sems("a_qk_in", NL)
        v_ld, band_ld, qk_hi, qk_ready = (k.sem("a_" + n) for n in ("v_in", "band_in", "qk_hi", "qk_ready"))
        vt_done, v_hi, v_lo, zeroed = (k.sem("a_" + n) for n in ("vt_done", "v_hi", "v_lo", "zeroed"))
        names = ("sc_done", "logits", "mx", "m", "neg_m", "exp", "sink_e", "den", "rden", "tp_done",
                 "hi_ready", "lo_ready", "o_done", "ot_ready", "yt_done", "half", "ysum", "y_ready")
        (sc_done, logits, mx_ready, m_ready, neg_ready, exp_done, sink_done, den_ready, rden_ready, tp_done,
         hi_ready, lo_ready, o_done, ot_ready, yt_done, half_ready, sum_ready, y_ready) = (k.sem("a_" + n) for n in names)
        y_saved = k.sems("a_y_saved", 2)
        k_split, passed, pool_passed = k.sem("a_k_split"), k.sem("a_passed"), k.sem("a_pool_passed")
        tiles = [(j, a) for j in range(RT) for a in ((1,) if j == 0 else (0, 1))]
        T0 = [sum(1 for x, _ in tiles if x < j) for j in range(RT + 1)]
        NK = T0[-1]
        mine = lambda j: [(n, a) for n, (x, a) in enumerate(tiles) if x == j]
        unit = lambda j: 0 <= j < RT

        start_counts(k)
        with nc.Block() as block:
            def load_qkv(sp, i):
                sp.wait_ge(qk_ready, START + i * NC)
                for c in range(NL):
                    cols = slice(c * S // NL, (c + 1) * S // NL)
                    for half in range(2):
                        rows = slice(half * HD, (half + 1) * HD)
                        sp.dma_start(k_in[rows, cols], proj[bass.ds(KA0 + i * HD, HD), cols]).then_inc(qk_ld[c], 16)
                        sp.dma_start(q_in[rows, :, cols], proj[bass.ds(QA0 + i * GA * HD, GA * HD), cols]
                                     .rearrange("(g d) s -> d g s", d=HD)).then_inc(qk_ld[c], 16)
                    if c == 0:
                        sp.wait_ge(vt_done, START + i * 2)
                        sp.dma_start(v_in[:, :], proj[bass.ds(VA0 + i * HD, HD), :]).then_inc(v_ld, 16)

            def load_band(sp, i):
                sp.wait_ge(logits, START + i * RT)
                sp.wait_ge(sink_done, START + i * RT)
                sp.dma_start(band[:, :, :], band_in[bass.ds(i, 1), :, :, :].rearrange("o p g c -> p (o g) c"))\
                  .then_inc(band_ld, 16)
                sp.dma_start(sink[:, :], sinks[:, bass.ds(i * GA, GA)].to_broadcast([P, GA])).then_inc(band_ld, 16)

            def store(sp, i, j):
                sp.wait_ge(y_ready, START + i * RT + j + 1)
                sp.dma_start(y[j * P:(j + 1) * P, bass.ds(i * GA * HD, GA * HD)],
                             y_out[j % 2][:, :, :].rearrange("p g d -> p (g d)")).then_inc(y_saved[j % 2], 16)

            @block.sync
            def _(sp):
                load_qkv(sp, 0)
                load_band(sp, 0)
                with sp.Fori(0, KVA - 1) as i:
                    for j in range(RT):
                        store(sp, i, j)
                        if j == RT // 2:
                            load_qkv(sp, i + 1)
                        if j == RT - 3:
                            load_band(sp, i + 1)
                for j in range(RT):
                    store(sp, KVA - 1, j)
                for s in range(2):
                    sp.wait_ge(y_saved[s], START + KVA * RT // 2 * 16)

            @block.gpsimd
            def _(pool):
                with pool.Fori(0, KVA) as i:
                    for c in range(NC):
                        keys = slice(c * S // NC, (c + 1) * S // NC)
                        n = i * NC + c + 1
                        pool.wait_ge(qk_ld[c * NL // NC], START + (i + 1) * 64)
                        wait_apart(pool, pool_passed, qk_ready, START + n - 1)
                        wait_apart(pool, pool_passed, sc_done, START + i * RT - RT + min((c + 1) * RT // NC + 1, RT))
                        nc.gpsimd.tensor_copy(k_hi[:, keys], k_in[:, keys]).then_inc(qk_hi, 1)
                        nc.gpsimd.tensor_copy(q_st[:, :, keys], q_in[:, :, keys]).then_inc(qk_hi, 1)
                        wait_apart(pool, pool_passed, qk_hi, START + 2 * n)
                        nc.gpsimd.tensor_tensor(k_lo[:, keys], k_in[:, keys], f32(k_hi[:, keys]), ALU.subtract)\
                          .then_inc(k_split, 1)
                        wait_apart(pool, pool_passed, k_split, START + n)
                        nc.gpsimd.tensor_tensor(q_st[HD:P, :, keys], q_in[HD:P, :, keys], f32(q_st[HD:P, :, keys]),
                                                ALU.subtract).then_inc(qk_ready, 1)

            @block.tensor
            def _(pe):
                with pe.Fori(0, KVA) as i:
                    for b in range(2):
                        pe.wait_ge(v_ld, START + (i + 1) * 16)
                        pe.wait_ge(lo_ready, START + i * NK)
                        wait_apart(pe, passed, v_lo, START + i * 2)
                        for j in range(8):
                            last = nc.tensor.transpose(vt[b][:, j * HD:(j + 1) * HD],
                                                       v_in[:, (b * 8 + j) * P:(b * 8 + j + 1) * P], k.ident[0:HD, 0:HD])
                        last.then_inc(vt_done, 1)

                    def scores(j):
                        pe.wait_ge(qk_ready, START + i * NC + j * NC // RT + 1)
                        pe.wait_ge(logits, START + i * RT + j - 1)
                        c0 = HD if j else P
                        keys = slice((j - 1) * P + c0, (j + 1) * P)
                        for g in range(GA):
                            q = q_st[:, g, j * P:(j + 1) * P]
                            nc.tensor.matmul(sc[j % 2][:, g, c0:], q, k_hi[:, keys], start=True, stop=False)
                            last = nc.tensor.matmul(sc[j % 2][:, g, c0:], q, k_lo[:, keys], start=False, stop=True)
                        last.then_inc(sc_done, 1)

                    def probs_t(j):
                        if j == 0:
                            pe.wait_ge(zeroed, START + 2)
                            pe.wait_ge(v_lo, START + i * 2 + 2)
                        pe.wait_ge(exp_done, START + i * RT + j + 1)
                        for n, a in mine(j):
                            pe.wait_ge(lo_ready, START + i * NK + (n - 1 if n >= 2 else 0))
                            for g in range(GA):
                                last = nc.tensor.transpose(tp[n % 2][:, g * P:(g + 1) * P],
                                                           prob[j % 2][:, g, a * P:(a + 1) * P], k.ident[:, :])
                            last.then_inc(tp_done, 1)

                    def with_v(j):
                        pe.wait_ge(ot_ready, START + i * RT + j)
                        for n, a in mine(j):
                            pe.wait_ge(lo_ready, START + i * NK + n + 1)
                            v = v_st[:, j - 1 + a, :]
                            nc.tensor.matmul(oacc[:, :], v, pt_hi[n % 4][:, :], start=(n == mine(j)[0][0]), stop=False)
                            nc.tensor.matmul(oacc[:, :], v, pt_lo[n % 4][:, :], start=False, stop=(n == mine(j)[-1][0]))\
                              .then_inc(o_done, 1)

                    def out_rows(j):
                        pe.wait_ge(ot_ready, START + i * RT + j + 1)
                        pe.wait_ge(sum_ready, START + i * RT + j)
                        for g in range(GA):
                            last = nc.tensor.transpose(yt[:, g * P:(g + 1) * P], ot[j % 2][:, g * P:(g + 1) * P],
                                                       k.ident[:, :])
                        last.then_inc(yt_done, 1)

                    for j in range(-2, RT + 2):
                        if unit(j):
                            probs_t(j)
                        if unit(j - 2):
                            out_rows(j - 2)
                        if unit(j + 2):
                            scores(j + 2)
                        if unit(j - 1):
                            with_v(j - 1)

            @block.scalar
            def _(act):
                with act.Fori(0, KVA) as i:
                    for b in range(2):
                        act.wait_ge(vt_done, START + i * 2 + b + 1)
                        act.wait_ge(o_done, START + i * NK)
                        nc.scalar.activation(v_st[:, b * 8:(b + 1) * 8, 0:HD],
                                             vt[b][:, :].rearrange("p (j d) -> p j d", d=HD), ACT.Copy).then_inc(v_hi, 1)

                    def exps(j):
                        act.wait_ge(neg_ready, START + i * RT + j + 1)
                        act.wait_ge(den_ready, START + i * RT + j - 1)
                        c0 = HD if j else P
                        for g in range(GA):
                            p = prob[j % 2][:, g, c0:]
                            last = nc.scalar.activation(p, p, ACT.Exp, bias=neg_m[:, j % 2, g:g + 1],
                                                        accum_out=den[:, j % 2, g:g + 1])
                        last.then_inc(exp_done, 1)
                        nc.scalar.activation(sink_e[:, j % 2, :], sink_m[:, j % 2, :], ACT.Exp).then_inc(sink_done, 1)

                    def high_parts(j):
                        for n, _ in mine(j):
                            act.wait_ge(tp_done, START + i * NK + n + 1)
                            act.wait_ge(o_done, START + i * NK + (n - 3 if n >= 4 else 0))
                            nc.scalar.activation(pt_hi[n % 4][:, :], tp[n % 2][:, :], ACT.Copy).then_inc(hi_ready, 1)

                    def out_t(j):
                        act.wait_ge(o_done, START + i * NK + T0[j + 1])
                        act.wait_ge(yt_done, START + i * RT + j - 1)
                        nc.scalar.activation(ot[j % 2][:, :], oacc[:, :], ACT.Copy).then_inc(ot_ready, 1)

                    def half_rows(j):
                        act.wait_ge(yt_done, START + i * RT + j + 1)
                        act.wait_ge(sum_ready, START + i * RT + j)
                        nc.scalar.activation(y_half[:, :, :], yt[:, :].rearrange("p (t c) -> p t c", c=P)[:, :, HD:P],
                                             ACT.Copy).then_inc(half_ready, 1)

                    for j in range(-1, RT + 2):
                        if unit(j):
                            high_parts(j)
                        if unit(j - 2):
                            half_rows(j - 2)
                        if unit(j + 1):
                            exps(j + 1)
                        if unit(j - 1):
                            out_t(j - 1)

            @block.vector
            def _(dve):
                for s in range(2):
                    nc.vector.memset(prob[s][:, :, 0:HD], 0.0).then_inc(zeroed, 1)
                with dve.Fori(0, KVA) as i:
                    for b in range(2):
                        dve.wait_ge(v_hi, START + i * 2 + b + 1)
                        v = v_st[:, b * 8:(b + 1) * 8, :]
                        nc.vector.tensor_sub(v[:, :, HD:P], vt[b][:, :].rearrange("p (j d) -> p j d", d=HD),
                                             f32(v[:, :, 0:HD])).then_inc(v_lo, 1)

                    def maxima(j):
                        s = j % 2
                        c0 = HD if j else P
                        n = i * RT + j + 1
                        dve.wait_ge(sc_done, START + n)
                        if j == 0:
                            dve.wait_ge(band_ld, START + (i + 1) * 32)
                        dve.wait_ge(tp_done, START + i * NK + (T0[j - 1] if j >= 2 else 0))
                        nc.vector.scalar_tensor_tensor(prob[s][:, :, c0:], sc[s][:, :, c0:], SCALE, band[:, :, c0 - HD:],
                                                       ALU.mult, ALU.add).then_inc(logits, 1)
                        dve.wait_ge(logits, START + n)
                        nc.vector.reduce_max(mx[:, s, :], prob[s][:, :, c0:], AXX).then_inc(mx_ready, 1)
                        dve.wait_ge(mx_ready, START + n)
                        nc.vector.tensor_tensor(m[:, s, :], mx[:, s, :], sink[:, :], ALU.max).then_inc(m_ready, 1)
                        dve.wait_ge(m_ready, START + n)
                        dve.wait_ge(sink_done, START + i * RT + j - 1)
                        nc.vector.tensor_sub(sink_m[:, s, :], sink[:, :], m[:, s, :])
                        nc.vector.tensor_scalar(neg_m[:, s, :], m[:, s, :], -1.0, None, ALU.mult).then_inc(neg_ready, 1)

                    def low_parts(j):
                        for n, _ in mine(j):
                            dve.wait_ge(hi_ready, START + i * NK + n + 1)
                            nc.vector.tensor_sub(pt_lo[n % 4][:, :], tp[n % 2][:, :], f32(pt_hi[n % 4][:, :]))\
                              .then_inc(lo_ready, 1)

                    def denominators(j):
                        s = j % 2
                        n = i * RT + j + 1
                        dve.wait_ge(sink_done, START + n)
                        dve.wait_ge(exp_done, START + n)
                        nc.vector.tensor_add(den_all[:, s, :], den[:, s, :], sink_e[:, s, :]).then_inc(den_ready, 1)
                        dve.wait_ge(den_ready, START + n)
                        nc.vector.reciprocal(rden[:, j % 4, :], den_all[:, s, :]).then_inc(rden_ready, 1)

                    def outputs(j):
                        s = j % 2
                        n = i * RT + j + 1
                        dve.wait_ge(half_ready, START + n)
                        dve.wait_ge(y_ready, START + n - 1)
                        nc.vector.tensor_add(y_sum[:, :, :], yt[:, :].rearrange("p (t c) -> p t c", c=P)[:, :, 0:HD],
                                             y_half[:, :, :]).then_inc(sum_ready, 1)
                        dve.wait_ge(sum_ready, START + n)
                        dve.wait_ge(rden_ready, START + n)
                        dve.wait_ge(y_saved[s], START + i * (RT // 2 * 16) + j // 2 * 16)
                        nc.vector.tensor_tensor(y_out[s][:, :, :], y_sum[:, :, :],
                                                rden[:, j % 4, :].unsqueeze(2).to_broadcast([P, GA, HD]), ALU.mult)\
                          .then_inc(y_ready, 1)

                    for j in range(-1, RT + 2):
                        if unit(j + 1):
                            maxima(j + 1)
                        if unit(j):
                            low_parts(j)
                            denominators(j)
                        if unit(j - 2):
                            outputs(j - 2)


def stage_mix_output(k, y, x, w_out, eps, x1_t, h2_t):
    nc = k.nc
    HALF = DT // 2
    with ExitStack() as st:
        w_hi = [k.sbuf(f"wo_hi{o}", [P, DT, P], F32R, stack=st) for o in range(DT)]
        w_lo = [k.sbuf(f"wo_lo{o}", [P, DT, P], F32R, stack=st) for o in range(DT)]
        y_row = [k.sbuf(f"y_row{b}", [P, TPG, D], stack=st) for b in range(2)]
        x_row = k.sbuf("x_row", [P, TPG, D], stack=st)
        y_hi = k.sbuf("y_hi", [P, DT, RG], F32R, stack=st)
        y_lo = k.sbuf("y_lo", [P, DT, RG], F32R, stack=st)
        xt = [k.sbuf(f"x1_{b}", [P, DT, RG], stack=st) for b in range(2)]
        w_raw = [xt[o // HALF][:, 2 * (o % HALF):2 * (o % HALF) + 2, :].rearrange("p a (b c) -> p (a b) c", c=P)
                 for o in range(DT)]
        y_tmp = [k.sbuf(f"y_tmp{s}", [P, RG], stack=st) for s in range(2)]
        sq = [k.sbuf(f"m_sq{s}", [P, RG], stack=st) for s in range(2)]
        sq_hi = [k.sbuf(f"m_sq_hi{s}", [P, RG], F32R, stack=st) for s in range(2)]
        sq_lo = [k.sbuf(f"m_sq_lo{s}", [P, RG], F32R, stack=st) for s in range(2)]
        rms = k.sbuf("m_rms", [P, RG], stack=st)
        rstd = k.sbuf("m_rstd", [P, RG], stack=st)
        ssq, g_rms, g_rstd = (k.sbuf("m_" + n, [P, 2 * TPG], stack=st) for n in ("ssq", "g_rms", "g_rstd"))
        acc = k.banks("m_acc", HALF, st)
        tr = k.banks("m_tr", 2, st)
        total = k.banks("m_total", 1, st)[0]
        junk = k.banks("m_junk", 1, st)[0]
        w_ld = k.sems("m_w_in", DT)
        y_in = k.sems("m_y_in", 2)
        names = ("w_hi", "w_lo", "x_in", "squared", "g_rms", "g_rstd", "scaled", "tr", "copied", "y_hi", "y_lo",
                 "k_done", "acc", "resid", "sq", "sq_hi", "sq_lo", "sum", "rms", "rstd", "xn", "h2")
        S_ = {n: k.sem("m_" + n) for n in names}
        x1_saved, h2_saved = k.sems("m_x1_saved", 2), k.sems("m_h2_saved", 2)
        wo_v = w_out.rearrange("o (t p) n -> p (o t) n", p=P)
        rows_of = lambda v, r: v[bass.ds(r, 1), :, :, :].rearrange("o p t d -> p (o t) d")
        y_v = y.rearrange("(r t p) d -> r p t d", p=P, t=TPG)
        x_v = x.rearrange("o (r t p) d -> (o r) p t d", p=P, t=TPG)
        x1_v, h2_v = (v.rearrange("(t p) n -> p t n", p=P) for v in (x1_t, h2_t))
        TR = 4 * DT
        Y_AT, X_AT = (0, 2 * DT), (DT, 3 * DT)

        start_counts(k)
        with nc.Block() as block:
            def store_x1(act, i, b, half):
                o = slice(half * HALF, (half + 1) * HALF)
                act.wait_ge(S_["resid"], START + (i * 2 + b) * DT + (half + 1) * HALF)
                act.dma_start(x1_v[:, o, bass.ds((i * 2 + b) * RG, RG)], xt[b][:, o, :]).then_inc(x1_saved[b], 16)

            def store_h2(act, i, b):
                act.wait_ge(S_["h2"], START + (i * 2 + b + 1) * DT)
                act.dma_start(h2_v[:, :, bass.ds((i * 2 + b) * RG, RG)], xt[b][:, :, :]).then_inc(h2_saved[b], 16)

            @block.sync
            def _(sp):
                for o in range(DT):
                    sp.dma_start(w_raw[o], wo_v[:, :, o * P:(o + 1) * P]).then_inc(w_ld[o], 16)
                with sp.Fori(0, NRG // 2) as i:
                    for b in range(2):
                        sp.wait_ge(S_["tr"], START + i * TR + Y_AT[b] + DT - TR)
                        sp.dma_start(y_row[b][:, :, :], rows_of(y_v, i * 2 + b)).then_inc(y_in[b], 16)
                    for b in range(2):
                        sp.wait_ge(S_["tr"], START + i * TR + X_AT[b - 1] + DT - (TR if b == 0 else 0))
                        sp.dma_start(x_row[:, :, :], rows_of(x_v, i * 2 + b)).then_inc(S_["x_in"], 16)

            @block.tensor
            def _(pe):
                def transposes(i, n, rows, t):
                    pe.wait_ge(S_["copied"], START + i * TR + n - 1)
                    for q in range(TPG):
                        last = nc.tensor.transpose(tr[n % 2][:, q * P:(q + 1) * P], rows[:, q, t * P:(t + 1) * P],
                                                   k.ident[:, :])
                    last.then_inc(S_["tr"], 1)

                def products(r, half, j):
                    for o in range(HALF):
                        if j == 0:
                            pe.wait_ge(S_["resid"], START + r * DT + (half - 1) * HALF + o + 1)
                        out = half * HALF + o
                        last = split_product(nc, acc[o][:, :], w_hi[out][:, j, :], w_lo[out][:, j, :],
                                             y_hi[:, j, :], y_lo[:, j, :], j == 0, j == DT - 1)
                        if j == DT - 1:
                            last.then_inc(S_["acc"], 1)
                    if j < DT - 1:
                        last.then_inc(S_["k_done"], 1)

                def sums(r, t):
                    pe.wait_ge(S_["sq_lo"], START + r * DT + t + 1)
                    if t == 0:
                        pe.wait_ge(S_["rms"], START + r)
                    nc.tensor.matmul(total[:, :], k.ones_r[:, :], sq_hi[t % 2][:, :], start=(t == 0), stop=False)
                    nc.tensor.matmul(total[:, :], k.ones_r[:, :], sq_lo[t % 2][:, :], start=False, stop=(t == DT - 1))\
                      .then_inc(S_["sum"], 1)

                pe.wait_ge(S_["w_lo"], START + DT)
                with pe.Fori(0, NRG // 2) as i:
                    pe.wait_ge(S_["scaled"], START + (i * 2 + 1) * 2 * TPG)
                    for t in range(DT):
                        transposes(i, Y_AT[0] + t, y_row[0], t)
                    for b in range(2):
                        r = i * 2 + b
                        for j in range(DT):
                            if j == 0:
                                pe.wait_ge(S_["x_in"], START + (r + 1) * 16)
                            transposes(i, X_AT[b] + j, x_row, j)
                            pe.wait_ge(S_["y_lo"], START + r * DT + j + 1)
                            products(r, 0, j)
                            if b == 1 and j > 0:
                                sums(r - 1, j - 1)
                        if b == 1:
                            sums(r - 1, DT - 1)
                        for j in range(DT):
                            products(r, 1, j)
                            if b == 0:
                                if j == 0:
                                    pe.wait_ge(S_["scaled"], START + (r + 2) * 2 * TPG)
                                transposes(i, Y_AT[1] + j, y_row[1], j)
                            elif j >= HALF:
                                sums(r, j - HALF)
                    for t in range(HALF, DT):
                        sums(i * 2 + 1, t)

            @block.scalar
            def _(act):
                def y_squares(i, b, n):
                    r = i * 2 + b
                    if n == 0:
                        act.wait_ge(y_in[b], START + (i + 1) * 16)
                        act.wait_ge(S_["g_rms"], START + r)
                    act.wait_ge(S_["squared"], START + r * 2 * TPG + n)
                    q, a = n // 2, n % 2
                    nc.scalar.activation(junk[:, :], y_row[b][:, q, a * WA:(a + 1) * WA], ACT.Square,
                                         accum_out=ssq[:, n:n + 1]).then_inc(S_["squared"], 1)

                def y_root(r):
                    act.wait_ge(S_["squared"], START + (r + 1) * 2 * TPG)
                    act.wait_ge(S_["g_rstd"], START + r)
                    nc.scalar.activation(g_rms[:, :], ssq[:, :], ACT.Sqrt, bias=eps[:, 0:1], scale=1.0 / WA)\
                      .then_inc(S_["g_rms"], 1)

                def y_copy(i, b, t):
                    n = Y_AT[b] + t
                    act.wait_ge(S_["tr"], START + i * TR + n + 1)
                    act.wait_ge(S_["y_lo"], START + (i * 2 + b) * DT + t - 1)
                    nc.scalar.activation(y_tmp[t % 2][:, :], tr[n % 2][:, :], ACT.Copy,
                                         scale=k.cols[:, V_GGRP + t:V_GGRP + t + 1]).then_inc(S_["copied"], 1)

                def x_copy(i, b, t):
                    n = X_AT[b] + t
                    if t == 0:
                        act.wait_ge(h2_saved[b], START + i * 16)
                    act.wait_ge(S_["tr"], START + i * TR + n + 1)
                    nc.scalar.activation(xt[b][:, t, :], tr[n % 2][:, :], ACT.Copy).then_inc(S_["copied"], 1)

                def square(i, b, t):
                    r = i * 2 + b
                    act.wait_ge(S_["resid"], START + r * DT + t + 1)
                    act.wait_ge(S_["sq_lo"], START + r * DT + t - 1)
                    nc.scalar.activation(sq[t % 2][:, :], xt[b][:, t, :], ACT.Square).then_inc(S_["sq"], 1)

                def root(r):
                    act.wait_ge(S_["sum"], START + (r + 1) * DT)
                    act.wait_ge(S_["rstd"], START + r)
                    nc.scalar.activation(rms[:, :], total[:, :], ACT.Sqrt, bias=eps[:, 0:1], scale=1.0 / D)\
                      .then_inc(S_["rms"], 1)

                def affine(i, b, t):
                    act.wait_ge(S_["xn"], START + (i * 2 + b) * DT + t + 1)
                    nc.scalar.activation(xt[b][:, t, :], xt[b][:, t, :], ACT.Identity,
                                         bias=k.mod[:, 3 * DT + t:3 * DT + t + 1], scale=k.a_ffn[:, t:t + 1])\
                      .then_inc(S_["h2"], 1)

                with act.Fori(0, NRG // 2) as i:
                    for n in range(2 * TPG):
                        y_squares(i, 0, n)
                    y_root(i * 2)
                    for t in range(DT):
                        y_copy(i, 0, t)
                    for t in range(DT):
                        x_copy(i, 0, t)
                        if t < TPG:
                            y_squares(i, 1, 2 * t)
                            y_squares(i, 1, 2 * t + 1)
                        if t == TPG:
                            y_root(i * 2 + 1)
                    for t in range(DT):
                        y_copy(i, 1, t)
                        if t == 1:
                            store_x1(act, i, 0, 0)
                    for t in range(DT):
                        x_copy(i, 1, t)
                        if t == 0:
                            store_x1(act, i, 0, 1)
                        square(i, 0, t)
                    root(i * 2)
                    for t in range(DT):
                        affine(i, 0, t)
                    store_h2(act, i, 0)
                    for t in range(DT):
                        square(i, 1, t)
                        if t == HALF - 1:
                            store_x1(act, i, 1, 0)
                    store_x1(act, i, 1, 1)
                    root(i * 2 + 1)
                    for t in range(DT):
                        affine(i, 1, t)
                    store_h2(act, i, 1)
                for b in range(2):
                    act.wait_ge(x1_saved[b], START + NRG // 2 * 32)
                    act.wait_ge(h2_saved[b], START + NRG // 2 * 16)

            @block.vector
            def _(dve):
                for o in range(DT):
                    dve.wait_ge(w_ld[o], START + 16)
                    nc.vector.tensor_copy(w_hi[o][:, :, :], w_raw[o]).then_inc(S_["w_hi"], 1)
                    dve.wait_ge(S_["w_hi"], START + o + 1)
                    nc.vector.tensor_sub(w_lo[o][:, :, :], w_raw[o], f32(w_hi[o][:, :, :])).then_inc(S_["w_lo"], 1)

                def y_scale(r, b):
                    dve.wait_ge(S_["g_rms"], START + r + 1)
                    nc.vector.reciprocal(g_rstd[:, :], g_rms[:, :]).then_inc(S_["g_rstd"], 1)
                    dve.wait_ge(S_["g_rstd"], START + r + 1)
                    for n in range(2 * TPG):
                        part = y_row[b][:, n // 2, (n % 2) * WA:(n % 2 + 1) * WA]
                        nc.vector.tensor_scalar(part, part, g_rstd[:, n:n + 1], None, ALU.mult).then_inc(S_["scaled"], 1)

                def y_split(i, b, t):
                    r = i * 2 + b
                    dve.wait_ge(S_["copied"], START + i * TR + Y_AT[b] + t + 1)
                    if t < DT - 1:
                        dve.wait_ge(S_["k_done"], START + r * 2 * (DT - 1) - (DT - 1) + t + 1)
                    else:
                        dve.wait_ge(S_["acc"], START + r * DT)
                    nc.vector.tensor_copy(y_hi[:, t, :], y_tmp[t % 2][:, :]).then_inc(S_["y_hi"], 1)
                    dve.wait_ge(S_["y_hi"], START + r * DT + t + 1)
                    nc.vector.tensor_sub(y_lo[:, t, :], y_tmp[t % 2][:, :], f32(y_hi[:, t, :])).then_inc(S_["y_lo"], 1)

                def residual(i, b, half):
                    for t in range(half * HALF, (half + 1) * HALF):
                        if t == half * HALF:
                            dve.wait_ge(S_["copied"], START + i * TR + X_AT[b] + DT)
                        dve.wait_ge(S_["acc"], START + (i * 2 + b) * DT + t + 1)
                        nc.vector.scalar_tensor_tensor(xt[b][:, t, :], acc[t % HALF][:, :],
                                                       k.mod[:, 2 * DT + t:2 * DT + t + 1], xt[b][:, t, :],
                                                       ALU.mult, ALU.add).then_inc(S_["resid"], 1)

                def square_split(r, t):
                    dve.wait_ge(S_["sq"], START + r * DT + t + 1)
                    dve.wait_ge(S_["sum"], START + r * DT + t - 1)
                    nc.vector.tensor_copy(sq_hi[t % 2][:, :], sq[t % 2][:, :]).then_inc(S_["sq_hi"], 1)
                    dve.wait_ge(S_["sq_hi"], START + r * DT + t + 1)
                    nc.vector.tensor_sub(sq_lo[t % 2][:, :], sq[t % 2][:, :], f32(sq_hi[t % 2][:, :]))\
                      .then_inc(S_["sq_lo"], 1)

                def normalise(i, b):
                    r = i * 2 + b
                    dve.wait_ge(S_["rms"], START + r + 1)
                    nc.vector.reciprocal(rstd[:, :], rms[:, :]).then_inc(S_["rstd"], 1)
                    dve.wait_ge(S_["rstd"], START + r + 1)
                    dve.wait_ge(x1_saved[b], START + (i + 1) * 32)
                    for t in range(DT):
                        nc.vector.tensor_tensor(xt[b][:, t, :], xt[b][:, t, :], rstd[:, :], ALU.mult)\
                          .then_inc(S_["xn"], 1)

                with dve.Fori(0, NRG // 2) as i:
                    y_scale(i * 2, 0)
                    for t in range(DT):
                        y_split(i, 0, t)
                    y_scale(i * 2 + 1, 1)
                    residual(i, 0, 0)
                    for t in range(DT):
                        y_split(i, 1, t)
                    residual(i, 0, 1)
                    for t in range(DT):
                        square_split(i * 2, t)
                    residual(i, 1, 0)
                    normalise(i, 0)
                    for t in range(HALF):
                        square_split(i * 2 + 1, t)
                    residual(i, 1, 1)
                    for t in range(HALF, DT):
                        square_split(i * 2 + 1, t)
                    normalise(i, 1)


def stage_ffn(k, x1_t, h2_t, w_gate_up, w_down, g_final, eps, out):
    nc = k.nc
    NSLOT = 4
    DOWN = [(0, 8), (8, 8), (16, FT - 16)]
    NX = 4
    with ExitStack() as st:
        raw = [k.sbuf(f"w_raw{s}", [P, DT, P], stack=st) for s in range(NSLOT)]
        hi = [k.sbuf(f"w_hi{s}", [P, DT, P], F32R, stack=st) for s in range(NSLOT)]
        lo = [k.sbuf(f"w_lo{s}", [P, DT, P], F32R, stack=st) for s in range(NSLOT)]
        act_hi = k.sbuf("act_hi", [P, FT, RG], F32R, stack=st)
        act_lo = k.sbuf("act_lo", [P, FT, RG], F32R, stack=st)
        h_hi = k.sbuf("f_h_hi", [P, DT, RG], F32R, stack=st)
        h_lo = k.sbuf("f_h_lo", [P, DT, RG], F32R, stack=st)
        h_raw = [k.sbuf(f"f_h_raw{s}", [P, RG], stack=st) for s in range(2)]
        x1 = [k.sbuf(f"f_x1_{s}", [P, RG], stack=st) for s in range(NX)]
        tmp = [k.sbuf(f"f_tmp{s}", [P, RG], stack=st) for s in range(2)]
        rows = k.sbuf("f_rows", [P, TPG, D], stack=st)
        h_first = [rows[:, t // 2, t % 2 * RG:(t % 2 + 1) * RG] for t in range(DT)]
        g_fin = k.sbuf("f_g_final", [P, D], stack=st)
        ssq = k.sbuf("f_ssq", [P, 2 * TPG], stack=st)
        mean, rms, rstd = (k.sbuf("f_" + n, [P, TPG], stack=st) for n in ("mean", "rms", "rstd"))
        bank = k.banks("f_bank", 8, st)
        w_ld, w_hi, w_lo, w_used = (k.sems("f_" + n, NSLOT) for n in ("w_in", "w_hi", "w_lo", "w_used"))
        names = ("g_in", "h_hi", "h_lo", "silu", "act_f", "act_hi", "act_lo", "final", "fin_t", "copied",
                 "squared", "ssq", "rms", "rstd", "o_ready", "saved")
        S_ = {n: k.sem("f_" + n) for n in names}
        h_first_in, h_in, x1_in = k.sems("f_h_first_in", DT), k.sems("f_h_in", 2), k.sems("f_x1_in", NX)
        wg_v = w_gate_up.rearrange("o (t p) n -> p (o t) n", p=P)
        wd_v = w_down.rearrange("o (t p) n -> p (o t) n", p=P)
        o_v = out.rearrange("o (r t p) d -> (o r) p t d", p=P, t=TPG)
        N_UP, N_DN = 2 * FT, len(DOWN) * DT
        PER = (N_UP + N_DN) // NSLOT
        DN0 = N_UP // NSLOT

        start_counts(k)
        with nc.Block() as block:
            @block.sync
            def _(sp):
                def load(s, t, dst, src):
                    sp.wait_ge(w_lo[s], START + t)
                    sp.dma_start(dst, src).then_inc(w_ld[s], 16)

                for t in range(DT):
                    sp.dma_start(h_first[t], h2_t[t * P:(t + 1) * P, 0:RG]).then_inc(h_first_in[t], 16)
                with sp.Fori(0, NRG) as r:
                    with sp.Fori(0, FT // 2) as a:
                        for s in range(NSLOT):
                            col = (a * 2 + s // 2) * P + (s % 2) * DFF
                            load(s, r * PER + a, raw[s][:, :, :], wg_v[:, :, bass.ds(col, P)])
                    with sp.Fori(0, DT // 4) as a:
                        for n in range(12):
                            t0, nt = DOWN[n % 3]
                            load(n % NSLOT, r * PER + DN0 + a * 3 + n // NSLOT,
                                 raw[n % NSLOT][:, 0:nt, :], wd_v[:, t0:t0 + nt, bass.ds((a * 4 + n // 3) * P, P)])

            @block.tensor
            def _(pe):
                def product(out_bank, s, t, rhs_hi, rhs_lo, nt, first, last):
                    pe.wait_ge(w_lo[s], START + t + 1)
                    for j in range(nt):
                        x_ = split_product(nc, out_bank, hi[s][:, j, :], lo[s][:, j, :], rhs_hi(j), rhs_lo(j),
                                           first and j == 0, last and j == nt - 1)
                    x_.then_inc(w_used[s], 1)

                def to_rows(r, a, i):
                    pe.wait_ge(S_["final"], START + r * DT + a * 4 + i + 1)
                    pe.wait_ge(S_["copied"], START + r * DT + a * 4 + i - 1)
                    for q in range(TPG):
                        last = nc.tensor.transpose(bank[6 + i % 2][:, q * P:(q + 1) * P], x1[i % NX][:, q * P:(q + 1) * P],
                                                   k.ident[:, :])
                    last.then_inc(S_["fin_t"], 1)

                with pe.Fori(0, NRG) as r:
                    with pe.Fori(0, FT // 2) as a:
                        pe.wait_ge(S_["h_lo"], START + (r + 1) * DT)
                        for n in range(4):
                            if n % 2 == 0:
                                pe.wait_ge(S_["act_f"], START + r * FT + a * 2 + (n // 2 - 1))
                            product(bank[n][:, :], n, r * PER + a,
                                    lambda j: h_hi[:, j, :], lambda j: h_lo[:, j, :], DT, True, True)
                    with pe.Fori(0, DT // 4) as a:
                        pe.wait_ge(S_["act_lo"], START + (r + 1) * FT)
                        for n in range(12):
                            t0, nt = DOWN[n % 3]
                            if n % 3 == 0:
                                pe.wait_ge(S_["final"], START + r * DT + a * 4 + (n // 3 - 1))
                            product(bank[4 + (n // 3) % 2][:, :], n % NSLOT, r * PER + DN0 + a * 3 + n // NSLOT,
                                    lambda j: act_hi[:, t0 + j, :], lambda j: act_lo[:, t0 + j, :], nt,
                                    n % 3 == 0, n % 3 == 2)
                            if n % 3 == 0 and n > 0:
                                to_rows(r, a, n // 3 - 1)
                        to_rows(r, a, 3)

            @block.scalar
            def _(act):
                def load_h(r, t):
                    act.wait_ge(S_["h_lo"], START + r * DT + t - 1)
                    act.dma_start(h_raw[t % 2][:, :], h2_t[t * P:(t + 1) * P, bass.ds(r * RG, RG)]).then_inc(h_in[t % 2], 16)

                def load_x1(r, t):
                    act.dma_start(x1[t % NX][:, :], x1_t[t * P:(t + 1) * P, bass.ds(r * RG, RG)]).then_inc(x1_in[t % NX], 16)

                def group(r, more):
                    with act.Fori(0, FT // 2) as a:
                        for n in range(2):
                            act.wait_ge(w_used[2 * n], START + r * PER + a + 1)
                            act.wait_ge(S_["act_lo"], START + r * FT + a * 2 + n - 1)
                            nc.scalar.activation(tmp[n][:, :], bank[2 * n][:, :], ACT.Silu).then_inc(S_["silu"], 1)
                    for t in range(NX - 1):
                        load_x1(r, t)
                    if more:
                        act.wait_ge(S_["act_lo"], START + (r + 1) * FT)
                        load_h(r + 1, 0)
                        load_h(r + 1, 1)
                    act.wait_ge(S_["saved"], START + r * 16)
                    for t in range(DT):
                        act.wait_ge(S_["fin_t"], START + r * DT + t + 1)
                        nc.scalar.activation(rows[:, :, t * P:(t + 1) * P],
                                             bank[6 + t % 2][:, :].rearrange("p (q c) -> p q c", c=P), ACT.Copy)\
                          .then_inc(S_["copied"], 1)
                        if t + NX - 1 < DT:
                            load_x1(r, t + NX - 1)
                        if more and t + 2 < DT:
                            load_h(r + 1, t + 2)
                    act.wait_ge(S_["copied"], START + (r + 1) * DT)
                    for n in range(2 * TPG):
                        q, half = n // 2, n % 2
                        act.wait_ge(S_["squared"], START + r * 2 * TPG + n)
                        nc.scalar.activation(bank[6][:, :], rows[:, q, half * RG:(half + 1) * RG], ACT.Square,
                                             accum_out=ssq[:, half * TPG + q:half * TPG + q + 1]).then_inc(S_["squared"], 1)
                    act.wait_ge(S_["ssq"], START + r + 1)
                    nc.scalar.activation(rms[:, :], mean[:, :], ACT.Sqrt, bias=eps[:, 0:1], scale=1.0 / D)\
                      .then_inc(S_["rms"], 1)
                    act.wait_ge(S_["o_ready"], START + (r + 1) * TPG)
                    act.dma_start(o_v[bass.ds(r, 1), :, :, :].rearrange("o p t d -> p (o t) d"), rows[:, :, :])\
                       .then_inc(S_["saved"], 16)

                act.wait_ge(w_lo[NSLOT - 1], START + 1)
                act.dma_start(g_fin[:, :], g_final.partition_broadcast(P)).then_inc(S_["g_in"], 16)
                with act.Fori(0, NRG - 1) as r:
                    group(r, True)
                group(NRG - 1, False)
                act.wait_ge(S_["saved"], START + NRG * 16)

            @block.vector
            def _(dve):
                def split(s, t, nt=DT):
                    dve.wait_ge(w_ld[s], START + (t + 1) * 16)
                    dve.wait_ge(w_used[s], START + t)
                    nc.vector.tensor_copy(hi[s][:, 0:nt, :], raw[s][:, 0:nt, :]).then_inc(w_hi[s], 1)
                    dve.wait_ge(w_hi[s], START + t + 1)
                    nc.vector.tensor_sub(lo[s][:, 0:nt, :], raw[s][:, 0:nt, :], f32(hi[s][:, 0:nt, :])).then_inc(w_lo[s], 1)

                def h_split(r, t, h):
                    nc.vector.tensor_copy(h_hi[:, t, :], h).then_inc(S_["h_hi"], 1)
                    dve.wait_ge(S_["h_hi"], START + r * DT + t + 1)
                    nc.vector.tensor_sub(h_lo[:, t, :], h, f32(h_hi[:, t, :])).then_inc(S_["h_lo"], 1)

                def gated(r, a, n):
                    ft = a * 2 + n
                    f = r * FT + ft
                    part = lambda v: v[:, bass.ds(ft, 1), :].rearrange("p o n -> p (o n)")
                    dve.wait_ge(S_["silu"], START + f + 1)
                    dve.wait_ge(w_used[2 * n + 1], START + r * PER + a + 1)
                    nc.vector.tensor_tensor(tmp[n][:, :], bank[2 * n + 1][:, :], tmp[n][:, :], ALU.mult).then_inc(S_["act_f"], 1)
                    dve.wait_ge(S_["act_f"], START + f + 1)
                    nc.vector.tensor_copy(part(act_hi), tmp[n][:, :]).then_inc(S_["act_hi"], 1)
                    dve.wait_ge(S_["act_hi"], START + f + 1)
                    nc.vector.tensor_sub(part(act_lo), tmp[n][:, :], f32(part(act_hi))).then_inc(S_["act_lo"], 1)

                def finish(r, t):
                    u = 3 * t + 2
                    dve.wait_ge(x1_in[t % NX], START + (r * (DT // NX) + t // NX + 1) * 16)
                    dve.wait_ge(w_used[u % NSLOT], START + r * PER + DN0 + u // NSLOT + 1)
                    nc.vector.scalar_tensor_tensor(x1[t % NX][:, :], bank[4 + t % 2][:, :], k.mod[:, 5 * DT + t:5 * DT + t + 1],
                                                   x1[t % NX][:, :], ALU.mult, ALU.add).then_inc(S_["final"], 1)

                def final_norm(r):
                    dve.wait_ge(S_["g_in"], START + 16)
                    dve.wait_ge(S_["squared"], START + (r + 1) * 2 * TPG)
                    nc.vector.tensor_tensor(mean[:, :], ssq[:, 0:TPG], ssq[:, TPG:2 * TPG], ALU.add).then_inc(S_["ssq"], 1)
                    dve.wait_ge(S_["rms"], START + r + 1)
                    nc.vector.reciprocal(rstd[:, :], rms[:, :]).then_inc(S_["rstd"], 1)
                    dve.wait_ge(S_["rstd"], START + r + 1)
                    for q in range(TPG):
                        nc.vector.scalar_tensor_tensor(rows[:, q, :], rows[:, q, :], rstd[:, q:q + 1], g_fin[:, :],
                                                       ALU.mult, ALU.mult).then_inc(S_["o_ready"], 1)

                def group(r, more):
                    with dve.Fori(0, FT // 2 - 1) as a:
                        for n in range(2):
                            gated(r, a, n)
                            for s in (2 * n, 2 * n + 1):
                                split(s, r * PER + a + 1)
                    for n in range(2):
                        gated(r, FT // 2 - 1, n)
                        for s in (2 * n, 2 * n + 1):
                            split(s, r * PER + DN0, DOWN[s % 3][1])
                    for n in range(N_DN):
                        m = n + NSLOT
                        if m < N_DN:
                            split(m % NSLOT, r * PER + DN0 + m // NSLOT, DOWN[m % 3][1])
                        elif more:
                            split(m % NSLOT, r * PER + DN0 + m // NSLOT)
                        if n % 3 == 1 and more:
                            t = n // 3
                            dve.wait_ge(h_in[t % 2], START + (r * (DT // 2) + t // 2 + 1) * 16)
                            h_split(r + 1, t, h_raw[t % 2][:, :])
                        if n % 3 == 2:
                            finish(r, n // 3)
                    final_norm(r)

                for t in range(DT):
                    dve.wait_ge(h_first_in[t], START + 16)
                    h_split(0, t, h_first[t])
                for s in range(NSLOT):
                    split(s, 0)
                with dve.Fori(0, NRG - 1) as r:
                    group(r, True)
                group(NRG - 1, False)


def build(nc, x, c, w_ada, b_ada, g_norm_mix, w_in, b_forget, sinks, g_grp_a, g_grp_b, w_out, g_norm_ffn,
          w_gate_up, w_down, g_final, ident, ones, mask, band, out):
    proj = nc.dram_tensor("proj_t", (PT * P, S), F32, kind="Internal").ap()
    nf = nc.dram_tensor("neg_f8", (HB, S), F32, kind="Internal").ap()
    y = nc.dram_tensor("y_heads", (S, WA + WB), F32, kind="Internal").ap()
    x1 = nc.dram_tensor("x1_t", (D, S), F32, kind="Internal").ap()
    h2 = nc.dram_tensor("h2_t", (D, S), F32, kind="Internal").ap()
    as_rows = lambda v: v.rearrange("o (t p) -> (o t) p", p=P)
    vectors = [(V_BADA, as_rows(b_ada)), (V_GMIX, as_rows(g_norm_mix)), (V_GFFN, as_rows(g_norm_ffn)),
               (V_GFIN, g_final.rearrange("(t p) -> t p", p=P)), (V_GGRP, as_rows(g_grp_a)),
               (V_GGRP + WA // P, as_rows(g_grp_b))]
    with ExitStack() as stack:
        k = Core(nc, stack)
        eps = k.sbuf("eps", [P, 1])
        eps_set = k.sem("eps_set")
        with nc.Block() as block:
            @block.vector
            def _(dve):
                nc.vector.memset(eps[:, :], EPS).then_inc(eps_set, 1)
                dve.wait_ge(eps_set, 1)
        stage_modulation(k, c, w_ada, vectors, ident, ones)
        k.end_stage()
        with ExitStack() as st:
            h_hi = k.sbuf("h_hi", [P, DT, S], F32R, stack=st)
            h_lo = k.sbuf("h_lo", [P, DT, S], F32R, stack=st)
            stage_input_norm(k, x, eps, h_hi, h_lo, st)
            k.end_stage()
            stage_projection(k, w_in, b_forget, w_ada, h_hi, h_lo, proj, nf)
            k.end_stage()
        stage_attention_b(k, proj, nf, mask, y)
        k.end_stage()
        stage_attention_a(k, proj, band, sinks, y)
        k.end_stage()
        stage_mix_output(k, y, x, w_out, eps, x1, h2)
        k.end_stage()
        stage_ffn(k, x1, h2, w_gate_up, w_down, g_final, eps, out)


_INS = ["x", "c", "w_ada", "b_ada", "g_norm_mix", "w_in", "b_forget", "sinks", "g_grp_a", "g_grp_b", "w_out",
        "g_norm_ffn", "w_gate_up", "w_down", "g_final"]


def _constants():
    import numpy as np
    q, key = np.arange(P)[:, None], np.arange(P)[None, :]
    mask = np.where(key <= q, 0.0, INV_SCALE * NEG).astype(np.float32)
    chunk = 64
    kb = np.arange(BAND)[None, :]
    dist = np.abs(q - (kb - chunk)).astype(np.float32)
    seen = (kb // chunk >= q // chunk) & (kb // chunk <= q // chunk + 1)
    slopes = np.exp2(-8.0 * (np.arange(HA, dtype=np.float32) + 1.0) / HA).astype(np.float32)
    band = np.where(seen[None], -slopes[:, None, None] * dist[None], np.float32(NEG)).astype(np.float32)
    band = np.ascontiguousarray(band.reshape(KVA, GA, P, BAND).transpose(0, 2, 1, 3))
    return {"ident": np.eye(P, dtype=np.float32), "ones": np.ones((P, P), np.float32), "mask": mask, "band": band}


def kernel(**inputs):
    import numpy as np
    import concourse.bacc as bacc
    from concourse.bass_utils import run_bass_kernel_spmd as run

    nc = bacc.Bacc("TRN2", target_bir_lowering=False, num_devices=1)
    arrays, args = {}, []
    for name, a in [(n, np.ascontiguousarray(inputs[n])) for n in _INS] + list(_constants().items()):
        arrays[f"in_{name}"] = a
        args.append(nc.dram_tensor(f"in_{name}", a.shape, mybir.dt.from_np(a.dtype), kind="ExternalInput").ap())
    args.append(nc.dram_tensor("out", (1, S, D), F32, kind="ExternalOutput").ap())
    build(nc, *args)
    r = run(nc, [arrays], core_ids=[0])
    return r.results[0]["out"]
```
